# Optimizing a Trainium2 kernel written in Bass

```python
import math
import jax, jax.numpy as jnp
from jax import lax
import numpy as np

D_MODEL = 1024
BATCH = 1
SEQ = 256
DEPTH = 1
DEC_BATCH = 8
DEC_SEQ = 8
PAST_LEN = 1024
PAGE_SIZE = 128

GLA_HEADS = 4
GLA_DK = D_MODEL // 2 // GLA_HEADS
GLA_DV = D_MODEL // GLA_HEADS
GLA_LOWRANK = 16
GLA_GATE_NORM = 16.0
GLA_CHUNK = 16
MOBA_HEADS = 8
MOBA_HD = 64
MOBA_BLOCK = 256
MOBA_TOPK = 3
MOBA_QCHUNK = 16
ROPE_THETA = 10000.0
N_EXPERTS = 32
TOP_K = 4
D_FF = D_MODEL
SWIGLU_LIMIT = 7.0
SWIGLU_ALPHA = 1.702
MOE_BLOCK = 128
EPS = 1e-6

GLA_KW = GLA_HEADS * GLA_DK
GLA_VW = GLA_HEADS * GLA_DV
MOBA_W = MOBA_HEADS * MOBA_HD
IN_SPLITS = (GLA_KW, GLA_KW, GLA_VW, GLA_VW, GLA_LOWRANK, MOBA_W, MOBA_W, MOBA_W, D_MODEL, D_MODEL)
IN_WIDTH = 2 * GLA_KW + 2 * GLA_VW + GLA_LOWRANK + 3 * MOBA_W + 2 * D_MODEL

kernel_name = 'hybrid_gla_moba_moe_decode_step'

def split_cols(t, sizes):
    out, start = [], 0
    for s in sizes:
        out.append(t[..., start:start + s])
        start += s
    return out

def rms_norm(x, g):
    x32 = x.astype(jnp.float32)
    y = x32 * lax.rsqrt(jnp.mean(x32 * x32, axis=-1, keepdims=True) + EPS)
    return y.astype(x.dtype) * g

def rotary(x, pos):
    half = x.shape[-1] // 2
    inv = 1.0 / (ROPE_THETA ** (jnp.arange(half, dtype=jnp.float32) / half))
    ang = pos.astype(jnp.float32)[:, None] * inv[None, :]
    cos = jnp.cos(ang)[None, :, None, :]
    sin = jnp.sin(ang)[None, :, None, :]
    x32 = x.astype(jnp.float32)
    x1, x2 = x32[..., :half], x32[..., half:]
    return jnp.concatenate([x1 * cos - x2 * sin, x2 * cos + x1 * sin], axis=-1).astype(x.dtype)

def gla_recurrence(q, k, v, log_a, s0):
    B, L, H, _ = q.shape
    DV = v.shape[-1]
    n = -(-L // GLA_CHUNK)
    pad = n * GLA_CHUNK - L

    def blocks(t):
        t = jnp.pad(t.astype(jnp.float32), ((0, 0), (0, pad), (0, 0), (0, 0)))
        return t.reshape(B, n, GLA_CHUNK, H, t.shape[-1]).transpose(1, 0, 3, 2, 4)

    causal = jnp.tril(jnp.ones((GLA_CHUNK, GLA_CHUNK), dtype=bool))

    def step(S, inp):
        qc, kc, vc, gc = inp
        b = jnp.cumsum(gc, axis=2)
        o_inter = jnp.einsum('bhtk,bhkv->bhtv', qc * jnp.exp(b), S)
        rel = jnp.where(causal[:, :, None], b[:, :, :, None, :] - b[:, :, None, :, :], -jnp.inf)
        att = jnp.einsum('bhtk,bhsk,bhtsk->bhts', qc, kc, jnp.exp(rel))
        o = o_inter + jnp.einsum('bhts,bhsv->bhtv', att, vc)
        b_last = b[:, :, -1:, :]
        S = jnp.exp(b_last[:, :, 0, :])[..., None] * S + jnp.einsum('bhsk,bhsv->bhkv', kc * jnp.exp(b_last - b), vc)
        return S, o

    S, o = lax.scan(step, s0.astype(jnp.float32), (blocks(q), blocks(k), blocks(v), blocks(log_a)))
    o = o.transpose(1, 0, 3, 2, 4).reshape(B, n * GLA_CHUNK, H, DV)[:, :L]
    return o.astype(v.dtype), S.astype(s0.dtype)

def moba_attention(q, k, v, pos0):
    B, L, H, hd = q.shape
    T = k.shape[1]
    nbk = -(-T // MOBA_BLOCK)
    pad = nbk * MOBA_BLOCK - T
    kb = jnp.pad(k, ((0, 0), (0, pad), (0, 0), (0, 0))).reshape(B, nbk, MOBA_BLOCK, H, hd)
    vb = jnp.pad(v, ((0, 0), (0, pad), (0, 0), (0, 0))).reshape(B, nbk, MOBA_BLOCK, H, hd)
    k_mean = jnp.mean(kb.astype(jnp.float32), axis=2)
    n_sel = min(MOBA_TOPK, nbk)
    qc = math.gcd(L, MOBA_QCHUNK)
    n_chunks = L // qc
    pos = pos0 + jnp.arange(L, dtype=jnp.int32)
    q_chunks = q.reshape(B, n_chunks, qc, H, hd).transpose(1, 0, 2, 3, 4)
    pos_chunks = pos.reshape(n_chunks, qc)
    blk_ids = jnp.arange(nbk, dtype=jnp.int32)
    offs = jnp.arange(MOBA_BLOCK, dtype=jnp.int32)
    b_idx = jnp.arange(B)[:, None, None, None]
    h_idx = jnp.arange(H)[None, :, None, None]
    scale = MOBA_HD ** -0.5

    def attend(args):
        qq, pp = args
        own = pp // MOBA_BLOCK
        gate = jnp.einsum('bqhd,bjhd->bhqj', qq.astype(jnp.float32), k_mean)
        gate = jnp.where(blk_ids[None, None, None, :] < own[None, None, :, None], gate, -jnp.inf)
        _, top = lax.top_k(gate, n_sel)
        own_b = jnp.broadcast_to(own[None, None, :, None], (B, H, qc, 1))
        sel = jnp.concatenate([top, own_b], axis=-1)
        keep = jnp.concatenate([top < own_b, jnp.ones_like(own_b, dtype=bool)], axis=-1)
        kg = kb[b_idx, sel, :, h_idx, :]
        vg = vb[b_idx, sel, :, h_idx, :]
        kpos = sel[..., None] * MOBA_BLOCK + offs
        mask = keep[..., None] & (kpos <= pp[None, None, :, None, None])
        logits = jnp.einsum('bqhd,bhqsnd->bhqsn', qq, kg).astype(jnp.float32) * scale
        logits = jnp.where(mask, logits, -jnp.inf).reshape(B, H, qc, -1)
        p = jax.nn.softmax(logits, axis=-1).reshape(mask.shape).astype(v.dtype)
        return jnp.einsum('bhqsn,bhqsnd->bqhd', p, vg)

    out = lax.map(attend, (q_chunks, pos_chunks))
    return out.transpose(1, 0, 2, 3, 4).reshape(B, L, H, hd)

def moe_ffn(h, w_router, b_router, w_gate_up, b_gate_up, w_down, b_down):
    T, D = h.shape
    logits = (h @ w_router + b_router).astype(jnp.float32)
    top_val, top_idx = lax.top_k(logits, TOP_K)
    gates = jax.nn.softmax(top_val, axis=-1)
    n_assign = T * TOP_K
    flat_e = top_idx.reshape(-1).astype(jnp.int32)
    order = jnp.argsort(flat_e).astype(jnp.int32)
    sorted_e = flat_e[order]
    sorted_tok = order // TOP_K
    counts = jnp.bincount(flat_e, length=N_EXPERTS).astype(jnp.int32)
    n_blocks_e = (counts + MOE_BLOCK - 1) // MOE_BLOCK
    blk_end = jnp.cumsum(n_blocks_e)
    blk_start = blk_end - n_blocks_e
    grp_start = jnp.cumsum(counts) - counts
    dest = blk_start[sorted_e] * MOE_BLOCK + (jnp.arange(n_assign, dtype=jnp.int32) - grp_start[sorted_e])
    n_blocks = -(-n_assign // MOE_BLOCK) + N_EXPERTS
    n_rows = n_blocks * MOE_BLOCK
    row_tok = jnp.full((n_rows,), T, dtype=jnp.int32).at[dest].set(sorted_tok)
    block_expert = jnp.minimum(jnp.searchsorted(blk_end, jnp.arange(n_blocks, dtype=jnp.int32), side='right'), N_EXPERTS - 1)
    h_pad = jnp.concatenate([h, jnp.zeros((1, D), h.dtype)], axis=0)
    xb = h_pad[row_tok].reshape(n_blocks, MOE_BLOCK, D)

    def expert_block(args):
        xe, e = args
        gu = xe @ w_gate_up[e] + b_gate_up[e]
        glu, lin = gu[:, :D_FF], gu[:, D_FF:]
        glu = jnp.minimum(glu, SWIGLU_LIMIT)
        lin = jnp.clip(lin, -SWIGLU_LIMIT, SWIGLU_LIMIT)
        act = glu * jax.nn.sigmoid(SWIGLU_ALPHA * glu) * (lin + 1.0)
        return act @ w_down[e] + b_down[e]

    yb = lax.map(expert_block, (xb, block_expert)).reshape(n_rows, D)
    y_sorted = yb[dest]
    g_sorted = gates.reshape(-1)[order].astype(y_sorted.dtype)
    return jax.ops.segment_sum(y_sorted * g_sorted[:, None], sorted_tok, num_segments=T)

def layer_forward(x, c, gla_s0, past_k, past_v, w_ada, b_ada, g_norm1, w_in, w_gla_a2, b_gla_a2,
                  g_gla_head, w_proj_gla, w_proj_moba, w_out, g_norm2, w_router, b_router,
                  w_gate_up, b_gate_up, w_down, b_down):
    B, L, D = x.shape
    pos0 = past_k.shape[1]
    mod = jax.nn.silu(c) @ w_ada + b_ada
    sh1, sc1, gt1, sh2, sc2, gt2 = jnp.split(mod[:, None, :], 6, axis=-1)
    h = rms_norm(x, g_norm1) * (1.0 + sc1) + sh1
    proj = h @ w_in
    gq, gk, gv, gr, ga, mq, mk, mv, ba, bb = split_cols(proj, IN_SPLITS)
    q_g = gq.reshape(B, L, GLA_HEADS, GLA_DK) * (GLA_DK ** -0.5)
    k_g = gk.reshape(B, L, GLA_HEADS, GLA_DK)
    v_g = gv.reshape(B, L, GLA_HEADS, GLA_DV)
    log_a = jax.nn.log_sigmoid((ga @ w_gla_a2 + b_gla_a2).astype(jnp.float32)) / GLA_GATE_NORM
    log_a = log_a.reshape(B, L, GLA_HEADS, GLA_DK)
    o_g, s_new = gla_recurrence(q_g, k_g, v_g, log_a, gla_s0)
    o_g = rms_norm(o_g, g_gla_head).reshape(B, L, GLA_VW) * jax.nn.silu(gr)
    y_a = o_g @ w_proj_gla
    pos = pos0 + jnp.arange(L, dtype=jnp.int32)
    q_m = rotary(mq.reshape(B, L, MOBA_HEADS, MOBA_HD), pos)
    k_m = rotary(mk.reshape(B, L, MOBA_HEADS, MOBA_HD), pos)
    v_m = mv.reshape(B, L, MOBA_HEADS, MOBA_HD)
    o_m = moba_attention(q_m, jnp.concatenate([past_k, k_m], axis=1), jnp.concatenate([past_v, v_m], axis=1), pos0)
    y_b = o_m.reshape(B, L, MOBA_W) @ w_proj_moba
    mix = jax.nn.sigmoid(ba) * y_a + jax.nn.sigmoid(bb) * y_b
    x = x + gt1 * (mix @ w_out)
    h2 = rms_norm(x, g_norm2) * (1.0 + sc2) + sh2
    y_ff = moe_ffn(h2.reshape(B * L, D), w_router, b_router, w_gate_up, b_gate_up, w_down, b_down)
    x = x + gt2 * y_ff.reshape(B, L, D)
    return x, k_m, v_m, s_new

def setup_inputs(seed: int = 0) -> dict:
    key = jax.random.key(seed)
    ks = jax.random.split(key, 32)
    n_pages = PAST_LEN // PAGE_SIZE
    n_used = DEC_BATCH * n_pages
    n_pool = n_used + (n_used + 3) // 4

    def nrm(k, shape, scale):
        return jax.random.normal(k, shape, jnp.float32) * scale

    D = D_MODEL
    return {
        'x_prompt': nrm(ks[0], (BATCH, SEQ, D), 1.0),
        'x_sample': nrm(ks[1], (DEC_BATCH, DEC_SEQ, D), 1.0),
        'cache_k': nrm(ks[2], (DEPTH, n_pool, PAGE_SIZE, MOBA_HEADS, MOBA_HD), 1.0),
        'cache_v': nrm(ks[3], (DEPTH, n_pool, PAGE_SIZE, MOBA_HEADS, MOBA_HD), 1.0),
        'state_gla': nrm(ks[4], (DEPTH, DEC_BATCH, GLA_HEADS, GLA_DK, GLA_DV), 1.0),
        'page_table': jax.random.permutation(ks[5], n_pool)[:n_used].reshape(DEC_BATCH, n_pages).astype(jnp.int32),
        'c_prompt': nrm(ks[6], (BATCH, D), 1.0),
        'c_sample': nrm(ks[7], (DEC_BATCH, D), 1.0),
        'w_ada': nrm(ks[8], (DEPTH, D, 6 * D), D ** -0.5),
        'b_ada': nrm(ks[9], (DEPTH, 6 * D), 0.01),
        'g_norm1': 1.0 + nrm(ks[10], (DEPTH, D), 0.02),
        'w_in': nrm(ks[11], (DEPTH, D, IN_WIDTH), D ** -0.5),
        'w_gla_a2': nrm(ks[12], (DEPTH, GLA_LOWRANK, GLA_KW), GLA_LOWRANK ** -0.5),
        'b_gla_a2': nrm(ks[13], (DEPTH, GLA_KW), 0.1),
        'g_gla_head': 1.0 + nrm(ks[14], (DEPTH, GLA_DV), 0.02),
        'w_proj_gla': nrm(ks[15], (DEPTH, GLA_VW, D), GLA_VW ** -0.5),
        'w_proj_moba': nrm(ks[16], (DEPTH, MOBA_W, D), MOBA_W ** -0.5),
        'w_out': nrm(ks[17], (DEPTH, D, D), D ** -0.5),
        'g_norm2': 1.0 + nrm(ks[18], (DEPTH, D), 0.02),
        'w_router': nrm(ks[19], (DEPTH, D, N_EXPERTS), D ** -0.5),
        'b_router': nrm(ks[20], (DEPTH, N_EXPERTS), 0.01),
        'w_gate_up': nrm(ks[21], (DEPTH, N_EXPERTS, D, 2 * D_FF), D ** -0.5),
        'b_gate_up': nrm(ks[22], (DEPTH, N_EXPERTS, 2 * D_FF), 0.01),
        'w_down': nrm(ks[23], (DEPTH, N_EXPERTS, D_FF, D), D_FF ** -0.5),
        'b_down': nrm(ks[24], (DEPTH, N_EXPERTS, D), 0.01),
        'g_final': 1.0 + nrm(ks[25], (D,), 0.02),
    }

def reference(x_prompt, x_sample, cache_k, cache_v, state_gla, page_table, c_prompt, c_sample,
              w_ada, b_ada, g_norm1, w_in, w_gla_a2, b_gla_a2, g_gla_head, w_proj_gla, w_proj_moba,
              w_out, g_norm2, w_router, b_router, w_gate_up, b_gate_up, w_down, b_down, g_final):
    nb_p = x_prompt.shape[0]
    nb_s = x_sample.shape[0]
    n_pages = page_table.shape[1]
    yp, ys = x_prompt, x_sample
    kp_l, vp_l, sp_l, ks_l, vs_l, ss_l = [], [], [], [], [], []
    for l in range(DEPTH):
        wl = (w_ada[l], b_ada[l], g_norm1[l], w_in[l], w_gla_a2[l], b_gla_a2[l], g_gla_head[l],
              w_proj_gla[l], w_proj_moba[l], w_out[l], g_norm2[l], w_router[l], b_router[l],
              w_gate_up[l], b_gate_up[l], w_down[l], b_down[l])
        empty = jnp.zeros((nb_p, 0, MOBA_HEADS, MOBA_HD), x_prompt.dtype)
        s0 = jnp.zeros((nb_p, GLA_HEADS, GLA_DK, GLA_DV), state_gla.dtype)
        yp, kp, vp, sp = layer_forward(yp, c_prompt, s0, empty, empty, *wl)
        past_k = cache_k[l][page_table].reshape(nb_s, n_pages * PAGE_SIZE, MOBA_HEADS, MOBA_HD)
        past_v = cache_v[l][page_table].reshape(nb_s, n_pages * PAGE_SIZE, MOBA_HEADS, MOBA_HD)
        ys, kn, vn, sn = layer_forward(ys, c_sample, state_gla[l], past_k, past_v, *wl)
        kp_l.append(kp); vp_l.append(vp); sp_l.append(sp)
        ks_l.append(kn); vs_l.append(vn); ss_l.append(sn)
    y_prompt = rms_norm(yp, g_final)
    y_sample = rms_norm(ys, g_final)
    return (y_prompt, y_sample, jnp.stack(kp_l), jnp.stack(vp_l), jnp.stack(sp_l),
            jnp.stack(ks_l), jnp.stack(vs_l), jnp.stack(ss_l))


_drawn_inputs = setup_inputs


def setup_inputs(seed=0):
    import zlib

    import numpy as np

    out = dict(_drawn_inputs(seed))
    spreads = {}
    factors = {'g_norm1': 2.721,
     'g_gla_head': 3.607,
     'b_gate_up': 38.225,
     'b_down': 55.177,
     'g_final': 7.639,
     'g_norm2': 3.526,
     'b_router': 6.247}
    for name, (base, spread) in spreads.items():
        noise = np.random.default_rng([zlib.crc32(name.encode()), seed]).standard_normal(out[name].shape)
        drawn = base * np.exp(spread * noise) if base else spread * noise
        out[name] = __import__('jax').numpy.asarray(drawn.astype(out[name].dtype))
    for name, factor in factors.items():
        out[name] = (out[name] * factor).astype(out[name].dtype)
    return out
```

```python
from contextlib import ExitStack

import concourse.bass as bass
from concourse import mybir

F32 = mybir.dt.float32
I32 = mybir.dt.int32
U32 = mybir.dt.uint32
ACT = mybir.ActivationFunctionType
ALU = mybir.AluOpType
AX = mybir.AxisListType.X

P = 128
D = 1024
KD = D // P
NP_TOK, NB, LS = 256, 8, 8
NS_TOK = NB * LS
T = NP_TOK + NS_TOK
TILES = ((0, 128), (128, 128), (256, 64))
GH, DK, DV = 4, 128, 256
CH = 16
MH, HD = 8, 64
PAIRS = MH // 2
PAGE, NPAGES = 128, 8
BLOCK = 256
NBLK = PAGE * NPAGES // BLOCK
NEG = -1e30
GATE_NORM = 16.0
CLAMP = 38.0 * GATE_NORM
EPS = 1e-6
NE, TOPK = 32, 4
BT = 64
NX = 19
NCOL = 52
FREE = 4096
LIMIT, ALPHA = 7.0, 1.702
C_GQ, C_GK, C_GV, C_GR, C_GA = 0, 512, 1024, 2048, 3072
C_MQ, C_MK, C_MV, C_BA, C_BB = 3088, 3600, 4112, 4624, 5648
SLOT = 4096
RING = 6
PRE = 4

NMEM = 27800

V_BADA, V_G1, V_G2, V_GF, V_BA2, V_GH = 0, 48, 56, 64, 72, 76
NVEC = 78

CST = {}
_at = 0
for _name, _n in (("ident", 128), ("ones", 128), ("gla_p", 128), ("gla_s", 64), ("rows_p", 8), ("rows_s", 8),
                  ("causal", 384), ("own", 512), ("cos", 96), ("sin", 96), ("before", 128), ("iota", 32),
                  ("tri", 16), ("scan", 320), ("row0", 64), ("half", 1)):
    CST[_name] = (_at, _n)
    _at += _n
NCST = _at


def constants():
    import numpy as np

    c = {n: np.zeros((P, w), np.float32) for n, (_, w) in CST.items()}
    r = np.arange(P)[:, None]
    q = np.arange(P)[None, :]
    c["ident"][:] = r == q
    c["ones"][:] = 1
    c["gla_p"][:] = (r <= q) & (r // CH == q // CH)
    c["gla_s"][:64] = ((r <= q) & (r // LS == q // LS))[:64, :64]
    c["rows_p"][:] = r // CH == np.arange(8)
    c["rows_s"][:64] = (r // LS == np.arange(8))[:64]
    c["causal"][:, 0:128] = np.where(q <= r, 0, NEG)
    c["causal"][:, 256:384] = np.where(q <= r, 0, NEG)
    col = np.arange(64)[None, :]
    for b in range(NB):
        c["own"][:, 64 * b:64 * b + 64] = np.where((col // LS == b) & (col % LS <= r % LS), 0, NEG)
    half = HD // 2
    inv = (np.float32(1.0) / (np.float32(10000.0) ** (np.arange(half, dtype=np.float32) / np.float32(half)))).astype(np.float32)
    for t, (t0, n) in enumerate(TILES):
        pos = np.arange(t0, t0 + P) if t < 2 else PAGE * NPAGES + np.arange(P) % LS
        ang = (pos.astype(np.float32)[:, None] * inv[None, :]).astype(np.float32)
        c["cos"][:, half * t:half * t + half] = np.cos(ang)
        c["sin"][:, half * t:half * t + half] = np.sin(ang)
    c["before"][:] = r < q
    c["iota"][:] = np.arange(32)
    c["tri"][:] = (np.arange(4)[None, :] < np.arange(4)[:, None]).astype(np.float32).reshape(1, 16)
    s = np.ones(T, np.float32)
    s[0:NP_TOK:CH] = 0
    s[NP_TOK::LS] = 0
    c["scan"][:] = s
    c["row0"][0] = 1
    c["half"][64:] = 1
    return np.ascontiguousarray(np.concatenate([c[n] for n in CST], axis=1))


class Steps:

    def __init__(self, engine, sem):
        self.engine, self.sem, self.fixed, self.local, self.loop, self.per = engine, sem, 0, 0, None, 0

    def link(self, ins):
        ins.then_inc(self.sem, 1)
        self.local += 1
        done = self.fixed + self.local
        self.engine.wait_ge(self.sem, done if self.loop is None else self.loop * self.per + done)

    def enter(self, loop, per):
        self.fixed, self.local, self.loop, self.per = self.fixed + self.local, 0, loop, per

    def leave(self, times):
        assert self.local == self.per, (self.local, self.per)
        self.fixed, self.local, self.loop = self.fixed + times * self.per, 0, None


def decoder_layer(nc, x_prompt, x_sample, cache_k, cache_v, state_gla, page_table, c_prompt, c_sample,
                  w_ada, b_ada, g_norm1, w_in, w_gla_a2, b_gla_a2, g_gla_head, w_proj_gla, w_proj_moba,
                  w_out, g_norm2, w_router, b_router, w_gate_up, b_gate_up, w_down, b_down, g_final, consts,
                  y_prompt, y_sample, k_prompt, v_prompt, gla_prompt, k_sample, v_sample, gla_sample):
    with ExitStack() as ctx:
        def sb(name, shape, dt=F32):
            return ctx.enter_context(nc.sbuf_tensor(name, shape, dt))

        def sem(name):
            return ctx.enter_context(nc.semaphore(name))

        h2_rows = nc.dram_tensor("h2_rows", [T, D], F32, kind="Internal").ap()
        y_rows = nc.dram_tensor("y_rows", [T * TOPK * 2, D // 2], F32, kind="Internal").ap()
        slot_rows = nc.dram_tensor("slot_rows", [BT * NCOL, 1], I32, kind="Internal").ap()

        ring = sb("ring", [P, RING, SLOT])
        mem = sb("mem", [P, NMEM])
        late = ring[:, PRE:RING, :].rearrange("p a b -> p (a b)")

        def part(base, at, *dims):
            n = 1
            for d in dims:
                n *= d
            v = base[:, at:at + n]
            if len(dims) == 2:
                v = v.rearrange("p (a b) -> p a b", b=dims[1])
            if len(dims) == 3:
                v = v.rearrange("p (a b c) -> p a b c", b=dims[1], c=dims[2])
            return v

        cst = mem[:, 0:NCST]

        def const(name):
            a, n = CST[name]
            return mem[:, a:a + n]

        ident, ones = const("ident"), const("ones")
        o = NCST
        xT = part(mem, o, KD, T)
        hT = part(mem, o + 2560, KD, T)
        grT = part(mem, o + 5120, KD, T)
        sq = grT
        v_tok = part(mem, o + 7680, 3, D)
        x_tok = v_tok
        oTm = part(mem, o + 7680, PAIRS, T)
        h2_tok = v_tok
        gqT = part(mem, o + 10752, GH, T)
        gkT = part(mem, o + 12032, GH, T)
        oTg = part(mem, o + 10752, KD, T)
        mqT = part(mem, o + 13312, PAIRS, T)
        mkT = part(mem, o + 14592, PAIRS, T)
        mv_tok = part(mem, o + 15872, 3, MH * HD)
        g0 = o + 17408
        state = part(mem, g0, 2, GH, DV)
        km = part(mem, g0 + 2048, 2, 8, DK)
        qm = part(mem, g0 + 4096, 2, 8, P)
        o_tok = part(mem, g0 + 6144, D)
        rot = part(mem, g0, 2, 3, MH * HD)
        pin = part(mem, g0, 2, 384)
        pexp = part(mem, g0 + 768, 2, 384)
        ptp = part(mem, g0 + 1536, 2, 384)
        om_tok = part(mem, g0 + 2304, 2, MH * HD)
        kTs = part(mem, g0, PAIRS, PAGE * NPAGES)
        pex = part(mem, g0 + 4096, PAGE * NPAGES + NS_TOK)
        pts = part(mem, g0 + 5184, NPAGES, P)
        pto = part(mem, g0 + 6208, P)
        qs = part(mem, g0 + 6336, PAIRS, 32)
        osm = part(mem, g0 + 6464, P)
        e0 = g0 + 7168
        modT = part(mem, e0, 6, KD, 9)
        vT = part(mem, e0 + 432, NVEC)
        w_ga = part(mem, e0 + 512, KD, 16)
        wa2 = part(mem, o + 13312, GH * DK)
        gaT = part(late, 7488, T)
        w_rt = part(mem, e0 + 640, KD, NE)
        b_rt = part(mem, e0 + 896, NE)
        small = e0 + 928
        s1 = part(mem, small, KD, 9)
        colA = part(mem, small + 72, 16)
        colB = part(mem, small + 88, 16)
        colC = part(mem, small + 104, 16)
        colD = part(mem, small + 120, 16)
        eps = part(mem, small + 136, 1)
        eqT = part(late, 0, GH, T)
        ekT = part(late, 1280, GH, T)
        e0T = part(late, 2560, GH, T)
        elT = part(late, 3840, GH, T)
        baT = part(late, 0, KD, T)
        bbT = part(late, 2560, KD, T)
        craw = part(late, 0, D)
        cexp = part(late, 1024, D)
        bT = part(late, 5120, GH, T)
        rstd = part(late, 6400, T)
        scT = part(late, 6720, KD, 32)
        mod_sb = part(late, 6976, 512)
        vraw = part(late, 6976, P)
        att = part(late, 7488, 2, P)
        edec = part(late, 7744, GH, 24)
        tmp = part(late, 7840, 320)
        m0 = o + 10752
        bias = [part(mem, m0, 3072), part(mem, m0 + 3072, 3072)]
        x_in = [part(mem, m0 + 6144, D), part(mem, m0 + 7168, D)]
        xeT = [part(mem, m0 + 8192, KD, BT), part(mem, m0 + 8704, KD, BT)]
        glu = part(mem, m0 + 9216, 512)
        lin = part(mem, m0 + 9728, 512)
        sig = part(mem, m0 + 10240, 512)
        act_m = part(mem, m0 + 10752, 512)
        actT = part(mem, m0 + 11264, 4, 2, BT)
        y_out = [part(mem, m0 + 11776, 512), part(mem, m0 + 12288, 512)]
        r0 = o + 5120
        lg = part(mem, r0, 3, NE)
        top = part(mem, r0 + 96, 3, 8)
        topf = part(mem, r0 + 120, 3, 8)
        oh = part(mem, r0 + 144, 3, TOPK, NE)
        pick = part(mem, r0 + 528, 3, NE)
        pos = part(mem, r0 + 624, 3, NE)
        cnt = part(mem, r0 + 720, NE)
        xtra = part(mem, r0 + 752, NE)
        xend = part(mem, r0 + 784, NE)
        nblk = part(mem, r0 + 816, 3, NE)
        base = part(mem, r0 + 912, 3, NE)
        rtmp = part(mem, r0 + 1008, TOPK, NE)
        slotf = part(mem, r0 + 1136, 3, TOPK)
        gates = part(mem, r0 + 1148, 3, TOPK)
        gsum = part(mem, r0 + 1160, 3)
        xcmp = part(mem, r0 + 1164, NX, NE)
        ysum = part(mem, o + 2560, 2, D)
        sq_tail = part(mem, o + 7680, KD, T)
        rstd_tail = part(mem, o + 10240, T)
        ff_tail = part(mem, m0 + 6144, KD, NS_TOK)
        topi = sb("topi", [P, 3, 8], U32)
        sloti = sb("sloti", [P, 3 * TOPK], I32)
        asg = sb("asg", [P, 3 * TOPK], I32)
        fill = sb("fill", [P, NCOL], I32)
        slots = sb("slots", [P, NCOL], I32)
        tok_ix = sb("tok_ix", [P, NCOL], I32)
        row_ix = sb("row_ix", [P, NCOL], I32)
        tok_col = sb("tok_col", [P, 2], I32)
        row_col = sb("row_col", [P, 2], I32)
        eid = sb("eid", [P, NX + 1], I32)
        ptab = sb("ptab", [P, NB * NPAGES], I32)

        ps = ctx.enter_context(nc.psum_tensor("ps", [P, 8, 512], F32))

        land = [sem(f"land{i}") for i in range(RING)]
        slot_used = sem("slot_used")
        s0_used = sem("s0_used")
        cst_in, vec_in, c_in, x_in_s, wsm_in, pt_in = (sem(n) for n in ("cst_in", "vec_in", "c_in", "x_land", "wsm_in", "pt_in"))
        dve_step, act_step, eps_sb = sem("dve_step"), sem("act_step"), sem("eps_sb")
        vecT_ps, vecT_sb, c_exp, c_silu, cT_ps, cT_sb = (sem(n) for n in ("vecT_ps", "vecT_sb", "c_exp", "c_silu", "cT_ps", "cT_sb"))
        xT_ps, xT_sb, sq_sb, ss_ps = (sem(n) for n in ("xT_ps", "xT_sb", "sq_sb", "ss_ps"))
        ada_ps, mod_rows, modT_ps, mod_done = (sem(n) for n in ("ada_ps", "mod_rows", "modT_ps", "mod_done"))
        h_done, rms_sb = sem("h_done"), sem("rms_sb")
        fm_ps, fm_sb, gr_sb, tm_ps, tm_sb = (sem(n) for n in ("fm_ps", "fm_sb", "gr_sb", "tm_ps", "tm_sb"))
        gla_d, gla_a = sem("gla_d"), sem("gla_a")
        kt_ps, km_sb, qm_sb, att_ps, att_sb, d_ps, s_new, o_part, o_ps = (
            sem(n) for n in ("kt_ps", "km_sb", "qm_sb", "att_ps", "att_sb", "d_ps", "s_new", "o_part", "o_ps"))
        o_sq, o_norm, ot_ps, ot_sb = (sem(n) for n in ("o_sq", "o_norm", "ot_ps", "ot_sb"))
        ms_ps, ms_max, ms_exp, mt_ps, mt_sb, mo_ps, mo_sb, mot_ps, mot_sb = (
            sem(n) for n in ("ms_ps", "ms_max", "ms_exp", "mt_ps", "mt_sb", "mo_ps", "mo_sb", "mot_ps", "mot_sb"))
        q_sb, kt2_ps, kt2_a, kt2_d, cs_ps, cs_max, cs_exp, cp_ps, cp_a, cp_d, co_ps, co_sb, cot_ps, cot_sb = (
            sem(n) for n in ("q_sb", "kt2_ps", "kt2_a", "kt2_d", "cs_ps", "cs_max", "cs_exp", "cp_ps", "cp_a", "cp_d",
                             "co_ps", "co_sb", "cot_ps", "cot_sb"))
        pj_ps, pj_sb, sq2_sb, ss2_ps, h2_done, rt_ps, h2t_ps, h2t_sb, h2_out = (
            sem(n) for n in ("pj_ps", "pj_sb", "sq2_sb", "ss2_ps", "h2_done", "rt_ps", "h2t_ps", "h2t_sb", "h2_out"))
        fill_ix, fill_out, picked, rank_ps, slots_sb, g_max, g_exp, scat, slots_in, ix_done, route_done = (
            sem(n) for n in ("fill_ix", "fill_out", "picked", "rank_ps", "slots_sb", "g_max", "g_exp", "scat", "slots_in",
                             "ix_done", "route_done"))
        x_land = [sem("xg_land0"), sem("xg_land1")]
        b_land = [sem("b_land0"), sem("b_land1")]
        y_sent = [sem("y_sent0"), sem("y_sent1")]
        ix_sb, xe_ps, xe_sb, glu_sb, sig_sb, act_sb, at_ps, at_sb, y_sb = (
            sem(n) for n in ("ix_sb", "xe_ps", "xe_sb", "glu_sb", "sig_sb", "act_sb", "at_ps", "at_sb", "y_sb"))
        dve_moe, zero_sb, moe_done, y_free, ys_sb, yt_ps, x3_sb, sq3_sb, ss3_ps, fin_sb, ft_ps, ft_sb, dve_tail = (
            sem(n) for n in ("dve_moe", "zero_sb", "moe_done", "y_free", "ys_sb", "yt_ps", "x3_sb", "sq3_sb", "ss3_ps", "fin_sb",
                             "ft_ps", "ft_sb", "dve_tail"))
        y_in = [sem(f"y_in{t}") for t in range(3)]
        turns = sem("turns")
        k_out, v_out, gs_out, y_stored = (sem(n) for n in ("k_out", "v_out", "gs_out", "y_stored"))

        N_ADA0, N_IN, N_GR, N_S0, N_BA, N_ADA1, N_CACHE, N_PROJ = 0, 4, 11, 13, 15, 19, 27, 43
        N_PRE = 48
        w_in2 = w_in[0]
        in_cols = [C_GQ, C_GK, C_GV, C_GV + 512, C_MQ, C_MK, C_MV, C_GR, C_GR + 512, None, None, C_BA, C_BA + 512, C_BB, C_BB + 512]
        w2d = {}
        for j in range(4):
            w2d[N_ADA0 + j] = (w_ada[0], 512 * j)
        for j, c0 in enumerate(in_cols):
            if c0 is not None:
                w2d[N_IN + j] = (w_in2, c0)
        for j in range(8):
            w2d[N_ADA1 + j] = (w_ada[0], 2048 + 512 * j)
        for n, w, c0 in ((N_PROJ, w_proj_gla, 0), (N_PROJ + 1, w_proj_gla, 512), (N_PROJ + 3, w_out, 0), (N_PROJ + 4, w_out, 512)):
            w2d[n] = (w[0], c0)
        landed, total = {}, [0] * PRE
        for n in range(N_PRE):
            total[n % PRE] += 16 * (NPAGES if N_CACHE <= n < N_PROJ else 1)
            landed[n] = total[n % PRE]
        land0 = total + [0, 0]
        used = {}
        for j in range(4):
            used[N_ADA0 + j], used[N_ADA1 + j], used[N_ADA1 + 4 + j] = (ada_ps, 1), (ada_ps, 2), (ada_ps, 3)
            used[N_BA + j] = (fm_ps, 33 + 4 * j)
        used[N_IN], used[N_IN + 1] = (fm_ps, 5), (fm_ps, 9)
        for c in range(5):
            used[N_IN + 2 + c] = (tm_ps, 3 * c + 3)
        used[N_GR], used[N_GR + 1] = (fm_ps, 17), (fm_ps, 21)
        for half in range(2):
            used[N_S0 + half] = (s0_used, 16 * (half + 1))
        for b in range(NB):
            used[N_CACHE + 2 * b], used[N_CACHE + 2 * b + 1] = (kt2_ps, 8 * b + 8), (co_ps, b + 1)
        for j, jobs in enumerate((4, 8, 16, 20, 24)):
            used[N_PROJ + j] = (pj_ps, jobs)

        def item(n):
            return ring[:, n % PRE, :].rearrange("p (a b) -> p a b", b=512)

        def wait_item(eng, n):
            eng.wait_ge(land[n % PRE], landed[n])

        k_pages = cache_k[0].rearrange("n s h d -> n s (h d)")
        v_pages = cache_v[0].rearrange("n s h d -> n s (h d)")
        block = ctx.enter_context(nc.Block())

        @block.sync
        def _(sp):
            sp.dma_start(cst, consts).then_inc(cst_in, 16)
            sp.dma_start(craw[0:1, :], c_prompt).then_inc(c_in, 16)
            sp.dma_start(craw[1:9, :], c_sample).then_inc(c_in, 16)
            for vec, at, n in ((b_ada, V_BADA, 48), (g_norm1, V_G1, 8), (g_norm2, V_G2, 8), (b_gla_a2, V_BA2, 4), (g_gla_head, V_GH, 2)):
                sp.dma_start(vraw[at:at + n, :], vec[0].rearrange("(a b) -> a b", b=P)).then_inc(vec_in, 16)
            sp.dma_start(vraw[V_GF:V_GF + 8, :], g_final.rearrange("(a b) -> a b", b=P)).then_inc(vec_in, 16)
            sp.dma_start(x_tok[:, 0:2, :], x_prompt[0].rearrange("(a p) d -> p a d", p=P)).then_inc(x_in_s, 16)
            sp.dma_start(x_tok[0:64, 2, :], x_sample.rearrange("b l d -> (b l) d")).then_inc(x_in_s, 16)
            sp.dma_start(w_ga, w_in2[:, C_GA:C_GA + 16].rearrange("(k p) n -> p k n", p=P)).then_inc(wsm_in, 16)
            sp.dma_start(wa2[0:16, :], w_gla_a2[0]).then_inc(wsm_in, 16)
            sp.dma_start(w_rt, w_router[0].rearrange("(k p) n -> p k n", p=P)).then_inc(wsm_in, 16)
            sp.dma_start(b_rt, b_router.to_broadcast([P, NE])).then_inc(wsm_in, 16)
            sp.dma_start(ptab[0:1, :], page_table.rearrange("(o b) n -> o (b n)", o=1)).then_inc(pt_in, 16)

            def load(n):
                if n >= PRE:
                    sp.wait_ge(*used[n - PRE])
                if n in w2d:
                    w, c0 = w2d[n]
                    sp.dma_start(item(n), w[:, c0:c0 + 512].rearrange("(k p) n -> p k n", p=P)).then_inc(land[n % PRE], 16)
                elif n in (N_S0, N_S0 + 1):
                    b = 4 * (n - N_S0)
                    sp.dma_start(ring[:, n % PRE, :].rearrange("p (b n) -> p b n", n=DV),
                                 state_gla[0, b:b + 4].rearrange("b h k v -> k (b h) v")).then_inc(land[n % PRE], 16)
                else:
                    sp.dma_start(ring[:, n % PRE, :].rearrange("p (k n) -> p k n", n=D),
                                 w_proj_moba[0].rearrange("(k p) n -> p k n", p=P)).then_inc(land[n % PRE], 16)

            for n in range(N_ADA0, N_S0 + PRE):
                load(n)
            sp.wait_ge(tm_sb, 12)
            sp.dma_start(k_prompt[0, 0].rearrange("(a p) h d -> p a (h d)", p=P), rot[:, 1, 0:2, :]).then_inc(k_out, 16)
            sp.dma_start(k_sample[0].rearrange("b l h d -> (b l) (h d)"), rot[0:64, 1, 2, :]).then_inc(k_out, 16)
            sp.wait_ge(tm_sb, 15)
            sp.dma_start(v_prompt[0, 0].rearrange("(a p) h d -> p a (h d)", p=P), mv_tok[:, 0:2, :]).then_inc(v_out, 16)
            sp.dma_start(v_sample[0].rearrange("b l h d -> (b l) (h d)"), mv_tok[0:64, 2, :]).then_inc(v_out, 16)
            sp.wait_ge(s_new, 8 * GH * 2)
            sp.dma_start(gla_prompt[0, 0].rearrange("h k v -> k h v"), state[:, 0]).then_inc(gs_out, 16)
            for half in range(2):
                sp.wait_ge(s_new, 8 * GH * 3)
                n = N_S0 + half
                sp.dma_start(gla_sample[0, 4 * half:4 * half + 4].rearrange("b h k v -> k (b h) v"),
                             ring[:, n % PRE, :].rearrange("p (b n) -> p b n", n=DV)).then_inc(s0_used, 16)
                sp.wait_ge(s0_used, 16 * (half + 1))
            for n in range(N_S0 + PRE, N_CACHE):
                load(n)
            sp.wait_ge(pt_in, 16)
            def pages_of(b, n):
                for j in range(NPAGES):
                    page = sp.value_load(ptab[0:1, bass.ds(b * NPAGES + j, 1)], min_val=0, max_val=cache_k.shape[1] - 1)
                    sp.dma_start(item(n)[:, j, :], (v_pages if (n - N_CACHE) % 2 else k_pages)[bass.ds(page, 1)]
                                 .rearrange("o s n -> s (o n)")).then_inc(land[n % PRE], 16)

            for n in range(N_CACHE, N_CACHE + 4):
                sp.wait_ge(*used[n - PRE])
                pages_of((n - N_CACHE) // 2, n)
            with sp.Fori(1, NB // 2) as i:
                for sub in range(2):
                    b = i * 2 + sub
                    sp.wait_ge(kt2_ps, b * 8 - 8)
                    sp.sem_inc(turns, 1)
                    pages_of(b, N_CACHE + 2 * sub)
                    sp.wait_ge(co_ps, b - 1)
                    sp.sem_inc(turns, 1)
                    pages_of(b, N_CACHE + 2 * sub + 1)
            for n in range(N_PROJ, N_PRE):
                load(n)

            def expert_slot(e, s):
                if s < PRE:
                    sp.dma_start(ring[:, s, :].rearrange("p (k n) -> p k n", k=2),
                                 w_gate_up[0, bass.ds(e, 1), 2 * P * s:2 * P * (s + 1), :].rearrange("o (k p) n -> p (o k) n", p=P)).then_inc(land[s], 16)
                else:
                    k = s - PRE
                    sp.dma_start(ring[:, s, :].rearrange("p (k n) -> p k n", k=4),
                                 w_down[0, bass.ds(e, 1), 4 * P * k:4 * P * (k + 1), :].rearrange("o (k p) n -> p (o k) n", p=P)).then_inc(land[s], 16)

            def expert_bias(e, par):
                sp.dma_start(bias[par][0:1, 0:2 * D], b_gate_up[0, bass.ds(e, 1), :]).then_inc(b_land[par], 16)
                sp.dma_start(bias[par][0:1, 2 * D:3 * D], b_down[0, bass.ds(e, 1), :]).then_inc(b_land[par], 16)

            for s in range(PRE):
                sp.wait_ge(*used[N_PRE - PRE + s])
                expert_slot(0, s)
            for t, (t0, n) in enumerate(TILES):
                sp.wait_ge(h2t_sb, 2 * t + 2)
                sp.dma_start(h2_rows[t0:t0 + n, :], h2_tok[0:n, t, :]).then_inc(h2_out, 16)
            sp.wait_ge(h2_done, 1)
            expert_slot(0, PRE)
            expert_slot(0, PRE + 1)
            sp.wait_ge(zero_sb, 2)
            expert_bias(0, 0)
            expert_bias(1, 1)

            def expert_loads(e):
                for s in range(RING):
                    sp.wait_ge(slot_used, e * RING + (s + 1 - RING))
                    expert_slot(e, s)

            expert_loads(1)
            with sp.Fori(1, NE // 2) as i:
                for par in range(2):
                    e = i * 2 + par
                    sp.wait_ge(slot_used, e * RING - RING)
                    expert_bias(e, par)
                    expert_loads(e)
            sp.wait_ge(route_done, 1)
            n_extra = sp.value_load(eid[0:1, NX:NX + 1], min_val=0, max_val=NX)
            with sp.Fori(0, NX) as i:
                with sp.If(i < n_extra):
                    e = sp.value_load(eid[0:1, bass.ds(i, 1)], min_val=0, max_val=NE - 1)
                    sp.wait_ge(slot_used, (i + NE) * RING)
                    expert_bias(e, 0)
                    for s in range(RING):
                        expert_slot(e, s)
                sp.nop()
            sp.wait_ge(moe_done, 1)
            for t, (t0, n) in enumerate(TILES):
                sp.dma_start(ring[0:n, t, :], y_rows[t0 * 8:(t0 + n) * 8, :].rearrange("(p a) d -> p (a d)", a=8)).then_inc(y_in[t], 16)
            for t, (t0, n) in enumerate(TILES):
                sp.wait_ge(ft_sb, 2 * t + 2)
                out = y_prompt[0, t0:t0 + n, :] if t < 2 else y_sample.rearrange("b l d -> (b l) d")
                sp.dma_start(out, ring[0:n, 3 + t, 0:D]).then_inc(y_stored, 16)
            sp.wait_ge(y_stored, 48)
            sp.wait_ge(k_out, 32)
            sp.wait_ge(v_out, 32)
            sp.wait_ge(gs_out, 16)
            sp.wait_ge(s0_used, 32)

        @block.tensor
        def _(pe):
            mm = nc.tensor.matmul

            def tr(out, in_, n=P):
                return nc.tensor.transpose(out, in_, ident[0:n, 0:n])

            pe.wait_ge(cst_in, 16)
            pe.wait_ge(vec_in, 96)
            tr(ps[:, 0, 0:NVEC], vraw[0:NVEC, :], NVEC).then_inc(vecT_ps, 1)
            pe.wait_ge(x_in_s, 32)
            for k in range(KD):
                if k >= 3:
                    pe.wait_ge(xT_sb, k - 2)
                for t, (t0, n) in enumerate(TILES):
                    last = tr(ps[:, 2 + k % 3, t0:t0 + n], x_tok[0:n, t, k * P:(k + 1) * P], n)
                last.then_inc(xT_ps, 1)
            pe.wait_ge(c_silu, 1)
            for k in range(KD):
                last = tr(ps[:, 1, 16 * k:16 * k + 9], craw[0:9, k * P:(k + 1) * P], 9)
            last.then_inc(cT_ps, 1)
            pe.wait_ge(sq_sb, 8)
            for k in range(KD):
                last = mm(ps[:, 5, 0:T], ones, sq[:, k, :], start=k == 0, stop=k == KD - 1)
            last.then_inc(ss_ps, 1)

            def modulation(g):
                n0 = N_ADA0 if g == 0 else N_ADA1 + 4 * (g - 1)
                if g:
                    pe.wait_ge(mod_done, g)
                else:
                    pe.wait_ge(cT_sb, 1)
                for j in range(4):
                    wait_item(pe, n0 + j)
                for k in range(KD):
                    for j in range(4):
                        last = mm(ps[32 * j:32 * j + 32, 6, :], scT[:, k, :], item(n0 + j)[:, k, :], start=k == 0, stop=k == KD - 1)
                last.then_inc(ada_ps, 1)
                pe.wait_ge(mod_rows, g + 1)
                for c in range(4):
                    last = tr(ps[:, 7, c * P:(c + 1) * P], mod_sb[:, c * P:(c + 1) * P])
                last.then_inc(modT_ps, 1)

            modulation(0)

            def fm_free(n):
                if n >= 3:
                    pe.wait_ge(fm_sb, n - 2)
                    if 13 <= n - 3 < 21:
                        pe.wait_ge(gr_sb, n - 15)

            def fm(n, w, M=P):
                fm_free(n)
                for k in range(KD):
                    last = mm(ps[0:M, n % 3, 0:T], w[:, k, :], hT[:, k, :], start=k == 0, stop=k == KD - 1)
                last.then_inc(fm_ps, 1)

            def fm_item(n0, it):
                wait_item(pe, it)
                for m in range(4):
                    fm(n0 + m, item(it)[:, :, m * P:(m + 1) * P])

            pe.wait_ge(h_done, 1)
            pe.wait_ge(wsm_in, 64)
            fm(0, w_ga, 16)
            fm_item(1, N_IN)
            fm_item(5, N_IN + 1)
            pe.wait_ge(fm_sb, 1)
            for h in range(GH):
                fm_free(9 + h)
                mm(ps[:, (9 + h) % 3, 0:T], wa2[0:16, h * DK:(h + 1) * DK], gaT[0:16, :], start=True, stop=True).then_inc(fm_ps, 1)
            for c in range(5):
                wait_item(pe, N_IN + 2 + c)
                for t, (t0, n) in enumerate(TILES):
                    if 3 * c + t >= 3:
                        pe.wait_ge(tm_sb, 3 * c + t - 2)
                    for k in range(KD):
                        last = mm(ps[0:n, 3 + t, :], hT[:, k, t0:t0 + n], item(N_IN + 2 + c)[:, k, :], start=k == 0, stop=k == KD - 1)
                    last.then_inc(tm_ps, 1)
            fm_item(13, N_GR)
            fm_item(17, N_GR + 1)
            pe.wait_ge(tm_sb, 12)
            for j in range(8):
                which, p = divmod(j, 4)
                fm_free(21 + j)
                for t, (t0, n) in enumerate(TILES):
                    last = tr(ps[:, (21 + j) % 3, t0:t0 + n], rot[0:n, which, t, p * P:(p + 1) * P], n)
                last.then_inc(fm_ps, 1)

            pe.wait_ge(fm_sb, 29)
            pe.wait_ge(gla_d, 5)
            pe.wait_ge(tm_sb, 15)
            for t, (t0, n) in enumerate(TILES):
                if t:
                    pe.wait_ge(km_sb, GH * t)
                for h in range(GH):
                    last = tr(ps[0:n, 3, h * DK:(h + 1) * DK], elT[:, h, t0:t0 + n])
                last.then_inc(kt_ps, 1)
                for h in range(GH):
                    u = GH * t + h
                    if u:
                        pe.wait_ge(att_sb, u)
                    mm(ps[0:n, 4, 0:n], ekT[:, h, t0:t0 + n], eqT[:, h, t0:t0 + n], start=True, stop=True).then_inc(att_ps, 1)
                    pe.wait_ge(att_sb, u + 1)
                    pe.wait_ge(km_sb, u + 1)
                    pe.wait_ge(qm_sb, u + 1)
                    if u >= 2:
                        pe.wait_ge(o_norm, u - 1)
                    values = v_tok[0:n, t, h * DV:(h + 1) * DV]
                    mm(ps[0:n, 5 + u % 2, 0:DV], att[0:n, u % 2, 0:n], values, start=True, stop=False)

                    def delta(c):
                        if 8 * u + c >= 2:
                            pe.wait_ge(s_new, 8 * u + c - 1)
                        mm(ps[:, c % 2, 0:DV], km[0:n, u % 2, c, :], values, start=True, stop=True).then_inc(d_ps, 1)

                    if t == 2 and h == 0:
                        wait_item(pe, N_S0)
                        wait_item(pe, N_S0 + 1)
                    delta(0)
                    delta(1)
                    for c in range(8):
                        if t < 2:
                            if c:
                                pe.wait_ge(s_new, 8 * u + c)
                            prior = state[:, c % 2, h, :]
                        else:
                            prior = ring[:, (N_S0 + c // 4) % PRE, ((c % 4) * GH + h) * DV:((c % 4) * GH + h + 1) * DV]
                        mm(ps[0:n, 5 + u % 2, 0:DV], qm[:, u % 2, c, 0:n], prior, start=False, stop=c == 7).then_inc(o_part, 1)
                        if c < 6:
                            delta(c + 2)
                pe.wait_ge(o_norm, GH * (t + 1))
                if t:
                    pe.wait_ge(ot_sb, t)
                for m in range(KD):
                    last = tr(ps[:, 7 if m < 4 else 2, (m % 4) * n:(m % 4 + 1) * n], o_tok[0:n, m * P:(m + 1) * P], n)
                last.then_inc(ot_ps, 1)

            pe.wait_ge(s_new, 96)
            pe.wait_ge(ot_sb, 3)
            for it in range(4):
                fm_item(29 + 4 * it, N_BA + it)
            modulation(1)
            modulation(2)

            pe.wait_ge(fm_sb, 45)

            def prompt_scores(h):
                p, q0 = h // 2, HD * (h % 2)
                if h >= 2:
                    pe.wait_ge(ms_max, h - 1)
                mm(ps[:, h % 2, 0:128], mqT[q0:q0 + HD, p, 0:128], mkT[q0:q0 + HD, p, 0:128], start=True, stop=True)
                mm(ps[:, h % 2, 128:384], mqT[q0:q0 + HD, p, 128:256], mkT[q0:q0 + HD, p, 0:256], start=True, stop=True).then_inc(ms_ps, 1)

            prompt_scores(0)
            for h in range(MH):
                if h + 1 < MH:
                    prompt_scores(h + 1)
                pe.wait_ge(ms_exp, h + 1)
                if h >= 2:
                    pe.wait_ge(mt_sb, h - 1)
                for j in range(3):
                    last = tr(ps[:, 3 + h % 2, j * P:(j + 1) * P], pexp[:, h % 2, j * P:(j + 1) * P])
                last.then_inc(mt_ps, 1)
                pe.wait_ge(mt_sb, h + 1)
                if h >= 2:
                    pe.wait_ge(mo_sb, h - 1)
                bank, hs = 5 + h % 2, slice(h * HD, (h + 1) * HD)
                mm(ps[:, bank, 0:HD], ptp[:, h % 2, 0:P], mv_tok[:, 0, hs], start=True, stop=True)
                mm(ps[:, bank, HD:2 * HD], ptp[:, h % 2, P:2 * P], mv_tok[:, 0, hs], start=True, stop=False)
                mm(ps[:, bank, HD:2 * HD], ptp[:, h % 2, 2 * P:3 * P], mv_tok[:, 1, hs], start=False, stop=True).then_inc(mo_ps, 1)
            pe.wait_ge(mo_sb, MH)
            for p in range(PAIRS):
                for t in range(2):
                    last = tr(ps[:, 3 + p // 2, (p % 2) * 256 + t * P:(p % 2) * 256 + (t + 1) * P], om_tok[:, t, p * P:(p + 1) * P])
            last.then_inc(mot_ps, 1)
            pe.wait_ge(mot_sb, 2)

            with pe.Fori(0, NB // 2) as i:
                for sub in range(2):
                    b = i * 2 + sub
                    nk, nv = N_CACHE + 2 * sub, N_CACHE + 2 * sub + 1
                    pe.wait_ge(land[nk % PRE], i * (16 * NPAGES) + landed[nk])
                    for jj in range(2 * PAIRS):
                        p, f = divmod(jj, 2)
                        if jj >= 4:
                            pe.wait_ge(kt2_d if jj % 2 else kt2_a, b * 4 + (jj - 4) // 2 + 1)
                        for q in range(4):
                            last = tr(ps[:, jj % 4, q * P:(q + 1) * P], item(nk)[:, 4 * f + q, p * P:(p + 1) * P])
                        last.then_inc(kt2_ps, 1)
                    pe.wait_ge(kt2_a, b * 4 + 4)
                    pe.wait_ge(kt2_d, b * 4 + 4)
                    pe.wait_ge(q_sb, b + 1)
                    for f in range(2):
                        for p in range(PAIRS):
                            mm(ps[32 * p:32 * p + 32, 4 + f, :], qs[:, p, :], kTs[:, p, 512 * f:512 * f + 512], start=True, stop=True)
                    for p in range(PAIRS):
                        last = mm(ps[32 * p:32 * p + 32, 6, 0:NS_TOK], qs[:, p, :], mkT[:, p, NP_TOK:T], start=True, stop=True)
                    last.then_inc(cs_ps, 1)
                    pe.wait_ge(cs_exp, b + 1)
                    for j in range(NPAGES):
                        last = tr(ps[:, j // 4, (j % 4) * P:(j % 4 + 1) * P], pex[:, j * P:(j + 1) * P])
                    last = tr(ps[0:NS_TOK, 2, 0:P], pex[:, PAGE * NPAGES:])
                    last.then_inc(cp_ps, 1)
                    pe.wait_ge(cp_a, b + 1)
                    pe.wait_ge(cp_d, b + 1)
                    pe.wait_ge(land[nv % PRE], i * (16 * NPAGES) + landed[nv])
                    for j in range(NPAGES + 1):
                        for p in range(PAIRS):
                            if j < NPAGES:
                                last = mm(ps[32 * p:32 * p + 32, 7, 0:P], pts[:, j, 32 * p:32 * p + 32], item(nv)[:, j, p * P:(p + 1) * P],
                                          start=j == 0, stop=False)
                            else:
                                last = mm(ps[32 * p:32 * p + 32, 7, 0:P], pto[0:NS_TOK, 32 * p:32 * p + 32],
                                          mv_tok[0:NS_TOK, 2, p * P:(p + 1) * P], start=False, stop=True)
                    last.then_inc(co_ps, 1)
                    pe.wait_ge(co_sb, b + 1)
                    tr(ps[:, 6, 0:P], osm).then_inc(cot_ps, 1)
                    pe.wait_ge(cot_sb, b + 1)

            for n in range(24):
                which, m = divmod(n, KD)
                it = N_PROJ + (m // 4 if which == 0 else 2 if which == 1 else 3 + m // 4)
                wait_item(pe, it)
                if n >= 4:
                    pe.wait_ge(pj_sb, n - 3)
                if n == 16:
                    pe.wait_ge(pj_sb, 16)
                kc = PAIRS if which == 1 else KD
                w = ring[:, it % PRE, :].rearrange("p (k n) -> p k n", k=kc)
                src = (oTg, oTm, hT)[which]
                c0 = m * P if which == 1 else (m % 4) * P
                for k in range(kc):
                    last = mm(ps[:, n % 4, 0:T], w[:, k, c0:c0 + P], src[:, k, :], start=k == 0, stop=k == kc - 1)
                last.then_inc(pj_ps, 1)

            pe.wait_ge(sq2_sb, 8)
            for k in range(KD):
                last = mm(ps[:, 4, 0:T], ones, sq[:, k, :], start=k == 0, stop=k == KD - 1)
            last.then_inc(ss2_ps, 1)
            pe.wait_ge(h2_done, 1)
            for t, (t0, n) in enumerate(TILES):
                for k in range(KD):
                    last = mm(ps[0:n, 5, NE * t:NE * t + NE], hT[:, k, t0:t0 + n], w_rt[:, k, :], start=k == 0, stop=k == KD - 1)
            last.then_inc(rt_ps, 1)
            for t, (t0, n) in enumerate(TILES):
                for f in range(2):
                    if 2 * t + f >= 4:
                        pe.wait_ge(h2t_sb, 2 * t + f - 3)
                    for q in range(4):
                        last = tr(ps[0:n, (2 * t + f) % 4, q * P:(q + 1) * P], hT[:, 4 * f + q, t0:t0 + n])
                    last.then_inc(h2t_ps, 1)
            pe.wait_ge(picked, 1)
            for t, (t0, n) in enumerate(TILES):
                for tt in range(t + 1):
                    nn = TILES[tt][1]
                    lhs = const("before")[0:nn, 0:n] if tt == t else ones[0:nn, 0:n]
                    mm(ps[0:n, 4, NE * t:NE * t + NE], lhs, pick[0:nn, tt, :], start=tt == 0, stop=tt == t)
            for tt in range(3):
                nn = TILES[tt][1]
                last = mm(ps[:, 4, 96:128], ones[0:nn, :], pick[0:nn, tt, :], start=tt == 0, stop=tt == 2)
            last.then_inc(rank_ps, 1)

            def xe_transposes(par, n, gathered):
                pe.wait_ge(x_land[par], gathered)
                pe.sem_inc(turns, 1)
                for k in range(KD):
                    last = tr(ps[:, par, k * BT:(k + 1) * BT], x_in[par][0:BT, k * P:(k + 1) * P], BT)
                last.then_inc(xe_ps, 1)

            def gate_up(par, n, biases, weights):
                pe.wait_ge(xe_sb, n + 1)
                pe.wait_ge(b_land[par], biases)
                for q in range(4):
                    out = ps[64 * (q % 2):64 * (q % 2) + 64, 2 + 2 * (q // 2) + par, :]
                    mm(out, const("row0"), bias[par][:, 512 * q:512 * q + 512], start=True, stop=False)
                for s in range(PRE):
                    pe.wait_ge(land[s], weights + land0[s])
                    w = ring[:, s, :].rearrange("p (k n) -> p k n", k=2)
                    for k in range(2):
                        for q in range(4):
                            out = ps[64 * (q % 2):64 * (q % 2) + 64, 2 + 2 * (q // 2) + par, :]
                            last = mm(out, xeT[par][:, 2 * s + k, :], w[:, k, 512 * q:512 * q + 512], start=False, stop=s == 3 and k == 1)
                    last.then_inc(slot_used, 1)

            def down(par, n, weights):
                pe.wait_ge(act_sb, n + 1)
                for c in range(4):
                    last = tr(ps[:, 6, c * P:(c + 1) * P], act_m[:, c * P:(c + 1) * P])
                last.then_inc(at_ps, 1)
                for f in range(2):
                    mm(ps[64 * f:64 * f + 64, 7, :], const("row0"), bias[par][:, 2048 + 512 * f:2560 + 512 * f], start=True, stop=False)
                pe.wait_ge(at_sb, n + 1)
                for s in range(2):
                    pe.wait_ge(land[PRE + s], weights)
                    w = ring[:, PRE + s, :].rearrange("p (k n) -> p k n", k=4)
                    for k in range(4):
                        for f in range(2):
                            last = mm(ps[64 * f:64 * f + 64, 7, :], actT[:, k, s, :], w[:, k, 512 * f:512 * f + 512], start=False, stop=s == 1 and k == 3)
                    last.then_inc(slot_used, 1)

            pe.wait_ge(slots_sb, 1)
            pe.wait_ge(h2t_sb, 6)
            with pe.Fori(0, NE // 2) as i:
                for par in range(2):
                    n = i * 2 + par
                    xe_transposes(par, n, (i + 1) * 16)
                    gate_up(par, n, (i + 1) * 32, (n + 1) * 16)
                    down(par, n, (n + 1) * 16)
            pe.wait_ge(route_done, 1)
            n_extra = pe.value_load(eid[0:1, NX:NX + 1], min_val=0, max_val=NX)
            with pe.Fori(0, NX) as i:
                with pe.If(i < n_extra):
                    n = i + NE
                    xe_transposes(0, n, (i + (NE // 2 + 1)) * 16)
                    gate_up(0, n, (i + (NE // 2 + 1)) * 32, (n + 1) * 16)
                    down(0, n, (n + 1) * 16)
                pe.nop()

            for t, (t0, n) in enumerate(TILES):
                pe.wait_ge(ys_sb, t + 1)
                for f in range(2):
                    for q in range(4):
                        last = tr(ps[:, 2 * t + f, q * n:(q + 1) * n], ysum[0:n, t % 2, (4 * f + q) * P:(4 * f + q + 1) * P], n)
                last.then_inc(yt_ps, 1)
            pe.wait_ge(sq3_sb, 1)
            for k in range(KD):
                last = mm(ps[:, 6, 0:T], ones, sq_tail[:, k, :], start=k == 0, stop=k == KD - 1)
            last.then_inc(ss3_ps, 1)
            pe.wait_ge(fin_sb, 1)
            for t, (t0, n) in enumerate(TILES):
                for f in range(2):
                    for q in range(4):
                        last = tr(ps[0:n, 2 * t + f, q * P:(q + 1) * P], xT[:, 4 * f + q, t0:t0 + n])
                    last.then_inc(ft_ps, 1)

        @block.scalar
        def _(act):
            a = nc.scalar
            act.wait_ge(c_in, 32)
            a.activation(cexp[0:9, :], craw[0:9, :], ACT.Exp, scale=-1.0).then_inc(c_exp, 1)
            for k in range(KD):
                act.wait_ge(xT_ps, k + 1)
                a.copy(xT[:, k, :], ps[:, 2 + k % 3, 0:T]).then_inc(xT_sb, 1)
            act.wait_ge(vecT_sb, 1)
            act.wait_ge(eps_sb, 1)
            act.wait_ge(ss_ps, 1)
            a.activation(rstd, ps[:, 5, 0:T], ACT.Sqrt, scale=1.0 / D, bias=eps).then_inc(rms_sb, 1)
            for n in range(13):
                act.wait_ge(fm_ps, n + 1)
                bank = ps[:, n % 3, 0:T]
                if n == 0:
                    a.copy(gaT[0:16, :], bank[0:16, :]).then_inc(fm_sb, 1)
                elif n < 5:
                    a.copy(gqT[:, n - 1, :], bank).then_inc(fm_sb, 1)
                elif n < 9:
                    a.copy(gkT[:, n - 5, :], bank).then_inc(fm_sb, 1)
                else:
                    h = n - 9
                    a.activation(elT[:, h, :], bank, ACT.Identity, bias=vT[:, V_BA2 + h:V_BA2 + h + 1]).then_inc(fm_sb, 1)
            act.wait_ge(gla_d, 1)
            a.activation(eqT, eqT, ACT.Exp).then_inc(act_step, 1)
            act.wait_ge(act_step, 1)
            a.activation(eqT, eqT, ACT.Ln, bias=1.0).then_inc(gla_a, 1)
            act.wait_ge(gla_d, 3)
            a.activation(ekT, eqT, ACT.Exp, scale=-1.0 / GATE_NORM).then_inc(act_step, 1)
            act.wait_ge(act_step, 2)
            a.activation(eqT, eqT, ACT.Exp, scale=1.0 / GATE_NORM).then_inc(act_step, 1)
            a.activation(e0T, bT, ACT.Exp, scale=1.0 / GATE_NORM).then_inc(gla_a, 1)
            act.wait_ge(gla_d, 4)
            a.activation(elT, elT, ACT.Exp, scale=1.0 / GATE_NORM).then_inc(gla_a, 1)
            for n in range(13, 21):
                act.wait_ge(fm_ps, n + 1)
                a.activation(grT[:, n - 13, :], ps[:, n % 3, 0:T], ACT.Sigmoid).then_inc(fm_sb, 1)
            for n in range(21, 29):
                act.wait_ge(fm_ps, n + 1)
                which, p = divmod(n - 21, 4)
                a.copy((mqT, mkT)[which][:, p, :], ps[:, n % 3, 0:T]).then_inc(fm_sb, 1)
            for t, (t0, n) in enumerate(TILES):
                for h in range(GH):
                    u = GH * t + h
                    act.wait_ge(o_part, 8 * u + 8)
                    if u:
                        act.wait_ge(o_sq, u)
                        act.wait_ge(o_norm, u)
                    a.activation(tmp[0:n, 0:DV], ps[0:n, 5 + u % 2, 0:DV], ACT.Square, accum_out=colA[0:n, 0:1]).then_inc(act_step, 1)
                    act.wait_ge(act_step, 4 + u)
                    a.activation(colC[0:n, 0:1], colA[0:n, 0:1], ACT.Sqrt, scale=1.0 / DV, bias=eps[0:n]).then_inc(o_sq, 1)
            for n in range(29, 45):
                act.wait_ge(fm_ps, n + 1)
                m = n - 29
                a.activation((baT if m < 8 else bbT)[:, m % 8, :], ps[:, n % 3, 0:T], ACT.Sigmoid).then_inc(fm_sb, 1)
            for h in range(MH):
                act.wait_ge(ms_max, h + 1)
                if h >= 2:
                    act.wait_ge(mt_ps, h - 1)
                    act.wait_ge(mo_sb, h - 1)
                e = pexp[:, h % 2, :]
                x = pin[:, h % 2, :]
                for t, (c0, c1) in enumerate(((0, P), (P, 3 * P))):
                    last = a.activation(e[:, c0:c1], x[:, c0:c1], ACT.Exp, scale=HD ** -0.5, bias=colB[:, 2 * (h % 2) + t:2 * (h % 2) + t + 1],
                                        accum_out=colC[:, 2 * (h % 2) + t:2 * (h % 2) + t + 1])
                last.then_inc(ms_exp, 1)
                act.wait_ge(mt_ps, h + 1)
                if h >= 2:
                    act.wait_ge(mo_ps, h - 1)
                a.copy(ptp[:, h % 2, :], ps[:, 3 + h % 2, 0:384]).then_inc(mt_sb, 1)
            act.wait_ge(mot_ps, 1)
            for f in range(2):
                a.copy(oTm[:, 2 * f:2 * f + 2, 0:NP_TOK], ps[:, 3 + f, :].rearrange("p (a b) -> p a b", b=NP_TOK)).then_inc(mot_sb, 1)
            with act.Fori(0, NB // 2) as i:
                for sub in range(2):
                    b = i * 2 + sub
                    for jj in range(0, 8, 2):
                        act.wait_ge(kt2_ps, b * 8 + jj + 1)
                        a.copy(kTs[:, jj // 2, 0:512], ps[:, jj % 4, :]).then_inc(kt2_a, 1)
                    act.wait_ge(cs_max, b + 1)
                    for j in range(NBLK + 1):
                        c0, c1 = (BLOCK * j, BLOCK * (j + 1)) if j < NBLK else (PAGE * NPAGES, PAGE * NPAGES + NS_TOK)
                        src = ps[:, 4 + j // 2, (j % 2) * BLOCK:(j % 2 + 1) * BLOCK] if j < NBLK else tmp[:, 0:NS_TOK]
                        last = a.activation(pex[:, c0:c1], src, ACT.Exp, scale=HD ** -0.5, bias=colB[:, j:j + 1], accum_out=colC[:, j:j + 1])
                    last.then_inc(cs_exp, 1)
                    act.wait_ge(cp_ps, b + 1)
                    a.copy(pts[:, 0:4, :], ps[:, 0, :].rearrange("p (a b) -> p a b", b=P))
                    a.copy(pto[0:NS_TOK, :], ps[0:NS_TOK, 2, 0:P]).then_inc(cp_a, 1)
            act.wait_ge(ss2_ps, 1)
            a.activation(rstd, ps[:, 4, 0:T], ACT.Sqrt, scale=1.0 / D, bias=eps).then_inc(rms_sb, 1)
            for j in range(6):
                t, f = divmod(j, 2)
                n = TILES[t][1]
                act.wait_ge(h2t_ps, j + 1)
                a.copy(h2_tok[0:n, t, 512 * f:512 * f + 512], ps[0:n, j % 4, :]).then_inc(h2t_sb, 1)
            act.wait_ge(g_max, 1)
            for t, (t0, n) in enumerate(TILES):
                last = a.activation(gates[0:n, t, :], top[0:n, t, 0:TOPK], ACT.Exp, bias=colD[0:n, t:t + 1], accum_out=gsum[0:n, t:t + 1])
            last.then_inc(g_exp, 1)

            def expert(par, n):
                act.wait_ge(xe_ps, n + 1)
                a.copy(xeT[par], ps[:, par, :].rearrange("p (k n) -> p k n", n=BT)).then_inc(xe_sb, 1)
                act.wait_ge(glu_sb, n + 1)
                a.activation(sig, glu, ACT.Sigmoid, scale=ALPHA).then_inc(sig_sb, 1)
                act.wait_ge(at_ps, n + 1)
                a.copy(actT, ps[:, 6, :].rearrange("p (c f n) -> p c f n", c=4, f=2)).then_inc(at_sb, 1)

            with act.Fori(0, NE // 2) as i:
                for par in range(2):
                    expert(par, i * 2 + par)
            act.wait_ge(route_done, 1)
            n_extra = act.value_load(eid[0:1, NX:NX + 1], min_val=0, max_val=NX)
            with act.Fori(0, NX) as i:
                with act.If(i < n_extra):
                    expert(0, i + NE)
                act.nop()
            act.wait_ge(ss3_ps, 1)
            a.activation(rstd_tail, ps[:, 6, 0:T], ACT.Sqrt, scale=1.0 / D, bias=eps).then_inc(rms_sb, 1)
            for j in range(6):
                t, f = divmod(j, 2)
                n = TILES[t][1]
                act.wait_ge(ft_ps, j + 1)
                a.copy(ring[0:n, 3 + t, 512 * f:512 * f + 512], ps[0:n, j, :]).then_inc(ft_sb, 1)

        @block.vector
        def _(dve):
            v = nc.vector
            st = Steps(dve, dve_step)
            link = st.link
            v.memset(eps, EPS).then_inc(eps_sb, 1)
            link(v.memset(scT, 0.0))
            dve.wait_ge(vecT_ps, 1)
            v.tensor_copy(vT, ps[:, 0, 0:NVEC]).then_inc(vecT_sb, 1)
            dve.wait_ge(c_exp, 1)
            link(v.tensor_scalar_add(cexp[0:9, :], cexp[0:9, :], 1.0))
            link(v.reciprocal(cexp[0:9, :], cexp[0:9, :]))
            v.tensor_tensor(craw[0:9, :], craw[0:9, :], cexp[0:9, :], ALU.mult).then_inc(c_silu, 1)
            for k in range(KD):
                dve.wait_ge(xT_sb, k + 1)
                v.tensor_tensor(sq[:, k, :], xT[:, k, :], xT[:, k, :], ALU.mult).then_inc(sq_sb, 1)
            dve.wait_ge(cT_ps, 1)
            v.tensor_copy(scT[:, :, 0:9], ps[:, 1, 0:128].rearrange("p (k n) -> p k n", n=16)[:, :, 0:9]).then_inc(cT_sb, 1)

            def inverse_rms(sm, n):
                dve.wait_ge(sm, n)
                link(v.reciprocal(rstd, rstd))

            inverse_rms(rms_sb, 1)

            def modulation(g):
                dve.wait_ge(ada_ps, g + 1)
                v.tensor_copy(mod_sb, ps[:, 6, :]).then_inc(mod_rows, 1)
                dve.wait_ge(modT_ps, g + 1)
                dve.wait_ge(vecT_sb, 1)
                for j in range(4):
                    src = ps[:, 7, :].rearrange("p (c r) -> p c r", c=4)[:, :, 32 * j:32 * j + 9]
                    add = vT[:, V_BADA + 16 * g + 4 * j:V_BADA + 16 * g + 4 * j + 4, None].to_broadcast([P, 4, 9])
                    last = v.tensor_tensor(modT[:, 2 * g + j // 2, 4 * (j % 2):4 * (j % 2) + 4, :], src, add, ALU.add)
                last.then_inc(mod_done, 1)

            def modulated(shift, gain, scale, done):
                g = vT[:, gain:gain + KD, None].to_broadcast([P, KD, 9])
                link(v.scalar_tensor_tensor(s1, modT[:, scale], 1.0, g, ALU.add, ALU.mult))
                for k in range(KD):
                    last = v.tensor_tensor(hT[:, k, :], xT[:, k, :], rstd, ALU.mult)
                link(last)
                for k in range(KD):
                    v.tensor_scalar(hT[:, k, 0:NP_TOK], hT[:, k, 0:NP_TOK], s1[:, k, 0:1], modT[:, shift, k, 0:1], ALU.mult, ALU.add)
                    hs = hT[:, k, NP_TOK:T].rearrange("p (b l) -> p b l", l=LS)
                    last = v.tensor_tensor(hs, hs, s1[:, k, 1:9, None].to_broadcast([P, NB, LS]), ALU.mult)
                link(last)
                for k in range(KD):
                    hs = hT[:, k, NP_TOK:T].rearrange("p (b l) -> p b l", l=LS)
                    last = v.tensor_tensor(hs, hs, modT[:, shift, k, 1:9, None].to_broadcast([P, NB, LS]), ALU.add)
                last.then_inc(done, 1)

            modulation(0)
            dve.wait_ge(mod_done, 1)
            modulated(0, V_G1, 1, h_done)

            def chunks(x, which):
                if which == 0:
                    return x[:, :, 0:NP_TOK].rearrange("p h (c l) -> p h c l", l=CH)
                return x[:, :, NP_TOK:T].rearrange("p h (c l) -> p h c l", l=LS)

            def against(out, at):
                for w, ln in ((0, CH), (1, LS)):
                    b = chunks(bT, w)
                    ref = b[:, :, :, at(ln):at(ln) + 1]
                    for h in range(GH):
                        yield chunks(out, w)[:, h], b[:, h], ref[:, h].to_broadcast([P, b.shape[2], ln])

            def decay(step):
                if step == 0:
                    dve.wait_ge(fm_sb, 13)
                    v.scalar_tensor_tensor(eqT, elT, -1.0, elT, ALU.mult, ALU.min).then_inc(gla_d, 1)
                if step == 1:
                    dve.wait_ge(gla_a, 1)
                    link(v.scalar_tensor_tensor(elT, elT, 0.0, eqT, ALU.min, ALU.subtract))
                    for h in range(GH):
                        last = v.tensor_tensor_scan(bT[:, h, :], const("scan"), elT[:, h, :], 0.0, ALU.mult, ALU.add)
                    last.then_inc(gla_d, 1)
                if step == 2:
                    dve.wait_ge(gla_d, 2)
                    for dst, x, y in against(eqT, lambda ln: ln // 2 - 1):
                        last = v.tensor_tensor(dst, x, y, ALU.subtract)
                    link(last)
                    v.tensor_scalar(eqT, eqT, CLAMP, -CLAMP, ALU.min, ALU.max).then_inc(gla_d, 1)
                if step == 3:
                    for dst, x, y in against(elT, lambda ln: ln - 1):
                        last = v.tensor_tensor(dst, y, x, ALU.subtract)
                    last.then_inc(gla_d, 1)
                if step == 4:
                    dve.wait_ge(gla_a, 2)
                    v.tensor_copy(edec[:, :, 0:16], chunks(e0T, 0)[:, :, :, CH - 1])
                    link(v.tensor_copy(edec[:, :, 16:24], chunks(e0T, 1)[:, :, :, LS - 1]))
                    v.scalar_tensor_tensor(eqT, gqT, DK ** -0.5, eqT, ALU.mult, ALU.mult)
                    v.tensor_tensor(ekT, gkT, ekT, ALU.mult)
                if step == 5:
                    v.scalar_tensor_tensor(e0T, gqT, DK ** -0.5, e0T, ALU.mult, ALU.mult)
                    dve.wait_ge(gla_a, 3)
                    v.tensor_tensor(elT, gkT, elT, ALU.mult).then_inc(gla_d, 1)

            for n in range(15):
                c, t = divmod(n, 3)
                rows = TILES[t][1]
                dve.wait_ge(tm_ps, n + 1)
                bank = ps[0:rows, 3 + t, :]
                if c < 2:
                    v.tensor_copy(v_tok[0:rows, t, 512 * c:512 * c + 512], bank).then_inc(tm_sb, 1)
                elif c < 4:
                    x = bank.rearrange("p (h a d) -> p h a d", a=2, d=HD // 2)
                    r = rot[0:rows, c - 2, t, :].rearrange("p (h a d) -> p h a d", a=2, d=HD // 2)
                    cos = const("cos")[0:rows, None, 32 * t:32 * t + 32].to_broadcast([rows, MH, 32])
                    sin = const("sin")[0:rows, None, 32 * t:32 * t + 32].to_broadcast([rows, MH, 32])
                    s = tmp[0:rows, 0:256].rearrange("p (h d) -> p h d", d=32)
                    v.tensor_tensor(r[:, :, 0, :], x[:, :, 0, :], cos, ALU.mult)
                    v.tensor_tensor(r[:, :, 1, :], x[:, :, 1, :], cos, ALU.mult)
                    link(v.tensor_tensor(s, x[:, :, 1, :], sin, ALU.mult))
                    link(v.tensor_tensor(r[:, :, 0, :], r[:, :, 0, :], s, ALU.subtract))
                    link(v.tensor_tensor(s, x[:, :, 0, :], sin, ALU.mult))
                    v.tensor_tensor(r[:, :, 1, :], r[:, :, 1, :], s, ALU.add).then_inc(tm_sb, 1)
                    dve.wait_ge(tm_sb, n + 1)
                else:
                    v.tensor_copy(mv_tok[0:rows, t, :], bank).then_inc(tm_sb, 1)
                if 6 <= n < 12:
                    decay(n - 6)
            for m in range(8):
                dve.wait_ge(fm_sb, 14 + m)
                v.tensor_tensor(grT[:, m, :], ps[:, (13 + m) % 3, 0:T], grT[:, m, :], ALU.mult).then_inc(gr_sb, 1)

            dve.wait_ge(fm_sb, 29)
            dve.wait_ge(k_out, 32)
            link(v.memset(mem[:, g0:g0 + 6144], 0.0))
            for t, (t0, n) in enumerate(TILES):
                ln = CH if t < 2 else LS
                for h in range(GH):
                    u = GH * t + h
                    if u >= 2:
                        dve.wait_ge(o_part, 8 * (u - 1))
                    if t == 2 and h < 2:
                        link(v.memset(qm[:, u % 2], 0.0))
                    at = g0 + 4096 + 1024 * (u % 2)
                    diag = mem[:, at:at + 8 * (P + ln)].rearrange("p (c x) -> p c x", x=P + ln)[:, :, 0:ln]
                    v.tensor_copy(diag, e0T[:, h, t0:t0 + n].rearrange("p (c l) -> p c l", l=ln)).then_inc(qm_sb, 1)
                    dve.wait_ge(att_ps, u + 1)
                    v.tensor_tensor(att[0:n, u % 2, 0:n], ps[0:n, 4, 0:n], const("gla_p" if t < 2 else "gla_s")[0:n, 0:n], ALU.mult).then_inc(att_sb, 1)
                    dve.wait_ge(kt_ps, t + 1)
                    v.tensor_tensor(km[0:n, u % 2], ps[0:n, 3, None, h * DK:(h + 1) * DK].to_broadcast([n, 8, DK]),
                                    const("rows_p" if t < 2 else "rows_s")[0:n, :, None].to_broadcast([n, 8, DK]), ALU.mult).then_inc(km_sb, 1)
                    for c in range(8):
                        dve.wait_ge(d_ps, 8 * u + c + 1)
                        dec = edec[:, h, 8 * t + c:8 * t + c + 1]
                        if t < 2:
                            if u or c:
                                dve.wait_ge(s_new, 8 * u + c)
                                dve.wait_ge(o_part, 8 * u + c)
                            old, new = state[:, c % 2, h, :], state[:, (c + 1) % 2, h, :]
                        else:
                            dve.wait_ge(o_part, 8 * u + c + 1)
                            old = new = ring[:, (N_S0 + c // 4) % PRE, ((c % 4) * GH + h) * DV:((c % 4) * GH + h + 1) * DV]
                        v.scalar_tensor_tensor(new, old, dec, ps[:, c % 2, 0:DV], ALU.mult, ALU.add).then_inc(s_new, 1)
                    dve.wait_ge(o_sq, u + 1)
                    link(v.reciprocal(colB[0:n, 0:1], colC[0:n, 0:1]))
                    if t and h == 0:
                        dve.wait_ge(ot_ps, t)
                    v.tensor_scalar(o_tok[0:n, h * DV:(h + 1) * DV], ps[0:n, 5 + u % 2, 0:DV], colB[0:n, 0:1], None, ALU.mult).then_inc(o_norm, 1)
                dve.wait_ge(ot_ps, t + 1)
                for f in range(2):
                    for j in range(2):
                        src = ps[:, 2 if f else 7, 0:4 * n].rearrange("p (h j n) -> p j h n", j=2, n=n)[:, j]
                        gr = grT[:, 4 * f:4 * f + 4, t0:t0 + n].rearrange("p (h j) n -> p j h n", j=2)[:, j]
                        to = oTg[:, 4 * f:4 * f + 4, t0:t0 + n].rearrange("p (h j) n -> p j h n", j=2)[:, j]
                        last = v.scalar_tensor_tensor(to, src, vT[:, V_GH + j:V_GH + j + 1], gr, ALU.mult, ALU.mult)
                last.then_inc(ot_sb, 1)

            modulation(1)
            modulation(2)

            dve.wait_ge(gs_out, 16)
            def prompt_out(h):
                dve.wait_ge(mo_ps, h + 1)
                link(v.reciprocal(colD[:, 2 * (h % 2):2 * (h % 2) + 2], colC[:, 2 * (h % 2):2 * (h % 2) + 2]))
                for t in range(2):
                    last = v.tensor_scalar(om_tok[:, t, h * HD:(h + 1) * HD], ps[:, 5 + h % 2, t * HD:(t + 1) * HD],
                                           colD[:, 2 * (h % 2) + t:2 * (h % 2) + t + 1], None, ALU.mult)
                last.then_inc(mo_sb, 1)

            for h in range(MH):
                dve.wait_ge(ms_ps, h + 1)
                if h >= 2:
                    dve.wait_ge(ms_exp, h - 1)
                x = pin[:, h % 2, :]
                link(v.tensor_tensor(x, ps[:, h % 2, 0:384], const("causal"), ALU.add))
                v.tensor_reduce(colA[:, 0:1], x[:, 0:P], AX, ALU.max)
                link(v.tensor_reduce(colA[:, 1:2], x[:, P:3 * P], AX, ALU.max))
                v.tensor_scalar(colB[:, 2 * (h % 2):2 * (h % 2) + 2], colA[:, 0:2], -HD ** -0.5, None, ALU.mult).then_inc(ms_max, 1)
                if h:
                    prompt_out(h - 1)
            prompt_out(MH - 1)

            dve.wait_ge(mot_sb, 2)
            link(v.memset(qs, 0.0))
            with dve.Fori(0, NB // 2) as i:
                st.enter(i, 22)
                for sub in range(2):
                    b = i * 2 + sub
                    for hh in range(2):
                        rows = slice(64 * hh, 64 * hh + 64)
                        last = v.tensor_copy(qs[rows, :, 8 * hh:8 * hh + 8], mqT[rows, :, bass.ds(b * LS + NP_TOK, LS)])
                    last.then_inc(q_sb, 1)
                    for jj in range(1, 8, 2):
                        dve.wait_ge(kt2_ps, b * 8 + jj + 1)
                        v.tensor_copy(kTs[:, jj // 2, 512:1024], ps[:, jj % 4, :]).then_inc(kt2_d, 1)
                    dve.wait_ge(cs_ps, b + 1)
                    sc = ps[:, 4:6, :].rearrange("p a (b c) -> p a b c", c=BLOCK)
                    gsum4 = colA[:, 0:4]
                    v.tensor_reduce(gsum4.rearrange("p (a b) -> p a b", b=2), sc, AX, ALU.add)
                    v.tensor_reduce(colD[:, 0:4].rearrange("p (a b) -> p a b", b=2), sc, AX, ALU.max)
                    link(v.tensor_tensor(tmp[:, 0:NS_TOK], ps[:, 6, 0:NS_TOK], const("own")[:, bass.ds(b * NS_TOK, NS_TOK)], ALU.add))
                    v.tensor_reduce(colD[:, 4:5], tmp[:, 0:NS_TOK], AX, ALU.max)
                    mine = gsum4[:, :, None].to_broadcast([P, 4, 4])
                    other = gsum4[:, None, :].to_broadcast([P, 4, 4])
                    w = tmp[:, 64:80].rearrange("p (a b) -> p a b", b=4)
                    w2 = tmp[:, 80:96].rearrange("p (a b) -> p a b", b=4)
                    tri = const("tri").rearrange("p (a b) -> p a b", b=4)
                    v.tensor_tensor(w, other, mine, ALU.is_gt)
                    link(v.tensor_tensor(w2, other, mine, ALU.is_equal))
                    link(v.tensor_tensor(w2, w2, tri, ALU.mult))
                    link(v.tensor_tensor(w, w, w2, ALU.add))
                    link(v.tensor_reduce(colA[:, 4:8], w, AX, ALU.add))
                    link(v.tensor_scalar(colA[:, 8:12], colA[:, 4:8], 3.0, NEG, ALU.is_ge, ALU.mult))
                    link(v.tensor_tensor(colD[:, 0:4], colD[:, 0:4], colA[:, 8:12], ALU.add))
                    link(v.tensor_reduce(colD[:, 5:6], colD[:, 0:5], AX, ALU.max))
                    link(v.tensor_scalar(colB[:, 4:5], colD[:, 5:6], -HD ** -0.5, None, ALU.mult))
                    v.tensor_scalar(colB[:, 0:4], colA[:, 8:12], colB[:, 4:5], None, ALU.add).then_inc(cs_max, 1)
                    dve.wait_ge(cs_exp, b + 1)
                    link(v.tensor_reduce(colD[:, 8:9], colC[:, 0:5], AX, ALU.add))
                    link(v.reciprocal(colD[:, 9:10], colD[:, 8:9]))
                    dve.wait_ge(cp_ps, b + 1)
                    v.tensor_copy(pts[:, 4:8, :], ps[:, 1, :].rearrange("p (a b) -> p a b", b=P)).then_inc(cp_d, 1)
                    dve.wait_ge(co_ps, b + 1)
                    v.tensor_scalar(osm, ps[:, 7, 0:P], colD[:, 9:10], None, ALU.mult).then_inc(co_sb, 1)
                    dve.wait_ge(cot_ps, b + 1)
                    for hh in range(2):
                        rows = slice(64 * hh, 64 * hh + 64)
                        src = ps[rows, 6, 0:P].rearrange("p (a r) -> p a r", r=32)[:, :, 8 * hh:8 * hh + 8]
                        last = v.tensor_copy(oTm[rows, :, bass.ds(b * LS + NP_TOK, LS)], src)
                    last.then_inc(cot_sb, 1)
            st.leave(NB // 2)

            for n in range(24):
                which, m = divmod(n, KD)
                dve.wait_ge(pj_ps, n + 1)
                bank = ps[:, n % 4, 0:T]
                if which == 0:
                    v.tensor_tensor(baT[:, m, :], bank, baT[:, m, :], ALU.mult).then_inc(pj_sb, 1)
                elif which == 1:
                    link(v.tensor_tensor(bbT[:, m, :], bank, bbT[:, m, :], ALU.mult))
                    v.tensor_tensor(hT[:, m, :], baT[:, m, :], bbT[:, m, :], ALU.add).then_inc(pj_sb, 1)
                else:
                    v.scalar_tensor_tensor(xT[:, m, 0:NP_TOK], bank[:, 0:NP_TOK], modT[:, 2, m, 0:1], xT[:, m, 0:NP_TOK], ALU.mult, ALU.add)
                    w = tmp[:, 0:NS_TOK].rearrange("p (b l) -> p b l", l=LS)
                    link(v.tensor_tensor(w, bank[:, NP_TOK:T].rearrange("p (b l) -> p b l", l=LS),
                                         modT[:, 2, m, 1:9, None].to_broadcast([P, NB, LS]), ALU.mult))
                    v.tensor_tensor(xT[:, m, NP_TOK:T], xT[:, m, NP_TOK:T], tmp[:, 0:NS_TOK], ALU.add).then_inc(pj_sb, 1)
                    dve.wait_ge(pj_sb, n + 1)
                    v.tensor_tensor(sq[:, m, :], xT[:, m, :], xT[:, m, :], ALU.mult).then_inc(sq2_sb, 1)
            inverse_rms(rms_sb, 2)
            modulated(3, V_G2, 4, h2_done)
            dve.wait_ge(pj_sb, 24)
            for par in range(2):
                v.memset(bias[par], 0.0).then_inc(zero_sb, 1)
            for par in range(2):
                last = v.memset(x_in[par], 0.0)
            last.then_inc(zero_sb, 1)

            dve.wait_ge(rt_ps, 1)
            link(v.memset(lg, 0.0))
            for t, (t0, n) in enumerate(TILES):
                last = v.tensor_tensor(lg[0:n, t, :], ps[0:n, 5, NE * t:NE * t + NE], b_rt[0:n, :], ALU.add)
            link(last)
            for t in range(3):
                last = v.max(top[:, t, :], lg[:, t, :])
            link(last)
            for t in range(3):
                last = v.max_index(topi[:, t, :], top[:, t, :], lg[:, t, :])
            link(last)
            v.tensor_scalar(colD[:, 0:3], top[:, :, 0], -1.0, None, ALU.mult).then_inc(g_max, 1)
            link(v.tensor_copy(topf, topi[:]))
            for t in range(3):
                for k in range(TOPK):
                    last = v.tensor_scalar(oh[:, t, k, :], const("iota"), topf[:, t, k:k + 1], None, ALU.is_equal)
            link(last)
            for t in range(3):
                last = v.tensor_reduce(pick[:, t, :], oh[:, t].rearrange("p k e -> p e k"), AX, ALU.add)
            last.then_inc(picked, 1)
            dve.wait_ge(rank_ps, 1)
            v.memset(pos, 0.0)
            link(v.tensor_copy(cnt, ps[:, 4, 96:128]))
            for t, (t0, n) in enumerate(TILES):
                last = v.tensor_copy(pos[0:n, t, :], ps[0:n, 4, NE * t:NE * t + NE])
            link(last)
            link(v.tensor_scalar(xtra, cnt, float(BT), None, ALU.is_gt))
            for j in range(2, 5):
                link(v.scalar_tensor_tensor(xtra, cnt, float(BT * j), xtra, ALU.is_gt, ALU.add))
            link(v.tensor_tensor_scan(xend, ones[:, 0:NE], xtra, 0.0, ALU.mult, ALU.add))
            link(v.tensor_scalar(nblk, pos, float(BT), None, ALU.is_ge))
            for j in range(2, 5):
                link(v.scalar_tensor_tensor(nblk, pos, float(BT * j), nblk, ALU.is_ge, ALU.add))
            link(v.tensor_tensor(xtra, xend, xtra, ALU.subtract))
            link(v.tensor_scalar_add(xtra, xtra, float(NE - 1)))
            link(v.tensor_tensor(cnt, const("iota"), xtra, ALU.subtract))
            link(v.tensor_scalar(base, nblk, 0.0, None, ALU.is_equal))
            link(v.tensor_tensor(base, base, cnt[:, None, :].to_broadcast([P, 3, NE]), ALU.mult))
            link(v.tensor_tensor(base, base, xtra[:, None, :].to_broadcast([P, 3, NE]), ALU.add))
            link(v.scalar_tensor_tensor(base, nblk, float(1 - BT * NCOL), base, ALU.mult, ALU.add))
            link(v.scalar_tensor_tensor(base, pos, float(NCOL), base, ALU.mult, ALU.add))
            for t in range(3):
                link(v.tensor_tensor(rtmp, oh[:, t], base[:, t, None, :].to_broadcast([P, TOPK, NE]), ALU.mult))
                link(v.tensor_reduce(slotf[:, t, :], rtmp, AX, ALU.add))
            v.tensor_copy(sloti[:], slotf.rearrange("p a b -> p (a b)")).then_inc(slots_sb, 1)
            link(v.tensor_tensor(xcmp[0:1], xend[0:1, None, :].to_broadcast([1, NX, NE]),
                                 const("iota")[0:1, 0:NX, None].to_broadcast([1, NX, NE]), ALU.is_le))
            link(v.tensor_reduce(cnt[0:1, 0:NX], xcmp[0:1], AX, ALU.add))
            link(v.tensor_scalar(cnt[0:1, 0:NX], cnt[0:1, 0:NX], float(NE - 1), None, ALU.min))
            link(v.tensor_copy(cnt[0:1, NX:NX + 1], xend[0:1, NE - 1:NE]))
            v.tensor_copy(eid[0:1, :], cnt[0:1, 0:NX + 1]).then_inc(route_done, 1)
            dve.wait_ge(g_exp, 1)
            for t, (t0, n) in enumerate(TILES):
                last = v.reciprocal(gsum[0:n, t:t + 1], gsum[0:n, t:t + 1])
            link(last)
            for t, (t0, n) in enumerate(TILES):
                last = v.tensor_scalar(gates[0:n, t, :], gates[0:n, t, :], gsum[0:n, t:t + 1], None, ALU.mult)
            link(last)
            dve.wait_ge(slots_in, 32)
            v.tensor_scalar(tok_ix[0:BT, :], slots[0:BT, :], 2, None, ALU.logical_shift_right)
            v.tensor_scalar(row_ix[:], slots[:], 2.0, const("half"), ALU.mult, ALU.add).then_inc(ix_done, 1)

            def expert(par, n):
                dve.wait_ge(slot_used, n * RING + PRE)
                v.tensor_scalar(glu, ps[:, 2 + par, :], LIMIT, None, ALU.min).then_inc(glu_sb, 1)
                v.tensor_scalar(lin, ps[:, 4 + par, :], LIMIT, -LIMIT, ALU.min, ALU.max).then_inc(dve_moe, 1)
                dve.wait_ge(dve_moe, n * 2 + 1)
                dve.wait_ge(glu_sb, n + 1)
                v.scalar_tensor_tensor(lin, lin, 1.0, glu, ALU.add, ALU.mult).then_inc(dve_moe, 1)
                dve.wait_ge(dve_moe, n * 2 + 2)
                dve.wait_ge(sig_sb, n + 1)
                v.tensor_tensor(act_m, lin, sig, ALU.mult).then_inc(act_sb, 1)
                dve.wait_ge(slot_used, n * RING + RING)
                dve.wait_ge(y_free, n + 1)
                v.tensor_copy(y_out[par], ps[:, 7, :]).then_inc(y_sb, 1)

            with dve.Fori(0, NE // 2) as i:
                for par in range(2):
                    expert(par, i * 2 + par)
            dve.wait_ge(route_done, 1)
            n_extra = dve.value_load(eid[0:1, NX:NX + 1], min_val=0, max_val=NX)
            with dve.Fori(0, NX) as i:
                with dve.If(i < n_extra):
                    expert(0, i + NE)
                dve.nop()

            st = Steps(dve, dve_tail)
            link = st.link
            for t, (t0, n) in enumerate(TILES):
                dve.wait_ge(moe_done, 1)
                dve.wait_ge(y_in[t], 16)
                y = ring[0:n, t, :].rearrange("p (k d) -> p k d", k=TOPK)
                acc = ysum[0:n, t % 2, :]
                if t == 2:
                    dve.wait_ge(yt_ps, 1)
                link(v.tensor_scalar(acc, y[:, 0, :], gates[0:n, t, 0:1], None, ALU.mult))
                for k in range(1, TOPK - 1):
                    link(v.scalar_tensor_tensor(acc, y[:, k, :], gates[0:n, t, k:k + 1], acc, ALU.mult, ALU.add))
                v.scalar_tensor_tensor(acc, y[:, TOPK - 1, :], gates[0:n, t, TOPK - 1:TOPK], acc, ALU.mult, ALU.add).then_inc(ys_sb, 1)
            for t, (t0, n) in enumerate(TILES):
                dve.wait_ge(yt_ps, t + 1)
                for m in range(KD):
                    src = ps[:, 2 * t + m // 4, (m % 4) * n:(m % 4 + 1) * n]
                    if t < 2:
                        last = v.scalar_tensor_tensor(xT[:, m, t0:t0 + n], src, modT[:, 5, m, 0:1], xT[:, m, t0:t0 + n], ALU.mult, ALU.add)
                    else:
                        w = ff_tail[:, m, :].rearrange("p (b l) -> p b l", l=LS)
                        last = v.tensor_tensor(w, src.rearrange("p (b l) -> p b l", l=LS), modT[:, 5, m, 1:9, None].to_broadcast([P, NB, LS]), ALU.mult)
            link(last)
            link(v.tensor_tensor(xT[:, :, NP_TOK:T], xT[:, :, NP_TOK:T], ff_tail, ALU.add))
            v.tensor_tensor(sq_tail, xT, xT, ALU.mult).then_inc(sq3_sb, 1)
            dve.wait_ge(rms_sb, 3)
            link(v.reciprocal(rstd_tail, rstd_tail))
            for k in range(KD):
                last = v.scalar_tensor_tensor(xT[:, k, :], xT[:, k, :], vT[:, V_GF + k:V_GF + k + 1], rstd_tail, ALU.mult, ALU.mult)
            last.then_inc(fin_sb, 1)

        @block.gpsimd
        def _(pool):
            g = nc.gpsimd
            g.iota(fill[:], pattern=[[0, NCOL]], base=FREE, channel_multiplier=0).then_inc(fill_ix, 1)
            g.iota(asg[:].rearrange("p (t k) -> p t k", k=TOPK), pattern=[[P * TOPK, 3], [1, TOPK]], base=0, channel_multiplier=TOPK).then_inc(fill_ix, 1)
            pool.wait_ge(fill_ix, 2)
            pool.dma_start(slot_rows.rearrange("(p a) o -> p (a o)", a=NCOL), fill[0:BT, :]).then_inc(fill_out, 16)
            pool.wait_ge(fill_out, 16)
            pool.wait_ge(slots_sb, 1)
            for t, (t0, n) in enumerate(TILES):
                for k in range(TOPK):
                    j = TOPK * t + k
                    pool.indirect_dma_start(out=slot_rows, out_offset=bass.IndirectOffsetOnAxis(ap=sloti[0:n, j:j + 1], axis=0),
                                            in_=asg[0:n, j:j + 1], in_offset=None).then_inc(scat, 16)
            pool.wait_ge(scat, 16 * 3 * TOPK)
            for half in range(2):
                pool.dma_start(slots[BT * half:BT * half + BT, :], slot_rows.rearrange("(p a) o -> p (a o)", a=NCOL)).then_inc(slots_in, 16)
            pool.wait_ge(ix_done, 1)
            pool.wait_ge(h2_out, 48)
            pool.wait_ge(zero_sb, 3)

            def gather(par, col, turn):
                g.tensor_copy(tok_col[0:BT, par:par + 1], tok_ix[0:BT, bass.ds(col, 1)]).then_inc(ix_sb, 1)
                pool.wait_ge(ix_sb, turn)
                pool.sem_inc(turns, 1)
                pool.indirect_dma_start(out=x_in[par][0:BT, :], out_offset=None, in_=h2_rows,
                                        in_offset=bass.IndirectOffsetOnAxis(ap=tok_col[0:BT, par:par + 1], axis=0),
                                        bounds_check=T - 1, oob_is_err=False).then_inc(x_land[par], 16)

            def scatter(par, col, turn):
                g.tensor_copy(row_col[:, par:par + 1], row_ix[:, bass.ds(col, 1)]).then_inc(ix_sb, 1)
                pool.wait_ge(ix_sb, turn)
                pool.sem_inc(turns, 1)
                pool.indirect_dma_start(out=y_rows, out_offset=bass.IndirectOffsetOnAxis(ap=row_col[:, par:par + 1], axis=0),
                                        in_=y_out[par], in_offset=None, bounds_check=T * TOPK * 2 - 1, oob_is_err=False).then_inc(y_sent[par], 16)

            pool.sem_inc(y_free, 2)
            gather(0, 0, 1)
            gather(1, 1, 2)
            with pool.Fori(0, NE // 2) as i:
                for par in range(2):
                    n = i * 2 + par
                    pool.wait_ge(y_sb, n + 1)
                    scatter(par, n, n * 2 + 3)
                    pool.wait_ge(xe_ps, n + 1)
                    gather(par, n + 2, n * 2 + 4)
                    pool.wait_ge(y_sent[par], (i + 1) * 16)
                    pool.sem_inc(y_free, 1)
            pool.wait_ge(x_land[0], 16 * (NE // 2 + 1))
            pool.wait_ge(x_land[1], 16 * (NE // 2 + 1))
            pool.wait_ge(route_done, 1)
            n_extra = pool.value_load(eid[0:1, NX:NX + 1], min_val=0, max_val=NX)
            with pool.Fori(0, NX) as i:
                with pool.If(i < n_extra):
                    pool.wait_ge(y_sb, i + NE + 1)
                    scatter(0, i + NE, i * 2 + 2 * NE + 3)
                    gather(0, i + NE + 1, i * 2 + 2 * NE + 4)
                    pool.wait_ge(y_sent[0], (i + (NE // 2 + 1)) * 16)
                    pool.sem_inc(y_free, 1)
                    pool.wait_ge(x_land[0], (i + (NE // 2 + 2)) * 16)
                pool.nop()
            pool.nop().then_inc(moe_done, 1)


_INS = ['x_prompt', 'x_sample', 'cache_k', 'cache_v', 'state_gla', 'page_table', 'c_prompt', 'c_sample',
        'w_ada', 'b_ada', 'g_norm1', 'w_in', 'w_gla_a2', 'b_gla_a2', 'g_gla_head', 'w_proj_gla', 'w_proj_moba',
        'w_out', 'g_norm2', 'w_router', 'b_router', 'w_gate_up', 'b_gate_up', 'w_down', 'b_down', 'g_final']
_OUTS = [(1, 256, 1024), (8, 8, 1024), (1, 1, 256, 8, 64), (1, 1, 256, 8, 64), (1, 1, 4, 128, 256),
         (1, 8, 8, 8, 64), (1, 8, 8, 8, 64), (1, 8, 4, 128, 256)]


def kernel(**inputs):
    import numpy as np
    import concourse.bacc as bacc
    from concourse.bass_utils import run_bass_kernel_spmd

    nc = bacc.Bacc("TRN2", target_bir_lowering=False, num_devices=1)
    arrays = {f"in_{name}": np.ascontiguousarray(inputs[name]) for name in _INS}
    arrays["in_consts"] = constants()
    args = [nc.dram_tensor(n, a.shape, mybir.dt.from_np(a.dtype), kind="ExternalInput").ap() for n, a in arrays.items()]
    args += [nc.dram_tensor(f"out_{i}", shape, F32, kind="ExternalOutput").ap() for i, shape in enumerate(_OUTS)]
    decoder_layer(nc, *args)
    r = run_bass_kernel_spmd(nc, [arrays], core_ids=[0])
    return tuple(r.results[0][f"out_{i}"] for i in range(len(_OUTS)))
```

```python
from contextlib import ExitStack

import concourse.bass as bass
from concourse import mybir

F32 = mybir.dt.float32
I32 = mybir.dt.int32
U32 = mybir.dt.uint32
ACT = mybir.ActivationFunctionType
ALU = mybir.AluOpType
AX = mybir.AxisListType.X

P = 128
D = 1024
KD = D // P
NP_TOK, NB, LS = 256, 8, 8
NS_TOK = NB * LS
T = NP_TOK + NS_TOK
TILES = ((0, 128), (128, 128), (256, 64))
GH, DK, DV = 4, 128, 256
CH = 16
MH, HD = 8, 64
PAIRS = MH // 2
PAGE, NPAGES = 128, 8
BLOCK = 256
NBLK = PAGE * NPAGES // BLOCK
NEG = -1e30
GATE_NORM = 16.0
LEVELS = (16, 32, 64)
CLAMP = 38.0 * GATE_NORM
EPS = 1e-6
NE, TOPK = 32, 4
BT = 64
NX = 19
NCOL = 52
FREE = 4096
LIMIT, ALPHA = 7.0, 1.702
C_GQ, C_GK, C_GV, C_GR, C_GA = 0, 512, 1024, 2048, 3072
C_MQ, C_MK, C_MV, C_BA, C_BB = 3088, 3600, 4112, 4624, 5648
SLOT = 4096
RING = 6
PRE = 4

NMEM = 28184

V_BADA, V_G1, V_G2, V_GF, V_BA2, V_GH = 0, 48, 56, 64, 72, 76
NVEC = 78

CST = {}
_at = 0
for _name, _n in (("ident", 128), ("ones", 128), ("gla_p", 512), ("gla_s", 64), ("rows_s", 8),
                  ("causal", 384), ("own", 512), ("cos", 96), ("sin", 96), ("before", 128), ("iota", 32),
                  ("tri", 16), ("scan", 320), ("row0", 64), ("half", 1)):
    CST[_name] = (_at, _n)
    _at += _n
NCST = _at


def constants():
    import numpy as np

    c = {n: np.zeros((P, w), np.float32) for n, (_, w) in CST.items()}
    r = np.arange(P)[:, None]
    q = np.arange(P)[None, :]
    c["ident"][:] = r == q
    c["ones"][:] = 1
    c["gla_p"][:, 0:P] = (r <= q) & (r // CH == q // CH)
    for j, w in enumerate(LEVELS):
        c["gla_p"][:, P * (j + 1):P * (j + 2)] = (r // (2 * w) == q // (2 * w)) & (r // w % 2 == 0) & (q // w % 2 == 1)
    c["gla_s"][:64] = ((r <= q) & (r // LS == q // LS))[:64, :64]
    c["rows_s"][:64] = (r // LS == np.arange(8))[:64]
    c["causal"][:, 0:128] = np.where(q <= r, 0, NEG)
    c["causal"][:, 256:384] = np.where(q <= r, 0, NEG)
    col = np.arange(64)[None, :]
    for b in range(NB):
        c["own"][:, 64 * b:64 * b + 64] = np.where((col // LS == b) & (col % LS <= r % LS), 0, NEG)
    half = HD // 2
    inv = (np.float32(1.0) / (np.float32(10000.0) ** (np.arange(half, dtype=np.float32) / np.float32(half)))).astype(np.float32)
    for t, (t0, n) in enumerate(TILES):
        pos = np.arange(t0, t0 + P) if t < 2 else PAGE * NPAGES + np.arange(P) % LS
        ang = (pos.astype(np.float32)[:, None] * inv[None, :]).astype(np.float32)
        c["cos"][:, half * t:half * t + half] = np.cos(ang)
        c["sin"][:, half * t:half * t + half] = np.sin(ang)
    c["before"][:] = r < q
    c["iota"][:] = np.arange(32)
    c["tri"][:] = (np.arange(4)[None, :] < np.arange(4)[:, None]).astype(np.float32).reshape(1, 16)
    s = np.ones(T, np.float32)
    s[0:NP_TOK:CH] = 0
    s[NP_TOK::LS] = 0
    c["scan"][:] = s
    c["row0"][0] = 1
    c["half"][64:] = 1
    return np.ascontiguousarray(np.concatenate([c[n] for n in CST], axis=1))


class Steps:

    def __init__(self, engine, sem):
        self.engine, self.sem, self.fixed, self.local, self.loop, self.per = engine, sem, 0, 0, None, 0

    def link(self, ins):
        ins.then_inc(self.sem, 1)
        self.local += 1
        done = self.fixed + self.local
        self.engine.wait_ge(self.sem, done if self.loop is None else self.loop * self.per + done)

    def enter(self, loop, per):
        self.fixed, self.local, self.loop, self.per = self.fixed + self.local, 0, loop, per

    def leave(self, times):
        assert self.local == self.per, (self.local, self.per)
        self.fixed, self.local, self.loop = self.fixed + times * self.per, 0, None


def decoder_layer(nc, x_prompt, x_sample, cache_k, cache_v, state_gla, page_table, c_prompt, c_sample,
                  w_ada, b_ada, g_norm1, w_in, w_gla_a2, b_gla_a2, g_gla_head, w_proj_gla, w_proj_moba,
                  w_out, g_norm2, w_router, b_router, w_gate_up, b_gate_up, w_down, b_down, g_final, consts,
                  y_prompt, y_sample, k_prompt, v_prompt, gla_prompt, k_sample, v_sample, gla_sample):
    with ExitStack() as ctx:
        def sb(name, shape, dt=F32):
            return ctx.enter_context(nc.sbuf_tensor(name, shape, dt))

        def sem(name):
            return ctx.enter_context(nc.semaphore(name))

        h2_rows = nc.dram_tensor("h2_rows", [T, D], F32, kind="Internal").ap()
        y_rows = nc.dram_tensor("y_rows", [T * TOPK * 2, D // 2], F32, kind="Internal").ap()
        slot_rows = nc.dram_tensor("slot_rows", [BT * NCOL, 1], I32, kind="Internal").ap()

        ring = sb("ring", [P, RING, SLOT])
        mem = sb("mem", [P, NMEM])
        late = ring[:, PRE:RING, :].rearrange("p a b -> p (a b)")

        def part(base, at, *dims):
            n = 1
            for d in dims:
                n *= d
            v = base[:, at:at + n]
            if len(dims) == 2:
                v = v.rearrange("p (a b) -> p a b", b=dims[1])
            if len(dims) == 3:
                v = v.rearrange("p (a b c) -> p a b c", b=dims[1], c=dims[2])
            return v

        cst = mem[:, 0:NCST]

        def const(name):
            a, n = CST[name]
            return mem[:, a:a + n]

        ident, ones = const("ident"), const("ones")
        o = NCST
        xT = part(mem, o, KD, T)
        hT = part(mem, o + 2560, KD, T)
        grT = part(mem, o + 5120, KD, T)
        sq = grT
        v_tok = part(mem, o + 7680, 3, D)
        x_tok = v_tok
        oTm = part(mem, o + 7680, PAIRS, T)
        h2_tok = v_tok
        gqT = part(mem, o + 10752, GH, T)
        gkT = part(mem, o + 12032, GH, T)
        oTg = part(mem, o + 10752, KD, T)
        mqT = part(mem, o + 13312, PAIRS, T)
        mkT = part(mem, o + 14592, PAIRS, T)
        mv_tok = part(mem, o + 15872, 3, MH * HD)
        g0 = o + 17408
        state = part(mem, g0, GH, DV)
        o_tok = part(mem, g0 + 1024, D)
        q32, k32, q64, k64 = (part(mem, g0 + 3072 + 1024 * j, GH, NP_TOK) for j in range(4))
        q128 = part(mem, g0 + 2048, GH, NP_TOK)
        k128 = part(late, 5120, GH, NP_TOK)
        k_tok = part(late, 6144, 2, GH * DK)
        km = part(mem, g0 + 3072, 2, 8, DK)
        qm = part(late, 5120, 2, 8, NS_TOK)
        rot = part(mem, g0, 2, 3, MH * HD)
        pin = part(mem, g0, 2, 384)
        pexp = part(mem, g0 + 768, 2, 384)
        ptp = part(mem, g0 + 1536, 2, 384)
        om_tok = part(mem, g0 + 2304, 2, MH * HD)
        kTs = part(mem, g0, PAIRS, PAGE * NPAGES)
        pex = part(mem, g0 + 4096, PAGE * NPAGES + NS_TOK)
        pts = part(mem, g0 + 5184, NPAGES, P)
        pto = part(mem, g0 + 6208, P)
        qs = part(mem, g0 + 6336, PAIRS, 32)
        osm = part(mem, g0 + 6464, P)
        e0 = g0 + 7168
        modT = part(mem, e0, 6, KD, 9)
        vT = part(mem, e0 + 432, NVEC)
        w_ga = part(mem, e0 + 512, KD, 16)
        wa2 = part(mem, o + 13312, GH * DK)
        gaT = part(late, 7488, T)
        w_rt = part(mem, e0 + 640, KD, NE)
        b_rt = part(mem, e0 + 896, NE)
        small = e0 + 928
        s1 = part(mem, small, KD, 9)
        colA = part(mem, small + 72, 16)
        colB = part(mem, small + 88, 16)
        colC = part(mem, small + 104, 16)
        colD = part(mem, small + 120, 16)
        eps = part(mem, small + 136, 1)
        eqT = part(late, 0, GH, T)
        ekT = part(late, 1280, GH, T)
        e0T = part(late, 2560, GH, T)
        elT = part(late, 3840, GH, T)
        baT = part(late, 0, KD, T)
        bbT = part(late, 2560, KD, T)
        craw = part(late, 0, D)
        cexp = part(late, 1024, D)
        bT = part(late, 5120, GH, T)
        rstd = part(late, 6400, T)
        scT = part(late, 6720, KD, 32)
        mod_sb = part(late, 6976, 512)
        vraw = part(late, 6976, P)
        att = part(late, 7488, 2, P)
        edec = part(late, 7744, GH, 24)
        tmp = part(late, 7840, 320)
        e32 = part(late, 8096, GH, 8)
        e64 = part(late, 8128, GH, 4)
        e128 = part(late, 8144, GH, 2)
        m0 = o + 10752
        bias = [part(mem, m0, 3072), part(mem, m0 + 3072, 3072)]
        x_in = [part(mem, m0 + 6144, D), part(mem, m0 + 7168, D)]
        xeT = [part(mem, m0 + 8192, KD, BT), part(mem, m0 + 8704, KD, BT)]
        glu = part(mem, m0 + 9216, 512)
        lin = part(mem, m0 + 9728, 512)
        sig = part(mem, m0 + 10240, 512)
        act_m = part(mem, m0 + 10752, 512)
        actT = part(mem, m0 + 11264, 4, 2, BT)
        y_out = [part(mem, m0 + 11776, 512), part(mem, m0 + 12288, 512)]
        r0 = o + 5120
        lg = part(mem, r0, 3, NE)
        top = part(mem, r0 + 96, 3, 8)
        topf = part(mem, r0 + 120, 3, 8)
        oh = part(mem, r0 + 144, 3, TOPK, NE)
        pick = part(mem, r0 + 528, 3, NE)
        pos = part(mem, r0 + 624, 3, NE)
        cnt = part(mem, r0 + 720, NE)
        xtra = part(mem, r0 + 752, NE)
        xend = part(mem, r0 + 784, NE)
        nblk = part(mem, r0 + 816, 3, NE)
        base = part(mem, r0 + 912, 3, NE)
        rtmp = part(mem, r0 + 1008, TOPK, NE)
        slotf = part(mem, r0 + 1136, 3, TOPK)
        gates = part(mem, r0 + 1148, 3, TOPK)
        gsum = part(mem, r0 + 1160, 3)
        xcmp = part(mem, r0 + 1164, NX, NE)
        ysum = part(mem, o + 2560, 2, D)
        sq_tail = part(mem, o + 7680, KD, T)
        rstd_tail = part(mem, o + 10240, T)
        ff_tail = part(mem, m0 + 6144, KD, NS_TOK)
        topi = sb("topi", [P, 3, 8], U32)
        sloti = sb("sloti", [P, 3 * TOPK], I32)
        asg = sb("asg", [P, 3 * TOPK], I32)
        fill = sb("fill", [P, NCOL], I32)
        slots = sb("slots", [P, NCOL], I32)
        tok_ix = sb("tok_ix", [P, NCOL], I32)
        row_ix = sb("row_ix", [P, NCOL], I32)
        tok_col = sb("tok_col", [P, 2], I32)
        row_col = sb("row_col", [P, 2], I32)
        eid = sb("eid", [P, NX + 1], I32)
        ptab = sb("ptab", [P, NB * NPAGES], I32)

        ps = ctx.enter_context(nc.psum_tensor("ps", [P, 8, 512], F32))

        land = [sem(f"land{i}") for i in range(RING)]
        slot_used = sem("slot_used")
        s0_used = sem("s0_used")
        cst_in, vec_in, c_in, x_in_s, wsm_in, pt_in = (sem(n) for n in ("cst_in", "vec_in", "c_in", "x_land", "wsm_in", "pt_in"))
        dve_step, act_step, eps_sb = sem("dve_step"), sem("act_step"), sem("eps_sb")
        vecT_ps, vecT_sb, c_exp, c_silu, cT_ps, cT_sb = (sem(n) for n in ("vecT_ps", "vecT_sb", "c_exp", "c_silu", "cT_ps", "cT_sb"))
        xT_ps, xT_sb, sq_sb, ss_ps = (sem(n) for n in ("xT_ps", "xT_sb", "sq_sb", "ss_ps"))
        ada_ps, mod_rows, modT_ps, mod_done = (sem(n) for n in ("ada_ps", "mod_rows", "modT_ps", "mod_done"))
        hp_sb, h_done, hs_done, rms_sb = sem("hp_sb"), sem("h_done"), sem("hs_done"), sem("rms_sb")
        fm_ps, fm_sb, gr_sb, tm_ps, tm_sb = (sem(n) for n in ("fm_ps", "fm_sb", "gr_sb", "tm_ps", "tm_sb"))
        gla_d, gla_a, q128_sb = sem("gla_d"), sem("gla_a"), sem("q128_sb")
        kt_ps, kt_sb, km_sb, qm_sb, att_ps, att_sb, d_ps, s_new, o_part, o_ps = (
            sem(n) for n in ("kt_ps", "kt_sb", "km_sb", "qm_sb", "att_ps", "att_sb", "d_ps", "s_new", "o_part", "o_ps"))
        o_sq, o_norm, ot_ps, ot_sb = (sem(n) for n in ("o_sq", "o_norm", "ot_ps", "ot_sb"))
        ms_ps, ms_max, ms_exp, mt_ps, mt_sb, mo_ps, mo_sb, mot_ps, mot_sb = (
            sem(n) for n in ("ms_ps", "ms_max", "ms_exp", "mt_ps", "mt_sb", "mo_ps", "mo_sb", "mot_ps", "mot_sb"))
        q_sb, kt2_ps, kt2_sb, cs_ps, cs_max, cs_exp, cp_ps, cp_a, cp_d, co_ps, co_sb, cot_ps, cot_sb = (
            sem(n) for n in ("q_sb", "kt2_ps", "kt2_sb", "cs_ps", "cs_max", "cs_exp", "cp_ps", "cp_a", "cp_d",
                             "co_ps", "co_sb", "cot_ps", "cot_sb"))
        pj_ps, pj_sb, sq2_sb, ss2_ps, rt_ps, h2t_ps, h2t_sb, h2_out = (
            sem(n) for n in ("pj_ps", "pj_sb", "sq2_sb", "ss2_ps", "rt_ps", "h2t_ps", "h2t_sb", "h2_out"))
        fill_ix, fill_out, picked, rank_ps, slots_sb, g_max, g_exp, scat, slots_in, ix_done, route_done = (
            sem(n) for n in ("fill_ix", "fill_out", "picked", "rank_ps", "slots_sb", "g_max", "g_exp", "scat", "slots_in",
                             "ix_done", "route_done"))
        v_land = [sem("v_land0"), sem("v_land1")]
        x_land = [sem("xg_land0"), sem("xg_land1")]
        b_land = [sem("b_land0"), sem("b_land1")]
        y_sent = [sem("y_sent0"), sem("y_sent1")]
        ix_sb, xe_ps, xe_sb, glu_sb, sig_sb, act_sb, at_ps, at_sb, y_sb = (
            sem(n) for n in ("ix_sb", "xe_ps", "xe_sb", "glu_sb", "sig_sb", "act_sb", "at_ps", "at_sb", "y_sb"))
        dve_moe, zero_sb, moe_done, y_free, ys_sb, yt_ps, x3_sb, sq3_sb, ss3_ps, fin_sb, ft_ps, ft_sb, dve_tail = (
            sem(n) for n in ("dve_moe", "zero_sb", "moe_done", "y_free", "ys_sb", "yt_ps", "x3_sb", "sq3_sb", "ss3_ps", "fin_sb",
                             "ft_ps", "ft_sb", "dve_tail"))
        y_in = [sem(f"y_in{t}") for t in range(3)]
        turns = sem("turns")
        k_out, v_out, gs_out, y_stored = (sem(n) for n in ("k_out", "v_out", "gs_out", "y_stored"))

        N_ADA = [[0, 1, 2, 3], [7, 9, 11, 13], [15, 17, 19, 20]]
        N_GQ, N_GK, N_TM, N_GR = 4, 5, (6, 8, 10, 12, 14), (16, 18)
        N_S0, N_BA, N_CACHE, N_PROJ = 21, 23, 27, 43
        N_PRE = 48
        w_in2 = w_in[0]
        w2d = {N_GQ: (w_in2, C_GQ), N_GK: (w_in2, C_GK)}
        for c, c0 in enumerate((C_GV, C_GV + 512, C_MQ, C_MK, C_MV)):
            w2d[N_TM[c]] = (w_in2, c0)
        for c in range(2):
            w2d[N_GR[c]], w2d[N_BA + c], w2d[N_BA + 2 + c] = (w_in2, C_GR + 512 * c), (w_in2, C_BA + 512 * c), (w_in2, C_BB + 512 * c)
        for n, w, c0 in ((N_PROJ, w_proj_gla, 0), (N_PROJ + 1, w_proj_gla, 512), (N_PROJ + 3, w_out, 0), (N_PROJ + 4, w_out, 512)):
            w2d[n] = (w[0], c0)
        ada_of = {N_ADA[g][q]: (g, q) for g in range(3) for q in range(4)}
        landed, total = {}, [0] * PRE
        for n in range(N_PRE):
            pages = N_CACHE <= n < N_PROJ
            if pages and (n - N_CACHE) % 2:
                continue
            total[n % PRE] += 16 * (NPAGES if pages else 1)
            landed[n] = total[n % PRE]
        land0 = total + [0, 0]
        used = {}
        for n, (g, q) in ada_of.items():
            used[n] = (ada_ps, 4 * g + q + 1)
        for j in range(4):
            used[N_BA + j] = (fm_ps, 33 + 4 * j)
        used[N_GQ], used[N_GK] = (fm_ps, 5), (fm_ps, 9)
        for c in range(5):
            used[N_TM[c]] = (tm_ps, 3 * c + 3)
        used[N_GR[0]], used[N_GR[1]] = (fm_ps, 17), (fm_ps, 21)
        for half in range(2):
            used[N_S0 + half] = (s0_used, 16 * (half + 1))
        for b in range(NB):
            used[N_CACHE + 2 * b], used[N_CACHE + 2 * b + 1] = (kt2_ps, 8 * b + 8), (co_ps, b + 1)
        for j, jobs in enumerate((4, 8, 16, 20, 24)):
            used[N_PROJ + j] = (pj_ps, jobs)

        def item(n):
            return ring[:, n % PRE, :].rearrange("p (a b) -> p a b", b=512)

        def wait_item(eng, n):
            eng.wait_ge(land[n % PRE], landed[n])

        k_pages = cache_k[0].rearrange("n s h d -> n s (h d)")
        v_pages = cache_v[0].rearrange("n s h d -> n s (h d)")
        block = ctx.enter_context(nc.Block())

        @block.sync
        def _(sp):
            sp.dma_start(cst, consts).then_inc(cst_in, 16)
            sp.dma_start(craw[0:1, :], c_prompt).then_inc(c_in, 16)
            sp.dma_start(craw[1:9, :], c_sample).then_inc(c_in, 16)
            for vec, at, n in ((b_ada, V_BADA, 48), (g_norm1, V_G1, 8), (g_norm2, V_G2, 8), (b_gla_a2, V_BA2, 4), (g_gla_head, V_GH, 2)):
                sp.dma_start(vraw[at:at + n, :], vec[0].rearrange("(a b) -> a b", b=P)).then_inc(vec_in, 16)
            sp.dma_start(vraw[V_GF:V_GF + 8, :], g_final.rearrange("(a b) -> a b", b=P)).then_inc(vec_in, 16)
            sp.dma_start(x_tok[:, 0:2, :], x_prompt[0].rearrange("(a p) d -> p a d", p=P)).then_inc(x_in_s, 16)
            sp.dma_start(x_tok[0:64, 2, :], x_sample.rearrange("b l d -> (b l) d")).then_inc(x_in_s, 16)
            sp.dma_start(w_ga, w_in2[:, C_GA:C_GA + 16].rearrange("(k p) n -> p k n", p=P)).then_inc(wsm_in, 16)
            sp.dma_start(wa2[0:16, :], w_gla_a2[0]).then_inc(wsm_in, 16)
            sp.dma_start(w_rt, w_router[0].rearrange("(k p) n -> p k n", p=P)).then_inc(wsm_in, 16)
            sp.dma_start(b_rt, b_router.to_broadcast([P, NE])).then_inc(wsm_in, 16)
            sp.dma_start(ptab[0:1, :], page_table.rearrange("(o b) n -> o (b n)", o=1)).then_inc(pt_in, 16)

            def load(n):
                if n >= PRE:
                    sp.wait_ge(*used[n - PRE])
                if n in w2d:
                    w, c0 = w2d[n]
                    sp.dma_start(item(n), w[:, c0:c0 + 512].rearrange("(k p) n -> p k n", p=P)).then_inc(land[n % PRE], 16)
                elif n in ada_of:
                    g, q = ada_of[n]
                    sp.dma_start(ring[:, n % PRE, :].rearrange("p (k n) -> p k n", k=2),
                                 w_ada[0, 2 * P * q:2 * P * (q + 1), 2048 * g:2048 * (g + 1)].rearrange("(k p) n -> p k n", p=P)).then_inc(land[n % PRE], 16)
                elif n in (N_S0, N_S0 + 1):
                    b = 4 * (n - N_S0)
                    sp.dma_start(ring[:, n % PRE, :].rearrange("p (b n) -> p b n", n=DV),
                                 state_gla[0, b:b + 4].rearrange("b h k v -> k (b h) v")).then_inc(land[n % PRE], 16)
                else:
                    sp.dma_start(ring[:, n % PRE, :].rearrange("p (k n) -> p k n", n=D),
                                 w_proj_moba[0].rearrange("(k p) n -> p k n", p=P)).then_inc(land[n % PRE], 16)

            for n in range(N_S0 + PRE):
                load(n)
            sp.wait_ge(tm_sb, 12)
            sp.dma_start(k_prompt[0, 0].rearrange("(a p) h d -> p a (h d)", p=P), rot[:, 1, 0:2, :]).then_inc(k_out, 16)
            sp.dma_start(k_sample[0].rearrange("b l h d -> (b l) (h d)"), rot[0:64, 1, 2, :]).then_inc(k_out, 16)
            sp.wait_ge(tm_sb, 15)
            sp.dma_start(v_prompt[0, 0].rearrange("(a p) h d -> p a (h d)", p=P), mv_tok[:, 0:2, :]).then_inc(v_out, 16)
            sp.dma_start(v_sample[0].rearrange("b l h d -> (b l) (h d)"), mv_tok[0:64, 2, :]).then_inc(v_out, 16)
            sp.wait_ge(s_new, 2 * GH)
            sp.dma_start(gla_prompt[0, 0].rearrange("h k v -> k h v"), state).then_inc(gs_out, 16)
            for half in range(2):
                sp.wait_ge(s_new, 2 * GH + 8 * GH)
                n = N_S0 + half
                sp.dma_start(gla_sample[0, 4 * half:4 * half + 4].rearrange("b h k v -> k (b h) v"),
                             ring[:, n % PRE, :].rearrange("p (b n) -> p b n", n=DV)).then_inc(s0_used, 16)
                sp.wait_ge(s0_used, 16 * (half + 1))
            for n in range(N_S0 + PRE, N_CACHE):
                load(n)
            sp.wait_ge(pt_in, 16)
            def key_pages(b, par):
                n = N_CACHE + 2 * par
                for j in range(NPAGES):
                    page = sp.value_load(ptab[0:1, bass.ds(b * NPAGES + j, 1)], min_val=0, max_val=cache_k.shape[1] - 1)
                    sp.dma_start(item(n)[:, j, :], k_pages[bass.ds(page, 1)].rearrange("o s n -> s (o n)")).then_inc(land[n % PRE], 16)

            for b in range(2):
                sp.wait_ge(*used[N_CACHE + 2 * b - PRE])
                key_pages(b, b)
            with sp.Fori(1, NB // 2) as i:
                for par in range(2):
                    b = i * 2 + par
                    sp.wait_ge(kt2_ps, b * 8 - 8)
                    sp.sem_inc(turns, 1)
                    key_pages(b, par)
            for n in range(N_PROJ, N_PRE):
                load(n)

            def expert_slot(e, s):
                if s < PRE:
                    sp.dma_start(ring[:, s, :].rearrange("p (k n) -> p k n", k=2),
                                 w_gate_up[0, bass.ds(e, 1), 2 * P * s:2 * P * (s + 1), :].rearrange("o (k p) n -> p (o k) n", p=P)).then_inc(land[s], 16)
                else:
                    k = s - PRE
                    sp.dma_start(ring[:, s, :].rearrange("p (k n) -> p k n", k=4),
                                 w_down[0, bass.ds(e, 1), 4 * P * k:4 * P * (k + 1), :].rearrange("o (k p) n -> p (o k) n", p=P)).then_inc(land[s], 16)

            def expert_bias(e, par):
                sp.dma_start(bias[par][0:1, 0:2 * D], b_gate_up[0, bass.ds(e, 1), :]).then_inc(b_land[par], 16)
                sp.dma_start(bias[par][0:1, 2 * D:3 * D], b_down[0, bass.ds(e, 1), :]).then_inc(b_land[par], 16)

            for s in range(PRE):
                sp.wait_ge(*used[N_PRE - PRE + s])
                expert_slot(0, s)
            for t, (t0, n) in enumerate(TILES):
                sp.wait_ge(h2t_sb, 2 * t + 2)
                sp.dma_start(h2_rows[t0:t0 + n, :], h2_tok[0:n, t, :]).then_inc(h2_out, 16)
            sp.wait_ge(hs_done, 2)
            sp.wait_ge(h_done, 2 * KD)
            expert_slot(0, PRE)
            expert_slot(0, PRE + 1)
            sp.wait_ge(zero_sb, 2)
            expert_bias(0, 0)
            expert_bias(1, 1)

            def expert_loads(e):
                for s in range(RING):
                    sp.wait_ge(slot_used, e * RING + (s + 1 - RING))
                    expert_slot(e, s)

            expert_loads(1)
            with sp.Fori(1, NE // 2) as i:
                for par in range(2):
                    e = i * 2 + par
                    sp.wait_ge(slot_used, e * RING - RING)
                    expert_bias(e, par)
                    expert_loads(e)
            sp.wait_ge(route_done, 1)
            n_extra = sp.value_load(eid[0:1, NX:NX + 1], min_val=0, max_val=NX)
            with sp.If(n_extra > 0):
                with sp.Fori(0, NX) as i:
                    with sp.If(i < n_extra):
                        e = sp.value_load(eid[0:1, bass.ds(i, 1)], min_val=0, max_val=NE - 1)
                        sp.wait_ge(slot_used, (i + NE) * RING)
                        expert_bias(e, 0)
                        for s in range(RING):
                            expert_slot(e, s)
                    sp.nop()
            sp.wait_ge(moe_done, 1)
            for t, (t0, n) in enumerate(TILES):
                sp.dma_start(ring[0:n, t, :], y_rows[t0 * 8:(t0 + n) * 8, :].rearrange("(p a) d -> p (a d)", a=8)).then_inc(y_in[t], 16)
            for t, (t0, n) in enumerate(TILES):
                sp.wait_ge(ft_sb, 2 * t + 2)
                out = y_prompt[0, t0:t0 + n, :] if t < 2 else y_sample.rearrange("b l d -> (b l) d")
                sp.dma_start(out, ring[0:n, 3 + t, 0:D]).then_inc(y_stored, 16)
            sp.wait_ge(y_stored, 48)
            sp.wait_ge(k_out, 32)
            sp.wait_ge(v_out, 32)
            sp.wait_ge(gs_out, 16)
            sp.wait_ge(s0_used, 32)

        @block.tensor
        def _(pe):
            mm = nc.tensor.matmul

            def tr(out, in_, n=P):
                return nc.tensor.transpose(out, in_, ident[0:n, 0:n])

            pe.wait_ge(cst_in, 16)
            pe.wait_ge(vec_in, 96)
            tr(ps[:, 0, 0:NVEC], vraw[0:NVEC, :], NVEC).then_inc(vecT_ps, 1)
            pe.wait_ge(x_in_s, 32)
            for k in range(KD):
                if k >= 3:
                    pe.wait_ge(xT_sb, k - 2)
                for t, (t0, n) in enumerate(TILES):
                    last = tr(ps[:, 2 + k % 3, t0:t0 + n], x_tok[0:n, t, k * P:(k + 1) * P], n)
                last.then_inc(xT_ps, 1)
            pe.wait_ge(c_silu, 1)
            for k in range(KD):
                last = tr(ps[:, 1, 16 * k:16 * k + 9], craw[0:9, k * P:(k + 1) * P], 9)
            last.then_inc(cT_ps, 1)
            pe.wait_ge(sq_sb, 8)
            for k in range(KD):
                last = mm(ps[:, 5, 0:T], ones, sq[:, k, :], start=k == 0, stop=k == KD - 1)
            last.then_inc(ss_ps, 1)

            def ada(g, q):
                if q == 0 and g:
                    pe.wait_ge(mod_done, g)
                elif q == 0:
                    pe.wait_ge(cT_sb, 1)
                wait_item(pe, N_ADA[g][q])
                w = ring[:, N_ADA[g][q] % PRE, :].rearrange("p (k n) -> p k n", k=2)
                for k in range(2):
                    for j in range(4):
                        last = mm(ps[32 * j:32 * j + 32, 6, :], scT[:, 2 * q + k, :], w[:, k, 512 * j:512 * j + 512],
                                  start=q == 0 and k == 0, stop=q == 3 and k == 1)
                last.then_inc(ada_ps, 1)

            def ada_rows(g):
                pe.wait_ge(mod_rows, g + 1)
                for c in range(4):
                    last = tr(ps[:, 7, c * P:(c + 1) * P], mod_sb[:, c * P:(c + 1) * P])
                last.then_inc(modT_ps, 1)

            for q in range(4):
                ada(0, q)
            ada_rows(0)

            def fm_free(n):
                if n >= 3:
                    pe.wait_ge(fm_sb, n - 2)
                    if 13 <= n - 3 < 21:
                        pe.wait_ge(gr_sb, n - 15)

            def fm(n, w, M=P):
                fm_free(n)
                for k in range(KD):
                    if n == 0:
                        pe.wait_ge(h_done, k + 1)
                    last = mm(ps[0:M, n % 3, 0:T], w[:, k, :], hT[:, k, :], start=k == 0, stop=k == KD - 1)
                last.then_inc(fm_ps, 1)

            def fm_item(n0, it):
                wait_item(pe, it)
                for m in range(4):
                    fm(n0 + m, item(it)[:, :, m * P:(m + 1) * P])

            pe.wait_ge(hs_done, 1)
            pe.wait_ge(wsm_in, 64)
            fm(0, w_ga, 16)
            fm_item(1, N_GQ)
            fm_item(5, N_GK)
            pe.wait_ge(fm_sb, 1)
            for h in range(GH):
                fm_free(9 + h)
                mm(ps[:, (9 + h) % 3, 0:T], wa2[0:16, h * DK:(h + 1) * DK], gaT[0:16, :], start=True, stop=True).then_inc(fm_ps, 1)
            for c in range(5):
                wait_item(pe, N_TM[c])
                for t, (t0, n) in enumerate(TILES):
                    if 3 * c + t >= 3:
                        pe.wait_ge(tm_sb, 3 * c + t - 2)
                    for k in range(KD):
                        last = mm(ps[0:n, 3 + t, :], hT[:, k, t0:t0 + n], item(N_TM[c])[:, k, :], start=k == 0, stop=k == KD - 1)
                    last.then_inc(tm_ps, 1)
                if c < 4:
                    ada(1, c)
            ada_rows(1)
            ada(2, 0)
            fm_item(13, N_GR[0])
            ada(2, 1)
            fm_item(17, N_GR[1])
            ada(2, 2)
            ada(2, 3)
            pe.wait_ge(tm_sb, 12)
            for j in range(8):
                which, p = divmod(j, 4)
                fm_free(21 + j)
                for t, (t0, n) in enumerate(TILES):
                    last = tr(ps[:, (21 + j) % 3, t0:t0 + n], rot[0:n, which, t, p * P:(p + 1) * P], n)
                last.then_inc(fm_ps, 1)
            ada_rows(2)

            pe.wait_ge(fm_sb, 29)
            pe.wait_ge(gla_d, 5)
            pe.wait_ge(tm_sb, 15)
            pe.wait_ge(mod_done, 3)
            for t, (t0, n) in enumerate(TILES):
                for h in range(GH):
                    last = tr(ps[0:n, (2, 7, 3)[t], h * DK:(h + 1) * DK], (elT if t == 2 else k128)[:, h, t0:t0 + n])
            last.then_inc(kt_ps, 1)

            def att_scores(u):
                t, h = divmod(u, GH)
                cols = slice(t * P, (t + 1) * P)
                if u:
                    pe.wait_ge(att_sb, u)
                for j, (kk, qq) in enumerate(((ekT, eqT), (elT, e0T), (k32, q32), (k64, q64))):
                    last = mm(ps[:, 4, j * P:(j + 1) * P], kk[:, h, cols], qq[:, h, cols], start=True, stop=True)
                last.then_inc(att_ps, 1)

            def o_and_delta(u):
                t, h = divmod(u, GH)
                values = v_tok[:, t, h * DV:(h + 1) * DV]
                pe.wait_ge(att_sb, u + 1)
                if u >= 2:
                    pe.wait_ge(o_norm, u - 1)
                if t:
                    pe.wait_ge(s_new, h + 1)
                    pe.wait_ge(q128_sb, 1)
                    mm(ps[:, 5 + u % 2, 0:DV], q128[:, h, P:2 * P], state[:, h, :], start=True, stop=False)
                mm(ps[:, 5 + u % 2, 0:DV], att[:, u % 2, :], values, start=t == 0, stop=True).then_inc(o_part, 1)
                pe.wait_ge(kt_sb, 1)
                if u >= 2:
                    pe.wait_ge(s_new, u - 1)
                mm(ps[:, u % 2, 0:DV], k_tok[:, t, h * DK:(h + 1) * DK], values, start=True, stop=True).then_inc(d_ps, 1)

            def o_transposes(t):
                n = TILES[t][1]
                pe.wait_ge(o_norm, GH * (t + 1))
                if t:
                    pe.wait_ge(ot_sb, t)
                for m in range(KD):
                    last = tr(ps[:, 7 if m < 4 else 2, (m % 4) * n:(m % 4 + 1) * n], o_tok[0:n, m * P:(m + 1) * P], n)
                last.then_inc(ot_ps, 1)

            att_scores(0)
            for u in range(2 * GH):
                if u + 1 < 2 * GH:
                    att_scores(u + 1)
                o_and_delta(u)
                if u == GH:
                    o_transposes(0)
            n, s0 = NS_TOK, slice(NP_TOK, T)
            for h in range(GH):
                u = 2 * GH + h
                x0 = 2 * GH + 8 * h
                pe.wait_ge(att_sb, u)
                mm(ps[0:n, 4, 0:n], ekT[:, h, s0], eqT[:, h, s0], start=True, stop=True).then_inc(att_ps, 1)
                if h == 0:
                    o_transposes(1)
                    wait_item(pe, N_S0)
                    wait_item(pe, N_S0 + 1)
                pe.wait_ge(att_sb, u + 1)
                pe.wait_ge(km_sb, h + 1)
                pe.wait_ge(qm_sb, h + 1)
                pe.wait_ge(o_norm, u - 1)
                values = v_tok[0:n, 2, h * DV:(h + 1) * DV]
                mm(ps[0:n, 5 + u % 2, 0:DV], att[0:n, u % 2, 0:n], values, start=True, stop=False)

                def delta(c):
                    pe.wait_ge(s_new, x0 + c - 1)
                    mm(ps[:, c % 2, 0:DV], km[0:n, h % 2, c, :], values, start=True, stop=True).then_inc(d_ps, 1)

                delta(0)
                delta(1)
                for c in range(8):
                    prior = ring[:, (N_S0 + c // 4) % PRE, ((c % 4) * GH + h) * DV:((c % 4) * GH + h + 1) * DV]
                    mm(ps[0:n, 5 + u % 2, 0:DV], qm[:, h % 2, c, :], prior, start=False, stop=c == 7).then_inc(o_part, 1)
                    if c < 6:
                        delta(c + 2)
            o_transposes(2)

            pe.wait_ge(s_new, 10 * GH)
            pe.wait_ge(ot_sb, 3)
            for it in range(4):
                fm_item(29 + 4 * it, N_BA + it)

            pe.wait_ge(fm_sb, 45)

            def prompt_scores(h):
                p, q0 = h // 2, HD * (h % 2)
                if h >= 2:
                    pe.wait_ge(ms_max, h - 1)
                mm(ps[:, h % 2, 0:128], mqT[q0:q0 + HD, p, 0:128], mkT[q0:q0 + HD, p, 0:128], start=True, stop=True)
                mm(ps[:, h % 2, 128:384], mqT[q0:q0 + HD, p, 128:256], mkT[q0:q0 + HD, p, 0:256], start=True, stop=True).then_inc(ms_ps, 1)

            prompt_scores(0)
            for h in range(MH):
                if h + 1 < MH:
                    prompt_scores(h + 1)
                pe.wait_ge(ms_exp, h + 1)
                if h >= 2:
                    pe.wait_ge(mt_sb, h - 1)
                for j in range(3):
                    last = tr(ps[:, 3 + h % 2, j * P:(j + 1) * P], pexp[:, h % 2, j * P:(j + 1) * P])
                last.then_inc(mt_ps, 1)
                pe.wait_ge(mt_sb, h + 1)
                if h >= 2:
                    pe.wait_ge(mo_sb, h - 1)
                bank, hs = 5 + h % 2, slice(h * HD, (h + 1) * HD)
                mm(ps[:, bank, 0:HD], ptp[:, h % 2, 0:P], mv_tok[:, 0, hs], start=True, stop=True)
                mm(ps[:, bank, HD:2 * HD], ptp[:, h % 2, P:2 * P], mv_tok[:, 0, hs], start=True, stop=False)
                mm(ps[:, bank, HD:2 * HD], ptp[:, h % 2, 2 * P:3 * P], mv_tok[:, 1, hs], start=False, stop=True).then_inc(mo_ps, 1)
            pe.wait_ge(mo_sb, MH)
            for p in range(PAIRS):
                for t in range(2):
                    last = tr(ps[:, 3 + p // 2, (p % 2) * 256 + t * P:(p % 2) * 256 + (t + 1) * P], om_tok[:, t, p * P:(p + 1) * P])
            last.then_inc(mot_ps, 1)
            pe.wait_ge(mot_sb, 2)

            def probs_copied(n):
                pe.wait_ge(cp_a, n)
                pe.wait_ge(cp_d, n)

            def cache_keys(b, half, par):
                nk = N_CACHE + 2 * par
                pe.wait_ge(land[nk % PRE], half * (16 * NPAGES) + landed[nk])
                for jj in range(2 * PAIRS):
                    p, f = divmod(jj, 2)
                    if jj >= 4:
                        pe.wait_ge(kt2_sb, b * 8 + jj - 3)
                    for q in range(4):
                        last = tr(ps[:, jj % 4, q * P:(q + 1) * P], item(nk)[:, 4 * f + q, p * P:(p + 1) * P])
                    last.then_inc(kt2_ps, 1)

            def cache_scores(b):
                pe.wait_ge(kt2_sb, b * 8 + 8)
                pe.wait_ge(q_sb, b + 1)
                for f in range(2):
                    for p in range(PAIRS):
                        mm(ps[32 * p:32 * p + 32, 4 + f, :], qs[:, p, :], kTs[:, p, 512 * f:512 * f + 512], start=True, stop=True)
                for p in range(PAIRS):
                    last = mm(ps[32 * p:32 * p + 32, 6, 0:NS_TOK], qs[:, p, :], mkT[:, p, NP_TOK:T], start=True, stop=True)
                last.then_inc(cs_ps, 1)

            def cache_probs(b, keys_before):
                pe.wait_ge(kt2_sb, keys_before)
                pe.wait_ge(cs_exp, b + 1)
                for j in range(NPAGES):
                    last = tr(ps[:, j // 4, (j % 4) * P:(j % 4 + 1) * P], pex[:, j * P:(j + 1) * P])
                last = tr(ps[0:NS_TOK, 2, 0:P], pex[:, PAGE * NPAGES:])
                last.then_inc(cp_ps, 1)

            def cache_values(b, half, par):
                nv = N_CACHE + 2 * par + 1
                pe.wait_ge(v_land[par], (half + 1) * (16 * NPAGES))
                for j in range(NPAGES + 1):
                    for p in range(PAIRS):
                        if j < NPAGES:
                            last = mm(ps[32 * p:32 * p + 32, 7, 0:P], pts[:, j, 32 * p:32 * p + 32], item(nv)[:, j, p * P:(p + 1) * P],
                                      start=j == 0, stop=False)
                        else:
                            last = mm(ps[32 * p:32 * p + 32, 7, 0:P], pto[0:NS_TOK, 32 * p:32 * p + 32],
                                      mv_tok[0:NS_TOK, 2, p * P:(p + 1) * P], start=False, stop=True)
                last.then_inc(co_ps, 1)

            def cache_out(b):
                pe.wait_ge(co_sb, b + 1)
                tr(ps[:, 7, 0:P], osm).then_inc(cot_ps, 1)

            cache_keys(0, 0, 0)
            cache_scores(0)
            cache_keys(1, 0, 1)
            cache_probs(0, 15)

            def cache_turn(b, half, par):
                cache_scores(b)
                probs_copied(b)
                cache_keys(b + 1, half + par, 1 - par)
                pe.wait_ge(cot_sb, b - 1)
                cache_values(b - 1, half + par - 1, 1 - par)
                cache_probs(b, b * 8 + 15)
                cache_out(b - 1)

            with pe.Fori(0, NB // 2 - 1) as i:
                for sub in range(2):
                    cache_turn(i * 2 + 1 + sub, i + sub, 1 - sub)
            cache_scores(NB - 1)
            probs_copied(NB - 1)
            pe.wait_ge(cot_sb, NB - 2)
            cache_values(NB - 2, NB // 2 - 1, 0)
            cache_probs(NB - 1, NB * 8)
            cache_out(NB - 2)
            probs_copied(NB)
            pe.wait_ge(cot_sb, NB - 1)
            cache_values(NB - 1, NB // 2 - 1, 1)
            cache_out(NB - 1)

            for n in range(24):
                which, m = divmod(n, KD)
                it = N_PROJ + (m // 4 if which == 0 else 2 if which == 1 else 3 + m // 4)
                wait_item(pe, it)
                if n >= 4:
                    pe.wait_ge(pj_sb, n - 3)
                if n == 16:
                    pe.wait_ge(pj_sb, 16)
                kc = PAIRS if which == 1 else KD
                w = ring[:, it % PRE, :].rearrange("p (k n) -> p k n", k=kc)
                src = (oTg, oTm, hT)[which]
                c0 = m * P if which == 1 else (m % 4) * P
                for k in range(kc):
                    last = mm(ps[:, n % 4, 0:T], w[:, k, c0:c0 + P], src[:, k, :], start=k == 0, stop=k == kc - 1)
                last.then_inc(pj_ps, 1)

            pe.wait_ge(sq2_sb, 8)
            for k in range(KD):
                last = mm(ps[:, 4, 0:T], ones, sq[:, k, :], start=k == 0, stop=k == KD - 1)
            last.then_inc(ss2_ps, 1)
            pe.wait_ge(h_done, 2 * KD)
            pe.wait_ge(hs_done, 2)
            for t, (t0, n) in enumerate(TILES):
                for k in range(KD):
                    last = mm(ps[0:n, 5, NE * t:NE * t + NE], hT[:, k, t0:t0 + n], w_rt[:, k, :], start=k == 0, stop=k == KD - 1)
            last.then_inc(rt_ps, 1)
            for t, (t0, n) in enumerate(TILES):
                for f in range(2):
                    if 2 * t + f >= 4:
                        pe.wait_ge(h2t_sb, 2 * t + f - 3)
                    for q in range(4):
                        last = tr(ps[0:n, (2 * t + f) % 4, q * P:(q + 1) * P], hT[:, 4 * f + q, t0:t0 + n])
                    last.then_inc(h2t_ps, 1)
            pe.wait_ge(picked, 1)
            for t, (t0, n) in enumerate(TILES):
                for tt in range(t + 1):
                    nn = TILES[tt][1]
                    lhs = const("before")[0:nn, 0:n] if tt == t else ones[0:nn, 0:n]
                    mm(ps[0:n, 4, NE * t:NE * t + NE], lhs, pick[0:nn, tt, :], start=tt == 0, stop=tt == t)
            for tt in range(3):
                nn = TILES[tt][1]
                last = mm(ps[:, 4, 96:128], ones[0:nn, :], pick[0:nn, tt, :], start=tt == 0, stop=tt == 2)
            last.then_inc(rank_ps, 1)

            def xe_transposes(par, n, gathered):
                pe.wait_ge(x_land[par], gathered)
                pe.sem_inc(turns, 1)
                for k in range(KD):
                    last = tr(ps[:, par, k * BT:(k + 1) * BT], x_in[par][0:BT, k * P:(k + 1) * P], BT)
                last.then_inc(xe_ps, 1)

            def gate_up(par, n, biases, weights):
                pe.wait_ge(xe_sb, n + 1)
                pe.wait_ge(b_land[par], biases)
                for q in range(4):
                    out = ps[64 * (q % 2):64 * (q % 2) + 64, 2 + 2 * (q // 2) + par, :]
                    mm(out, const("row0"), bias[par][:, 512 * q:512 * q + 512], start=True, stop=False)
                for s in range(PRE):
                    pe.wait_ge(land[s], weights + land0[s])
                    w = ring[:, s, :].rearrange("p (k n) -> p k n", k=2)
                    for k in range(2):
                        for q in range(4):
                            out = ps[64 * (q % 2):64 * (q % 2) + 64, 2 + 2 * (q // 2) + par, :]
                            last = mm(out, xeT[par][:, 2 * s + k, :], w[:, k, 512 * q:512 * q + 512], start=False, stop=s == 3 and k == 1)
                    last.then_inc(slot_used, 1)

            def down(par, n, weights):
                pe.wait_ge(act_sb, n + 1)
                for c in range(4):
                    last = tr(ps[:, 6, c * P:(c + 1) * P], act_m[:, c * P:(c + 1) * P])
                last.then_inc(at_ps, 1)
                for f in range(2):
                    mm(ps[64 * f:64 * f + 64, 7, :], const("row0"), bias[par][:, 2048 + 512 * f:2560 + 512 * f], start=True, stop=False)
                pe.wait_ge(at_sb, n + 1)
                for s in range(2):
                    pe.wait_ge(land[PRE + s], weights)
                    w = ring[:, PRE + s, :].rearrange("p (k n) -> p k n", k=4)
                    for k in range(4):
                        for f in range(2):
                            last = mm(ps[64 * f:64 * f + 64, 7, :], actT[:, k, s, :], w[:, k, 512 * f:512 * f + 512], start=False, stop=s == 1 and k == 3)
                    last.then_inc(slot_used, 1)

            pe.wait_ge(slots_sb, 1)
            pe.wait_ge(h2t_sb, 6)
            with pe.Fori(0, NE // 2) as i:
                for par in range(2):
                    n = i * 2 + par
                    xe_transposes(par, n, (i + 1) * 16)
                    gate_up(par, n, (i + 1) * 32, (n + 1) * 16)
                    down(par, n, (n + 1) * 16)
            pe.wait_ge(route_done, 1)
            n_extra = pe.value_load(eid[0:1, NX:NX + 1], min_val=0, max_val=NX)
            with pe.If(n_extra > 0):
                with pe.Fori(0, NX) as i:
                    with pe.If(i < n_extra):
                        n = i + NE
                        xe_transposes(0, n, (i + (NE // 2 + 1)) * 16)
                        gate_up(0, n, (i + (NE // 2 + 1)) * 32, (n + 1) * 16)
                        down(0, n, (n + 1) * 16)
                    pe.nop()

            for t, (t0, n) in enumerate(TILES):
                pe.wait_ge(ys_sb, t + 1)
                for f in range(2):
                    for q in range(4):
                        last = tr(ps[:, 2 * t + f, q * n:(q + 1) * n], ysum[0:n, t % 2, (4 * f + q) * P:(4 * f + q + 1) * P], n)
                last.then_inc(yt_ps, 1)
            pe.wait_ge(sq3_sb, 1)
            for k in range(KD):
                last = mm(ps[:, 6, 0:T], ones, sq_tail[:, k, :], start=k == 0, stop=k == KD - 1)
            last.then_inc(ss3_ps, 1)
            pe.wait_ge(fin_sb, 1)
            for t, (t0, n) in enumerate(TILES):
                for f in range(2):
                    for q in range(4):
                        last = tr(ps[0:n, 2 * t + f, q * P:(q + 1) * P], xT[:, 4 * f + q, t0:t0 + n])
                    last.then_inc(ft_ps, 1)

        @block.scalar
        def _(act):
            a = nc.scalar
            act.wait_ge(c_in, 32)
            a.activation(cexp[0:9, :], craw[0:9, :], ACT.Exp, scale=-1.0).then_inc(c_exp, 1)
            for k in range(KD):
                act.wait_ge(xT_ps, k + 1)
                a.copy(xT[:, k, :], ps[:, 2 + k % 3, 0:T]).then_inc(xT_sb, 1)
            act.wait_ge(vecT_sb, 1)
            act.wait_ge(eps_sb, 1)
            act.wait_ge(ss_ps, 1)
            a.activation(rstd, ps[:, 5, 0:T], ACT.Sqrt, scale=1.0 / D, bias=eps).then_inc(rms_sb, 1)

            def shifted(shift, before):
                for k in range(KD):
                    act.wait_ge(hp_sb, before + k + 1)
                    a.activation(hT[:, k, 0:NP_TOK], hT[:, k, 0:NP_TOK], ACT.Identity, bias=modT[:, shift, k, 0:1]).then_inc(h_done, 1)

            shifted(0, 0)
            for n in range(13):
                act.wait_ge(fm_ps, n + 1)
                bank = ps[:, n % 3, 0:T]
                if n == 0:
                    a.copy(gaT[0:16, :], bank[0:16, :]).then_inc(fm_sb, 1)
                elif n < 5:
                    a.copy(gqT[:, n - 1, :], bank).then_inc(fm_sb, 1)
                elif n < 9:
                    a.copy(gkT[:, n - 5, :], bank).then_inc(fm_sb, 1)
                else:
                    h = n - 9
                    a.activation(elT[:, h, :], bank, ACT.Identity, bias=vT[:, V_BA2 + h:V_BA2 + h + 1]).then_inc(fm_sb, 1)
            act.wait_ge(gla_d, 1)
            a.activation(eqT, eqT, ACT.Exp).then_inc(act_step, 1)
            act.wait_ge(act_step, 1)
            a.activation(eqT, eqT, ACT.Ln, bias=1.0).then_inc(gla_a, 1)
            act.wait_ge(gla_d, 3)
            a.activation(ekT, eqT, ACT.Exp, scale=-1.0 / GATE_NORM).then_inc(act_step, 1)
            act.wait_ge(act_step, 2)
            a.activation(eqT, eqT, ACT.Exp, scale=1.0 / GATE_NORM).then_inc(act_step, 1)
            a.activation(e0T, bT, ACT.Exp, scale=1.0 / GATE_NORM).then_inc(gla_a, 1)
            act.wait_ge(gla_d, 4)
            a.activation(elT, elT, ACT.Exp, scale=1.0 / GATE_NORM).then_inc(gla_a, 1)
            for n in range(13, 21):
                act.wait_ge(fm_ps, n + 1)
                a.activation(grT[:, n - 13, :], ps[:, n % 3, 0:T], ACT.Sigmoid).then_inc(fm_sb, 1)
            for n in range(21, 29):
                act.wait_ge(fm_ps, n + 1)
                which, p = divmod(n - 21, 4)
                a.copy((mqT, mkT)[which][:, p, :], ps[:, n % 3, 0:T]).then_inc(fm_sb, 1)
            act.wait_ge(kt_ps, 1)
            a.copy(k_tok[:, 0, :], ps[:, 2, :])
            a.copy(k_tok[:, 1, :], ps[:, 7, :]).then_inc(kt_sb, 1)
            for t, (t0, n) in enumerate(TILES):
                for h in range(GH):
                    u = GH * t + h
                    act.wait_ge(o_part, u + 1 if t < 2 else 2 * GH + 8 * h + 8)
                    if u:
                        act.wait_ge(o_sq, u)
                        act.wait_ge(o_norm, u)
                    a.activation(tmp[0:n, 0:DV], ps[0:n, 5 + u % 2, 0:DV], ACT.Square, accum_out=colA[0:n, 0:1]).then_inc(act_step, 1)
                    act.wait_ge(act_step, 4 + u)
                    a.activation(colC[0:n, 0:1], colA[0:n, 0:1], ACT.Sqrt, scale=1.0 / DV, bias=eps[0:n]).then_inc(o_sq, 1)
            for n in range(29, 45):
                act.wait_ge(fm_ps, n + 1)
                m = n - 29
                a.activation((baT if m < 8 else bbT)[:, m % 8, :], ps[:, n % 3, 0:T], ACT.Sigmoid).then_inc(fm_sb, 1)
            for h in range(MH):
                act.wait_ge(ms_max, h + 1)
                if h >= 2:
                    act.wait_ge(mt_ps, h - 1)
                    act.wait_ge(mo_sb, h - 1)
                e = pexp[:, h % 2, :]
                x = pin[:, h % 2, :]
                for t, (c0, c1) in enumerate(((0, P), (P, 3 * P))):
                    last = a.activation(e[:, c0:c1], x[:, c0:c1], ACT.Exp, scale=HD ** -0.5, bias=colB[:, 2 * (h % 2) + t:2 * (h % 2) + t + 1],
                                        accum_out=colC[:, 2 * (h % 2) + t:2 * (h % 2) + t + 1])
                last.then_inc(ms_exp, 1)
                act.wait_ge(mt_ps, h + 1)
                if h >= 2:
                    act.wait_ge(mo_ps, h - 1)
                a.copy(ptp[:, h % 2, :], ps[:, 3 + h % 2, 0:384]).then_inc(mt_sb, 1)
            act.wait_ge(mot_ps, 1)
            for f in range(2):
                a.copy(oTm[:, 2 * f:2 * f + 2, 0:NP_TOK], ps[:, 3 + f, :].rearrange("p (a b) -> p a b", b=NP_TOK)).then_inc(mot_sb, 1)
            def cache_keys(b):
                for jj in range(8):
                    act.wait_ge(kt2_ps, b * 8 + jj + 1)
                    f = jj % 2
                    a.copy(kTs[:, jj // 2, 512 * f:512 * f + 512], ps[:, jj % 4, :]).then_inc(kt2_sb, 1)

            def cache_exp(b):
                act.wait_ge(cs_max, b + 1)
                for j in range(NBLK + 1):
                    c0, c1 = (BLOCK * j, BLOCK * (j + 1)) if j < NBLK else (PAGE * NPAGES, PAGE * NPAGES + NS_TOK)
                    src = ps[:, 4 + j // 2, (j % 2) * BLOCK:(j % 2 + 1) * BLOCK] if j < NBLK else tmp[:, 0:NS_TOK]
                    last = a.activation(pex[:, c0:c1], src, ACT.Exp, scale=HD ** -0.5, bias=colB[:, j:j + 1], accum_out=colC[:, j:j + 1])
                last.then_inc(cs_exp, 1)
                act.wait_ge(cp_ps, b + 1)
                a.copy(pts[:, 0:4, :], ps[:, 0, :].rearrange("p (a b) -> p a b", b=P))
                a.copy(pto[0:NS_TOK, :], ps[0:NS_TOK, 2, 0:P]).then_inc(cp_a, 1)

            cache_keys(0)
            with act.Fori(0, NB - 1) as b:
                cache_keys(b + 1)
                cache_exp(b)
            cache_exp(NB - 1)
            act.wait_ge(ss2_ps, 1)
            a.activation(rstd, ps[:, 4, 0:T], ACT.Sqrt, scale=1.0 / D, bias=eps).then_inc(rms_sb, 1)
            shifted(3, KD)
            for j in range(6):
                t, f = divmod(j, 2)
                n = TILES[t][1]
                act.wait_ge(h2t_ps, j + 1)
                a.copy(h2_tok[0:n, t, 512 * f:512 * f + 512], ps[0:n, j % 4, :]).then_inc(h2t_sb, 1)
            act.wait_ge(g_max, 1)
            for t, (t0, n) in enumerate(TILES):
                last = a.activation(gates[0:n, t, :], top[0:n, t, 0:TOPK], ACT.Exp, bias=colD[0:n, t:t + 1], accum_out=gsum[0:n, t:t + 1])
            last.then_inc(g_exp, 1)

            def expert(par, n):
                act.wait_ge(xe_ps, n + 1)
                a.copy(xeT[par], ps[:, par, :].rearrange("p (k n) -> p k n", n=BT)).then_inc(xe_sb, 1)
                act.wait_ge(glu_sb, n + 1)
                a.activation(sig, glu, ACT.Sigmoid, scale=ALPHA).then_inc(sig_sb, 1)
                act.wait_ge(at_ps, n + 1)
                a.copy(actT, ps[:, 6, :].rearrange("p (c f n) -> p c f n", c=4, f=2)).then_inc(at_sb, 1)

            with act.Fori(0, NE // 2) as i:
                for par in range(2):
                    expert(par, i * 2 + par)
            act.wait_ge(route_done, 1)
            n_extra = act.value_load(eid[0:1, NX:NX + 1], min_val=0, max_val=NX)
            with act.If(n_extra > 0):
                with act.Fori(0, NX) as i:
                    with act.If(i < n_extra):
                        expert(0, i + NE)
                    act.nop()
            act.wait_ge(ss3_ps, 1)
            a.activation(rstd_tail, ps[:, 6, 0:T], ACT.Sqrt, scale=1.0 / D, bias=eps).then_inc(rms_sb, 1)
            for j in range(6):
                t, f = divmod(j, 2)
                n = TILES[t][1]
                act.wait_ge(ft_ps, j + 1)
                a.copy(ring[0:n, 3 + t, 512 * f:512 * f + 512], ps[0:n, j, :]).then_inc(ft_sb, 1)

        @block.vector
        def _(dve):
            v = nc.vector
            st = Steps(dve, dve_step)
            link = st.link
            v.memset(eps, EPS).then_inc(eps_sb, 1)
            link(v.memset(scT, 0.0))
            dve.wait_ge(vecT_ps, 1)
            v.tensor_copy(vT, ps[:, 0, 0:NVEC]).then_inc(vecT_sb, 1)
            dve.wait_ge(c_exp, 1)
            link(v.tensor_scalar_add(cexp[0:9, :], cexp[0:9, :], 1.0))
            link(v.reciprocal(cexp[0:9, :], cexp[0:9, :]))
            v.tensor_tensor(craw[0:9, :], craw[0:9, :], cexp[0:9, :], ALU.mult).then_inc(c_silu, 1)
            for k in range(KD):
                dve.wait_ge(xT_sb, k + 1)
                v.tensor_tensor(sq[:, k, :], xT[:, k, :], xT[:, k, :], ALU.mult).then_inc(sq_sb, 1)
            dve.wait_ge(cT_ps, 1)
            v.tensor_copy(scT[:, :, 0:9], ps[:, 1, 0:128].rearrange("p (k n) -> p k n", n=16)[:, :, 0:9]).then_inc(cT_sb, 1)

            def inverse_rms(sm, n):
                dve.wait_ge(sm, n)
                link(v.reciprocal(rstd, rstd))

            inverse_rms(rms_sb, 1)

            def modulation(g):
                dve.wait_ge(ada_ps, 4 * g + 4)
                v.tensor_copy(mod_sb, ps[:, 6, :]).then_inc(mod_rows, 1)
                dve.wait_ge(modT_ps, g + 1)
                dve.wait_ge(vecT_sb, 1)
                for j in range(4):
                    src = ps[:, 7, :].rearrange("p (c r) -> p c r", c=4)[:, :, 32 * j:32 * j + 9]
                    add = vT[:, V_BADA + 16 * g + 4 * j:V_BADA + 16 * g + 4 * j + 4, None].to_broadcast([P, 4, 9])
                    last = v.tensor_tensor(modT[:, 2 * g + j // 2, 4 * (j % 2):4 * (j % 2) + 4, :], src, add, ALU.add)
                last.then_inc(mod_done, 1)

            def modulated(shift, gain, scale):
                g = vT[:, gain:gain + KD, None].to_broadcast([P, KD, 9])
                hs = hT[:, :, NP_TOK:T].rearrange("p k (b l) -> p k b l", l=LS)
                link(v.scalar_tensor_tensor(s1, modT[:, scale], 1.0, g, ALU.add, ALU.mult))
                link(v.tensor_tensor(hT[:, :, NP_TOK:T], xT[:, :, NP_TOK:T], rstd[:, None, NP_TOK:T].to_broadcast([P, KD, NS_TOK]), ALU.mult))
                link(v.tensor_tensor(hs, hs, s1[:, :, 1:9, None].to_broadcast([P, KD, NB, LS]), ALU.mult))
                v.tensor_tensor(hs, hs, modT[:, shift, :, 1:9, None].to_broadcast([P, KD, NB, LS]), ALU.add).then_inc(hs_done, 1)
                for k in range(KD):
                    v.scalar_tensor_tensor(hT[:, k, 0:NP_TOK], xT[:, k, 0:NP_TOK], s1[:, k, 0:1], rstd[:, 0:NP_TOK], ALU.mult, ALU.mult).then_inc(hp_sb, 1)

            modulation(0)
            dve.wait_ge(mod_done, 1)
            modulated(0, V_G1, 1)

            def chunks(x, which):
                if which == 0:
                    return x[:, :, 0:NP_TOK].rearrange("p h (c l) -> p h c l", l=CH)
                return x[:, :, NP_TOK:T].rearrange("p h (c l) -> p h c l", l=LS)

            def against(out, at):
                for w, ln in ((0, CH), (1, LS)):
                    b = chunks(bT, w)
                    ref = b[:, :, :, at(ln):at(ln) + 1]
                    for h in range(GH):
                        yield chunks(out, w)[:, h], b[:, h], ref[:, h].to_broadcast([P, b.shape[2], ln])

            def level(w, q, k, e, q2, k2):
                for src, dst, mine, other in ((q, q2, 1, 0), (k, k2, 0, 1)):
                    if dst is None:
                        continue
                    for h in range(GH):
                        x, y = (z[:, h, 0:NP_TOK].rearrange("p (c a l) -> p a c l", a=2, l=w) for z in (src, dst))
                        d = e[:, h, 0:NP_TOK // w].rearrange("p (c a) -> p a c", a=2)[:, other, :, None].to_broadcast([P, NP_TOK // w // 2, w])
                        v.tensor_tensor(y[:, mine], x[:, mine], d, ALU.mult)
                        last = v.tensor_copy(y[:, other], x[:, other])
                return last

            def decay(step):
                if step == 0:
                    dve.wait_ge(fm_sb, 13)
                    v.scalar_tensor_tensor(eqT, elT, -1.0, elT, ALU.mult, ALU.min).then_inc(gla_d, 1)
                if step == 1:
                    dve.wait_ge(gla_a, 1)
                    link(v.scalar_tensor_tensor(elT, elT, 0.0, eqT, ALU.min, ALU.subtract))
                    for h in range(GH):
                        last = v.tensor_tensor_scan(bT[:, h, :], const("scan"), elT[:, h, :], 0.0, ALU.mult, ALU.add)
                    last.then_inc(gla_d, 1)
                if step == 2:
                    dve.wait_ge(gla_d, 2)
                    for dst, x, y in against(eqT, lambda ln: ln // 2 - 1):
                        last = v.tensor_tensor(dst, x, y, ALU.subtract)
                    link(last)
                    v.tensor_scalar(eqT, eqT, CLAMP, -CLAMP, ALU.min, ALU.max).then_inc(gla_d, 1)
                if step == 3:
                    for dst, x, y in against(elT, lambda ln: ln - 1):
                        last = v.tensor_tensor(dst, y, x, ALU.subtract)
                    last.then_inc(gla_d, 1)
                if step == 4:
                    dve.wait_ge(gla_a, 2)
                    v.tensor_copy(edec[:, :, 0:16], chunks(e0T, 0)[:, :, :, CH - 1])
                    link(v.tensor_copy(edec[:, :, 16:24], chunks(e0T, 1)[:, :, :, LS - 1]))
                    v.scalar_tensor_tensor(eqT, gqT, DK ** -0.5, eqT, ALU.mult, ALU.mult)
                    v.tensor_tensor(ekT, gkT, ekT, ALU.mult)
                if step == 5:
                    v.scalar_tensor_tensor(e0T, gqT, DK ** -0.5, e0T, ALU.mult, ALU.mult)
                    dve.wait_ge(gla_a, 3)
                    link(v.tensor_tensor(elT, gkT, elT, ALU.mult))
                if step == 6:
                    link(level(16, e0T, elT, edec, q32, k32))
                    link(v.tensor_tensor(e32, edec[:, :, 0:16:2], edec[:, :, 1:16:2], ALU.mult))
                if step == 7:
                    link(level(32, q32, k32, e32, q64, k64))
                    link(v.tensor_tensor(e64, e32[:, :, 0:8:2], e32[:, :, 1:8:2], ALU.mult))
                if step == 8:
                    link(level(64, q64, k64, e64, None, k128))
                    v.tensor_tensor(e128, e64[:, :, 0:4:2], e64[:, :, 1:4:2], ALU.mult).then_inc(gla_d, 1)

            for n in range(15):
                c, t = divmod(n, 3)
                rows = TILES[t][1]
                dve.wait_ge(tm_ps, n + 1)
                bank = ps[0:rows, 3 + t, :]
                if c < 2:
                    v.tensor_copy(v_tok[0:rows, t, 512 * c:512 * c + 512], bank).then_inc(tm_sb, 1)
                elif c < 4:
                    x = bank.rearrange("p (h a d) -> p h a d", a=2, d=HD // 2)
                    r = rot[0:rows, c - 2, t, :].rearrange("p (h a d) -> p h a d", a=2, d=HD // 2)
                    cos = const("cos")[0:rows, None, 32 * t:32 * t + 32].to_broadcast([rows, MH, 32])
                    sin = const("sin")[0:rows, None, 32 * t:32 * t + 32].to_broadcast([rows, MH, 32])
                    s = tmp[0:rows, 0:256].rearrange("p (h d) -> p h d", d=32)
                    v.tensor_tensor(r[:, :, 0, :], x[:, :, 0, :], cos, ALU.mult)
                    v.tensor_tensor(r[:, :, 1, :], x[:, :, 1, :], cos, ALU.mult)
                    link(v.tensor_tensor(s, x[:, :, 1, :], sin, ALU.mult))
                    link(v.tensor_tensor(r[:, :, 0, :], r[:, :, 0, :], s, ALU.subtract))
                    link(v.tensor_tensor(s, x[:, :, 0, :], sin, ALU.mult))
                    v.tensor_tensor(r[:, :, 1, :], r[:, :, 1, :], s, ALU.add).then_inc(tm_sb, 1)
                    dve.wait_ge(tm_sb, n + 1)
                else:
                    v.tensor_copy(mv_tok[0:rows, t, :], bank).then_inc(tm_sb, 1)
                if n >= 6:
                    decay(n - 6)
                if n == 11:
                    modulation(1)
            for m in range(8):
                dve.wait_ge(fm_sb, 14 + m)
                v.tensor_tensor(grT[:, m, :], ps[:, (13 + m) % 3, 0:T], grT[:, m, :], ALU.mult).then_inc(gr_sb, 1)
            modulation(2)

            dve.wait_ge(fm_sb, 29)
            dve.wait_ge(k_out, 32)
            level(64, q64, None, e64, q128, None).then_inc(q128_sb, 1)

            def masked(u):
                dve.wait_ge(att_ps, u + 1)
                four = ps[:, 4, :]
                link(v.tensor_tensor(four, four, const("gla_p"), ALU.mult))
                if u >= 2:
                    dve.wait_ge(o_part, u - 1)
                v.tensor_reduce(att[:, u % 2, :], four.rearrange("p (j n) -> p n j", j=4), AX, ALU.add).then_inc(att_sb, 1)

            def new_state(u):
                t, h = divmod(u, GH)
                dve.wait_ge(d_ps, u + 1)
                if t == 0:
                    v.tensor_copy(state[:, h, :], ps[:, u % 2, 0:DV]).then_inc(s_new, 1)
                else:
                    dve.wait_ge(o_part, u + 1)
                    v.scalar_tensor_tensor(state[:, h, :], state[:, h, :], e128[:, h, t:t + 1], ps[:, u % 2, 0:DV], ALU.mult, ALU.add).then_inc(s_new, 1)

            def normed(u):
                t, h = divmod(u, GH)
                n = TILES[t][1]
                dve.wait_ge(o_sq, u + 1)
                link(v.reciprocal(colB[0:n, 0:1], colC[0:n, 0:1]))
                if t and h == 0:
                    dve.wait_ge(ot_ps, t)
                v.tensor_scalar(o_tok[0:n, h * DV:(h + 1) * DV], ps[0:n, 5 + u % 2, 0:DV], colB[0:n, 0:1], None, ALU.mult).then_inc(o_norm, 1)

            def gated(t):
                t0, n = TILES[t]
                dve.wait_ge(ot_ps, t + 1)
                for f in range(2):
                    for j in range(2):
                        src = ps[:, 2 if f else 7, 0:4 * n].rearrange("p (h j n) -> p j h n", j=2, n=n)[:, j]
                        gr = grT[:, 4 * f:4 * f + 4, t0:t0 + n].rearrange("p (h j) n -> p j h n", j=2)[:, j]
                        to = oTg[:, 4 * f:4 * f + 4, t0:t0 + n].rearrange("p (h j) n -> p j h n", j=2)[:, j]
                        last = v.scalar_tensor_tensor(to, src, vT[:, V_GH + j:V_GH + j + 1], gr, ALU.mult, ALU.mult)
                last.then_inc(ot_sb, 1)

            masked(0)
            dve.wait_ge(kt_ps, 1)
            link(v.memset(qm, 0.0))
            for u in range(2 * GH):
                if u + 1 < 2 * GH:
                    masked(u + 1)
                new_state(u)
                normed(u)
                if u == GH:
                    gated(0)

            def sample_masks(h):
                if h >= 2:
                    dve.wait_ge(o_part, 2 * GH + 8 * (h - 1))
                else:
                    dve.wait_ge(att_ps, 2 * GH)
                at = 5120 + 8 * NS_TOK * (h % 2)
                diag = late[:, at:at + 8 * NS_TOK].rearrange("p (c x) -> p c x", x=NS_TOK)
                for c in range(8):
                    last = v.tensor_copy(diag[:, c, LS * c:LS * c + LS], e0T[:, h, NP_TOK + LS * c:NP_TOK + LS * c + LS])
                last.then_inc(qm_sb, 1)
                v.tensor_tensor(km[0:NS_TOK, h % 2], ps[0:NS_TOK, 3, None, h * DK:(h + 1) * DK].to_broadcast([NS_TOK, 8, DK]),
                                const("rows_s")[0:NS_TOK, :, None].to_broadcast([NS_TOK, 8, DK]), ALU.mult).then_inc(km_sb, 1)

            n = NS_TOK
            for h in range(GH):
                u = 2 * GH + h
                x0 = 2 * GH + 8 * h
                if h < 2:
                    sample_masks(h)
                dve.wait_ge(att_ps, u + 1)
                v.tensor_tensor(att[0:n, u % 2, 0:n], ps[0:n, 4, 0:n], const("gla_s")[0:n, 0:n], ALU.mult).then_inc(att_sb, 1)
                if h == 0:
                    gated(1)
                for c in range(8):
                    dve.wait_ge(d_ps, x0 + c + 1)
                    dve.wait_ge(o_part, x0 + c + 1)
                    s0 = ring[:, (N_S0 + c // 4) % PRE, ((c % 4) * GH + h) * DV:((c % 4) * GH + h + 1) * DV]
                    v.scalar_tensor_tensor(s0, s0, edec[:, h, 16 + c:17 + c], ps[:, c % 2, 0:DV], ALU.mult, ALU.add).then_inc(s_new, 1)
                if h + 2 < GH:
                    sample_masks(h + 2)
                normed(u)
            gated(2)

            dve.wait_ge(gs_out, 16)
            def prompt_out(h):
                dve.wait_ge(mo_ps, h + 1)
                link(v.reciprocal(colD[:, 2 * (h % 2):2 * (h % 2) + 2], colC[:, 2 * (h % 2):2 * (h % 2) + 2]))
                for t in range(2):
                    last = v.tensor_scalar(om_tok[:, t, h * HD:(h + 1) * HD], ps[:, 5 + h % 2, t * HD:(t + 1) * HD],
                                           colD[:, 2 * (h % 2) + t:2 * (h % 2) + t + 1], None, ALU.mult)
                last.then_inc(mo_sb, 1)

            for h in range(MH):
                dve.wait_ge(ms_ps, h + 1)
                if h >= 2:
                    dve.wait_ge(ms_exp, h - 1)
                x = pin[:, h % 2, :]
                link(v.tensor_tensor(x, ps[:, h % 2, 0:384], const("causal"), ALU.add))
                v.tensor_reduce(colA[:, 0:1], x[:, 0:P], AX, ALU.max)
                link(v.tensor_reduce(colA[:, 1:2], x[:, P:3 * P], AX, ALU.max))
                v.tensor_scalar(colB[:, 2 * (h % 2):2 * (h % 2) + 2], colA[:, 0:2], -HD ** -0.5, None, ALU.mult).then_inc(ms_max, 1)
                if h:
                    prompt_out(h - 1)
            prompt_out(MH - 1)

            dve.wait_ge(mot_sb, 2)
            link(v.memset(qs, 0.0))
            def queries(b):
                for hh in range(2):
                    rows = slice(64 * hh, 64 * hh + 64)
                    last = v.tensor_copy(qs[rows, :, 8 * hh:8 * hh + 8], mqT[rows, :, bass.ds(b * LS + NP_TOK, LS)])
                last.then_inc(q_sb, 1)

            def cache_max(b):
                dve.wait_ge(cs_ps, b + 1)
                sc = ps[:, 4:6, :].rearrange("p a (b c) -> p a b c", c=BLOCK)
                gsum4 = colA[:, 0:4]
                v.tensor_reduce(gsum4.rearrange("p (a b) -> p a b", b=2), sc, AX, ALU.add)
                v.tensor_reduce(colD[:, 0:4].rearrange("p (a b) -> p a b", b=2), sc, AX, ALU.max)
                link(v.tensor_tensor(tmp[:, 0:NS_TOK], ps[:, 6, 0:NS_TOK], const("own")[:, bass.ds(b * NS_TOK, NS_TOK)], ALU.add))
                v.tensor_reduce(colD[:, 4:5], tmp[:, 0:NS_TOK], AX, ALU.max)
                mine = gsum4[:, :, None].to_broadcast([P, 4, 4])
                other = gsum4[:, None, :].to_broadcast([P, 4, 4])
                w = tmp[:, 64:80].rearrange("p (a b) -> p a b", b=4)
                w2 = tmp[:, 80:96].rearrange("p (a b) -> p a b", b=4)
                tri = const("tri").rearrange("p (a b) -> p a b", b=4)
                v.tensor_tensor(w, other, mine, ALU.is_gt)
                link(v.tensor_tensor(w2, other, mine, ALU.is_equal))
                link(v.tensor_tensor(w2, w2, tri, ALU.mult))
                link(v.tensor_tensor(w, w, w2, ALU.add))
                link(v.tensor_reduce(colA[:, 4:8], w, AX, ALU.add))
                link(v.tensor_scalar(colA[:, 8:12], colA[:, 4:8], 3.0, NEG, ALU.is_ge, ALU.mult))
                link(v.tensor_tensor(colD[:, 0:4], colD[:, 0:4], colA[:, 8:12], ALU.add))
                link(v.tensor_reduce(colD[:, 5:6], colD[:, 0:5], AX, ALU.max))
                link(v.tensor_scalar(colB[:, 4:5], colD[:, 5:6], -HD ** -0.5, None, ALU.mult))
                v.tensor_scalar(colB[:, 0:4], colA[:, 8:12], colB[:, 4:5], None, ALU.add).then_inc(cs_max, 1)

            def cache_probs(b):
                dve.wait_ge(cs_exp, b + 1)
                link(v.tensor_reduce(colD[:, 8:9], colC[:, 0:5], AX, ALU.add))
                link(v.reciprocal(colD[:, 9:10], colD[:, 8:9]))
                dve.wait_ge(cp_ps, b + 1)
                v.tensor_copy(pts[:, 4:8, :], ps[:, 1, :].rearrange("p (a b) -> p a b", b=P)).then_inc(cp_d, 1)

            def cache_scale(b):
                dve.wait_ge(co_ps, b + 1)
                v.tensor_scalar(osm, ps[:, 7, 0:P], colD[:, 9:10], None, ALU.mult).then_inc(co_sb, 1)

            def cache_out(b):
                dve.wait_ge(cot_ps, b + 1)
                for hh in range(2):
                    rows = slice(64 * hh, 64 * hh + 64)
                    src = ps[rows, 7, 0:P].rearrange("p (a r) -> p a r", r=32)[:, :, 8 * hh:8 * hh + 8]
                    last = v.tensor_copy(oTm[rows, :, bass.ds(b * LS + NP_TOK, LS)], src)
                last.then_inc(cot_sb, 1)

            queries(0)
            cache_max(0)
            queries(1)
            cache_probs(0)
            with dve.Fori(0, NB - 2) as i:
                st.enter(i, 11)
                cache_max(i + 1)
                queries(i + 2)
                cache_scale(i)
                cache_probs(i + 1)
                cache_out(i)
            st.leave(NB - 2)
            cache_max(NB - 1)
            cache_scale(NB - 2)
            cache_probs(NB - 1)
            cache_out(NB - 2)
            cache_scale(NB - 1)
            cache_out(NB - 1)

            for n in range(24):
                which, m = divmod(n, KD)
                dve.wait_ge(pj_ps, n + 1)
                bank = ps[:, n % 4, 0:T]
                if which == 0:
                    v.tensor_tensor(baT[:, m, :], bank, baT[:, m, :], ALU.mult).then_inc(pj_sb, 1)
                elif which == 1:
                    link(v.tensor_tensor(bbT[:, m, :], bank, bbT[:, m, :], ALU.mult))
                    v.tensor_tensor(hT[:, m, :], baT[:, m, :], bbT[:, m, :], ALU.add).then_inc(pj_sb, 1)
                else:
                    v.scalar_tensor_tensor(xT[:, m, 0:NP_TOK], bank[:, 0:NP_TOK], modT[:, 2, m, 0:1], xT[:, m, 0:NP_TOK], ALU.mult, ALU.add)
                    w = tmp[:, 0:NS_TOK].rearrange("p (b l) -> p b l", l=LS)
                    link(v.tensor_tensor(w, bank[:, NP_TOK:T].rearrange("p (b l) -> p b l", l=LS),
                                         modT[:, 2, m, 1:9, None].to_broadcast([P, NB, LS]), ALU.mult))
                    v.tensor_tensor(xT[:, m, NP_TOK:T], xT[:, m, NP_TOK:T], tmp[:, 0:NS_TOK], ALU.add).then_inc(pj_sb, 1)
                    dve.wait_ge(pj_sb, n + 1)
                    v.tensor_tensor(sq[:, m, :], xT[:, m, :], xT[:, m, :], ALU.mult).then_inc(sq2_sb, 1)
            inverse_rms(rms_sb, 2)
            modulated(3, V_G2, 4)
            dve.wait_ge(pj_sb, 24)
            for par in range(2):
                v.memset(bias[par], 0.0).then_inc(zero_sb, 1)
            for par in range(2):
                last = v.memset(x_in[par], 0.0)
            last.then_inc(zero_sb, 1)

            dve.wait_ge(rt_ps, 1)
            link(v.memset(lg, 0.0))
            for t, (t0, n) in enumerate(TILES):
                last = v.tensor_tensor(lg[0:n, t, :], ps[0:n, 5, NE * t:NE * t + NE], b_rt[0:n, :], ALU.add)
            link(last)
            for t in range(3):
                last = v.max(top[:, t, :], lg[:, t, :])
            link(last)
            for t in range(3):
                last = v.max_index(topi[:, t, :], top[:, t, :], lg[:, t, :])
            link(last)
            v.tensor_scalar(colD[:, 0:3], top[:, :, 0], -1.0, None, ALU.mult).then_inc(g_max, 1)
            link(v.tensor_copy(topf, topi[:]))
            for t in range(3):
                for k in range(TOPK):
                    last = v.tensor_scalar(oh[:, t, k, :], const("iota"), topf[:, t, k:k + 1], None, ALU.is_equal)
            link(last)
            for t in range(3):
                last = v.tensor_reduce(pick[:, t, :], oh[:, t].rearrange("p k e -> p e k"), AX, ALU.add)
            last.then_inc(picked, 1)
            dve.wait_ge(rank_ps, 1)
            v.memset(pos, 0.0)
            link(v.tensor_copy(cnt, ps[:, 4, 96:128]))
            for t, (t0, n) in enumerate(TILES):
                last = v.tensor_copy(pos[0:n, t, :], ps[0:n, 4, NE * t:NE * t + NE])
            link(last)
            link(v.tensor_scalar(xtra, cnt, float(BT), None, ALU.is_gt))
            for j in range(2, 5):
                link(v.scalar_tensor_tensor(xtra, cnt, float(BT * j), xtra, ALU.is_gt, ALU.add))
            link(v.tensor_tensor_scan(xend, ones[:, 0:NE], xtra, 0.0, ALU.mult, ALU.add))
            link(v.tensor_scalar(nblk, pos, float(BT), None, ALU.is_ge))
            for j in range(2, 5):
                link(v.scalar_tensor_tensor(nblk, pos, float(BT * j), nblk, ALU.is_ge, ALU.add))
            link(v.tensor_tensor(xtra, xend, xtra, ALU.subtract))
            link(v.tensor_scalar_add(xtra, xtra, float(NE - 1)))
            link(v.tensor_tensor(cnt, const("iota"), xtra, ALU.subtract))
            link(v.tensor_scalar(base, nblk, 0.0, None, ALU.is_equal))
            link(v.tensor_tensor(base, base, cnt[:, None, :].to_broadcast([P, 3, NE]), ALU.mult))
            link(v.tensor_tensor(base, base, xtra[:, None, :].to_broadcast([P, 3, NE]), ALU.add))
            link(v.scalar_tensor_tensor(base, nblk, float(1 - BT * NCOL), base, ALU.mult, ALU.add))
            link(v.scalar_tensor_tensor(base, pos, float(NCOL), base, ALU.mult, ALU.add))
            for t in range(3):
                link(v.tensor_tensor(rtmp, oh[:, t], base[:, t, None, :].to_broadcast([P, TOPK, NE]), ALU.mult))
                link(v.tensor_reduce(slotf[:, t, :], rtmp, AX, ALU.add))
            v.tensor_copy(sloti[:], slotf.rearrange("p a b -> p (a b)")).then_inc(slots_sb, 1)
            link(v.tensor_tensor(xcmp[0:1], xend[0:1, None, :].to_broadcast([1, NX, NE]),
                                 const("iota")[0:1, 0:NX, None].to_broadcast([1, NX, NE]), ALU.is_le))
            link(v.tensor_reduce(cnt[0:1, 0:NX], xcmp[0:1], AX, ALU.add))
            link(v.tensor_scalar(cnt[0:1, 0:NX], cnt[0:1, 0:NX], float(NE - 1), None, ALU.min))
            link(v.tensor_copy(cnt[0:1, NX:NX + 1], xend[0:1, NE - 1:NE]))
            v.tensor_copy(eid[0:1, :], cnt[0:1, 0:NX + 1]).then_inc(route_done, 1)
            dve.wait_ge(g_exp, 1)
            for t, (t0, n) in enumerate(TILES):
                last = v.reciprocal(gsum[0:n, t:t + 1], gsum[0:n, t:t + 1])
            link(last)
            for t, (t0, n) in enumerate(TILES):
                last = v.tensor_scalar(gates[0:n, t, :], gates[0:n, t, :], gsum[0:n, t:t + 1], None, ALU.mult)
            link(last)
            dve.wait_ge(slots_in, 32)
            v.tensor_scalar(tok_ix[0:BT, :], slots[0:BT, :], 2, None, ALU.logical_shift_right)
            v.tensor_scalar(row_ix[:], slots[:], 2.0, const("half"), ALU.mult, ALU.add).then_inc(ix_done, 1)

            def expert(par, n):
                dve.wait_ge(slot_used, n * RING + PRE)
                v.tensor_scalar(glu, ps[:, 2 + par, :], LIMIT, None, ALU.min).then_inc(glu_sb, 1)
                v.tensor_scalar(lin, ps[:, 4 + par, :], LIMIT, -LIMIT, ALU.min, ALU.max).then_inc(dve_moe, 1)
                dve.wait_ge(dve_moe, n * 2 + 1)
                dve.wait_ge(glu_sb, n + 1)
                v.scalar_tensor_tensor(lin, lin, 1.0, glu, ALU.add, ALU.mult).then_inc(dve_moe, 1)
                dve.wait_ge(dve_moe, n * 2 + 2)
                dve.wait_ge(sig_sb, n + 1)
                v.tensor_tensor(act_m, lin, sig, ALU.mult).then_inc(act_sb, 1)
                dve.wait_ge(slot_used, n * RING + RING)
                dve.wait_ge(y_free, n + 1)
                v.tensor_copy(y_out[par], ps[:, 7, :]).then_inc(y_sb, 1)

            with dve.Fori(0, NE // 2) as i:
                for par in range(2):
                    expert(par, i * 2 + par)
            dve.wait_ge(route_done, 1)
            n_extra = dve.value_load(eid[0:1, NX:NX + 1], min_val=0, max_val=NX)
            with dve.If(n_extra > 0):
                with dve.Fori(0, NX) as i:
                    with dve.If(i < n_extra):
                        expert(0, i + NE)
                    dve.nop()

            st = Steps(dve, dve_tail)
            link = st.link
            for t, (t0, n) in enumerate(TILES):
                dve.wait_ge(moe_done, 1)
                dve.wait_ge(y_in[t], 16)
                y = ring[0:n, t, :].rearrange("p (k d) -> p k d", k=TOPK)
                acc = ysum[0:n, t % 2, :]
                if t == 2:
                    dve.wait_ge(yt_ps, 1)
                link(v.tensor_scalar(acc, y[:, 0, :], gates[0:n, t, 0:1], None, ALU.mult))
                for k in range(1, TOPK - 1):
                    link(v.scalar_tensor_tensor(acc, y[:, k, :], gates[0:n, t, k:k + 1], acc, ALU.mult, ALU.add))
                v.scalar_tensor_tensor(acc, y[:, TOPK - 1, :], gates[0:n, t, TOPK - 1:TOPK], acc, ALU.mult, ALU.add).then_inc(ys_sb, 1)
            for t, (t0, n) in enumerate(TILES):
                dve.wait_ge(yt_ps, t + 1)
                for m in range(KD):
                    src = ps[:, 2 * t + m // 4, (m % 4) * n:(m % 4 + 1) * n]
                    if t < 2:
                        last = v.scalar_tensor_tensor(xT[:, m, t0:t0 + n], src, modT[:, 5, m, 0:1], xT[:, m, t0:t0 + n], ALU.mult, ALU.add)
                    else:
                        w = ff_tail[:, m, :].rearrange("p (b l) -> p b l", l=LS)
                        last = v.tensor_tensor(w, src.rearrange("p (b l) -> p b l", l=LS), modT[:, 5, m, 1:9, None].to_broadcast([P, NB, LS]), ALU.mult)
            link(last)
            link(v.tensor_tensor(xT[:, :, NP_TOK:T], xT[:, :, NP_TOK:T], ff_tail, ALU.add))
            v.tensor_tensor(sq_tail, xT, xT, ALU.mult).then_inc(sq3_sb, 1)
            dve.wait_ge(rms_sb, 3)
            link(v.reciprocal(rstd_tail, rstd_tail))
            for k in range(KD):
                last = v.scalar_tensor_tensor(xT[:, k, :], xT[:, k, :], vT[:, V_GF + k:V_GF + k + 1], rstd_tail, ALU.mult, ALU.mult)
            last.then_inc(fin_sb, 1)

        @block.gpsimd
        def _(pool):
            g = nc.gpsimd
            g.iota(fill[:], pattern=[[0, NCOL]], base=FREE, channel_multiplier=0).then_inc(fill_ix, 1)
            g.iota(asg[:].rearrange("p (t k) -> p t k", k=TOPK), pattern=[[P * TOPK, 3], [1, TOPK]], base=0, channel_multiplier=TOPK).then_inc(fill_ix, 1)
            pool.wait_ge(fill_ix, 2)
            pool.dma_start(slot_rows.rearrange("(p a) o -> p (a o)", a=NCOL), fill[0:BT, :]).then_inc(fill_out, 16)
            pool.wait_ge(fill_out, 16)
            pool.wait_ge(pt_in, 16)
            def value_pages(b, par):
                n = N_CACHE + 2 * par + 1
                for j in range(NPAGES):
                    page = pool.value_load(ptab[0:1, bass.ds(b * NPAGES + j, 1)], min_val=0, max_val=cache_k.shape[1] - 1)
                    pool.dma_start(item(n)[:, j, :], v_pages[bass.ds(page, 1)].rearrange("o s n -> s (o n)")).then_inc(v_land[par], 16)

            for b in range(2):
                pool.wait_ge(*used[N_CACHE + 2 * b + 1 - PRE])
                value_pages(b, b)
            with pool.Fori(1, NB // 2) as i:
                for par in range(2):
                    b = i * 2 + par
                    pool.wait_ge(co_ps, b - 1)
                    pool.sem_inc(turns, 1)
                    value_pages(b, par)
            pool.wait_ge(slots_sb, 1)
            for t, (t0, n) in enumerate(TILES):
                for k in range(TOPK):
                    j = TOPK * t + k
                    pool.indirect_dma_start(out=slot_rows, out_offset=bass.IndirectOffsetOnAxis(ap=sloti[0:n, j:j + 1], axis=0),
                                            in_=asg[0:n, j:j + 1], in_offset=None).then_inc(scat, 16)
            pool.wait_ge(scat, 16 * 3 * TOPK)
            for half in range(2):
                pool.dma_start(slots[BT * half:BT * half + BT, :], slot_rows.rearrange("(p a) o -> p (a o)", a=NCOL)).then_inc(slots_in, 16)
            pool.wait_ge(ix_done, 1)
            pool.wait_ge(h2_out, 48)
            pool.wait_ge(zero_sb, 3)

            def gather(par, col, turn):
                g.tensor_copy(tok_col[0:BT, par:par + 1], tok_ix[0:BT, bass.ds(col, 1)]).then_inc(ix_sb, 1)
                pool.wait_ge(ix_sb, turn)
                pool.sem_inc(turns, 1)
                pool.indirect_dma_start(out=x_in[par][0:BT, :], out_offset=None, in_=h2_rows,
                                        in_offset=bass.IndirectOffsetOnAxis(ap=tok_col[0:BT, par:par + 1], axis=0),
                                        bounds_check=T - 1, oob_is_err=False).then_inc(x_land[par], 16)

            def scatter(par, col, turn):
                g.tensor_copy(row_col[:, par:par + 1], row_ix[:, bass.ds(col, 1)]).then_inc(ix_sb, 1)
                pool.wait_ge(ix_sb, turn)
                pool.sem_inc(turns, 1)
                pool.indirect_dma_start(out=y_rows, out_offset=bass.IndirectOffsetOnAxis(ap=row_col[:, par:par + 1], axis=0),
                                        in_=y_out[par], in_offset=None, bounds_check=T * TOPK * 2 - 1, oob_is_err=False).then_inc(y_sent[par], 16)

            pool.sem_inc(y_free, 2)
            gather(0, 0, 1)
            gather(1, 1, 2)
            with pool.Fori(0, NE // 2) as i:
                for par in range(2):
                    n = i * 2 + par
                    pool.wait_ge(y_sb, n + 1)
                    scatter(par, n, n * 2 + 3)
                    pool.wait_ge(xe_ps, n + 1)
                    gather(par, n + 2, n * 2 + 4)
                    pool.wait_ge(y_sent[par], (i + 1) * 16)
                    pool.sem_inc(y_free, 1)
            pool.wait_ge(x_land[0], 16 * (NE // 2 + 1))
            pool.wait_ge(x_land[1], 16 * (NE // 2 + 1))
            pool.wait_ge(route_done, 1)
            n_extra = pool.value_load(eid[0:1, NX:NX + 1], min_val=0, max_val=NX)
            with pool.If(n_extra > 0):
                with pool.Fori(0, NX) as i:
                    with pool.If(i < n_extra):
                        pool.wait_ge(y_sb, i + NE + 1)
                        scatter(0, i + NE, i * 2 + 2 * NE + 3)
                        gather(0, i + NE + 1, i * 2 + 2 * NE + 4)
                        pool.wait_ge(y_sent[0], (i + (NE // 2 + 1)) * 16)
                        pool.sem_inc(y_free, 1)
                        pool.wait_ge(x_land[0], (i + (NE // 2 + 2)) * 16)
                    pool.nop()
            pool.nop().then_inc(moe_done, 1)


_INS = ['x_prompt', 'x_sample', 'cache_k', 'cache_v', 'state_gla', 'page_table', 'c_prompt', 'c_sample',
        'w_ada', 'b_ada', 'g_norm1', 'w_in', 'w_gla_a2', 'b_gla_a2', 'g_gla_head', 'w_proj_gla', 'w_proj_moba',
        'w_out', 'g_norm2', 'w_router', 'b_router', 'w_gate_up', 'b_gate_up', 'w_down', 'b_down', 'g_final']
_OUTS = [(1, 256, 1024), (8, 8, 1024), (1, 1, 256, 8, 64), (1, 1, 256, 8, 64), (1, 1, 4, 128, 256),
         (1, 8, 8, 8, 64), (1, 8, 8, 8, 64), (1, 8, 4, 128, 256)]


def kernel(**inputs):
    import numpy as np
    import concourse.bacc as bacc
    from concourse.bass_utils import run_bass_kernel_spmd

    nc = bacc.Bacc("TRN2", target_bir_lowering=False, num_devices=1)
    arrays = {f"in_{name}": np.ascontiguousarray(inputs[name]) for name in _INS}
    arrays["in_consts"] = constants()
    args = [nc.dram_tensor(n, a.shape, mybir.dt.from_np(a.dtype), kind="ExternalInput").ap() for n, a in arrays.items()]
    args += [nc.dram_tensor(f"out_{i}", shape, F32, kind="ExternalOutput").ap() for i, shape in enumerate(_OUTS)]
    decoder_layer(nc, *args)
    r = run_bass_kernel_spmd(nc, [arrays], core_ids=[0])
    return tuple(r.results[0][f"out_{i}"] for i in range(len(_OUTS)))
```

```python
from contextlib import ExitStack

import concourse.bass as bass
from concourse import mybir

F32 = mybir.dt.float32
I32 = mybir.dt.int32
U32 = mybir.dt.uint32
ACT = mybir.ActivationFunctionType
ALU = mybir.AluOpType
AX = mybir.AxisListType.X

P = 128
D = 1024
KD = D // P
NP_TOK, NB, LS = 256, 8, 8
NS_TOK = NB * LS
T = NP_TOK + NS_TOK
TILES = ((0, 128), (128, 128), (256, 64))
GH, DK, DV = 4, 128, 256
CH = 16
MH, HD = 8, 64
PAIRS = MH // 2
PAGE, NPAGES = 128, 8
BLOCK = 256
NBLK = PAGE * NPAGES // BLOCK
NEG = -1e30
GATE_NORM = 16.0
LEVELS = (16, 32, 64)
CLAMP = 38.0 * GATE_NORM
EPS = 1e-6
NE, TOPK = 32, 4
BT = 64
NX = 19
NCOL = 52
FREE = 4096
TAIL = (2, 0, 1)
LIMIT, ALPHA = 7.0, 1.702
C_GQ, C_GK, C_GV, C_GR, C_GA = 0, 512, 1024, 2048, 3072
C_MQ, C_MK, C_MV, C_BA, C_BB = 3088, 3600, 4112, 4624, 5648
SLOT = 4096
RING = 6
PRE = 4

NMEM = 28248

V_BADA, V_G1, V_G2, V_BA2, V_GH = 0, 48, 56, 64, 68
NVEC = 70

CST = {}
_at = 0
for _name, _n in (("ident", 128), ("ones", 128), ("gla_p", 512), ("gla_s", 64), ("rows_s", 8),
                  ("causal", 384), ("own", 512), ("cos", 96), ("sin", 96), ("before", 128), ("iota", 64), ("stack", 32),
                  ("tri", 16), ("scan", 320), ("row0", 64), ("half", 1)):
    CST[_name] = (_at, _n)
    _at += _n
NCST = _at


def constants():
    import numpy as np

    c = {n: np.zeros((P, w), np.float32) for n, (_, w) in CST.items()}
    r = np.arange(P)[:, None]
    q = np.arange(P)[None, :]
    c["ident"][:] = r == q
    c["ones"][:] = 1
    c["gla_p"][:, 0:P] = (r <= q) & (r // CH == q // CH)
    for j, w in enumerate(LEVELS):
        c["gla_p"][:, P * (j + 1):P * (j + 2)] = (r // (2 * w) == q // (2 * w)) & (r // w % 2 == 0) & (q // w % 2 == 1)
    c["gla_s"][:64] = ((r <= q) & (r // LS == q // LS))[:64, :64]
    c["rows_s"][:64] = (r // LS == np.arange(8))[:64]
    c["causal"][:, 0:128] = np.where(q <= r, 0, NEG)
    c["causal"][:, 256:384] = np.where(q <= r, 0, NEG)
    col = np.arange(64)[None, :]
    for b in range(NB):
        c["own"][:, 64 * b:64 * b + 64] = np.where((col // LS == b) & (col % LS <= r % LS), 0, NEG)
    half = HD // 2
    inv = (np.float32(1.0) / (np.float32(10000.0) ** (np.arange(half, dtype=np.float32) / np.float32(half)))).astype(np.float32)
    for t, (t0, n) in enumerate(TILES):
        pos = np.arange(t0, t0 + P) if t < 2 else PAGE * NPAGES + np.arange(P) % LS
        ang = (pos.astype(np.float32)[:, None] * inv[None, :]).astype(np.float32)
        c["cos"][:, half * t:half * t + half] = np.cos(ang)
        c["sin"][:, half * t:half * t + half] = np.sin(ang)
    c["before"][:] = r < q
    c["iota"][:] = np.arange(64)
    c["stack"][:] = r % 32 == np.arange(32)
    c["tri"][:] = (np.arange(4)[None, :] < np.arange(4)[:, None]).astype(np.float32).reshape(1, 16)
    s = np.ones(T, np.float32)
    s[0:NP_TOK:CH] = 0
    s[NP_TOK::LS] = 0
    c["scan"][:] = s
    c["row0"][0] = 1
    c["half"][64:] = 1
    return np.ascontiguousarray(np.concatenate([c[n] for n in CST], axis=1))


class Steps:

    def __init__(self, engine, sem):
        self.engine, self.sem, self.fixed, self.local, self.loop, self.per = engine, sem, 0, 0, None, 0

    def link(self, ins):
        ins.then_inc(self.sem, 1)
        self.local += 1
        done = self.fixed + self.local
        self.engine.wait_ge(self.sem, done if self.loop is None else self.loop * self.per + done)

    def enter(self, loop, per):
        self.fixed, self.local, self.loop, self.per = self.fixed + self.local, 0, loop, per

    def leave(self, times):
        assert self.local == self.per, (self.local, self.per)
        self.fixed, self.local, self.loop = self.fixed + times * self.per, 0, None


def decoder_layer(nc, x_prompt, x_sample, cache_k, cache_v, state_gla, page_table, c_prompt, c_sample,
                  w_ada, b_ada, g_norm1, w_in, w_gla_a2, b_gla_a2, g_gla_head, w_proj_gla, w_proj_moba,
                  w_out, g_norm2, w_router, b_router, w_gate_up, b_gate_up, w_down, b_down, g_final, consts,
                  y_prompt, y_sample, k_prompt, v_prompt, gla_prompt, k_sample, v_sample, gla_sample):
    with ExitStack() as ctx:
        def sb(name, shape, dt=F32):
            return ctx.enter_context(nc.sbuf_tensor(name, shape, dt))

        def sem(name):
            return ctx.enter_context(nc.semaphore(name))

        h2_rows = nc.dram_tensor("h2_rows", [T, D], F32, kind="Internal").ap()
        y_rows = nc.dram_tensor("y_rows", [T * TOPK * 2, D // 2], F32, kind="Internal").ap()

        ring = sb("ring", [P, RING, SLOT])
        mem = sb("mem", [P, NMEM])
        late = ring[:, PRE:RING, :].rearrange("p a b -> p (a b)")

        def part(base, at, *dims):
            n = 1
            for d in dims:
                n *= d
            v = base[:, at:at + n]
            if len(dims) == 2:
                v = v.rearrange("p (a b) -> p a b", b=dims[1])
            if len(dims) == 3:
                v = v.rearrange("p (a b c) -> p a b c", b=dims[1], c=dims[2])
            return v

        cst = mem[:, 0:NCST]

        def const(name):
            a, n = CST[name]
            return mem[:, a:a + n]

        ident, ones = const("ident"), const("ones")
        o = NCST
        xT = part(mem, o, KD, T)
        hT = part(mem, o + 2560, KD, T)
        grT = part(mem, o + 5120, KD, T)
        sq = grT
        v_tok = part(mem, o + 7680, 3, D)
        x_tok = v_tok
        oTm = part(mem, o + 7680, PAIRS, T)
        h2_tok = v_tok
        gqT = part(mem, o + 10752, GH, T)
        gkT = part(mem, o + 12032, GH, T)
        oTg = part(mem, o + 10752, KD, T)
        mqT = part(mem, o + 13312, PAIRS, T)
        mkT = part(mem, o + 14592, PAIRS, T)
        mv_tok = part(mem, o + 15872, 3, MH * HD)
        g0 = o + 17408
        state = part(mem, g0, GH, DV)
        o_tok = part(mem, g0 + 1024, D)
        q32, k32, q64, k64 = (part(mem, g0 + 3072 + 1024 * j, GH, NP_TOK) for j in range(4))
        q128 = part(mem, g0 + 2048, GH, NP_TOK)
        k128 = part(late, 5120, GH, NP_TOK)
        k_tok = part(late, 6144, 2, GH * DK)
        raw = part(mem, g0 + 3072, MH * HD)
        km = part(mem, g0 + 3072, 2, 8, DK)
        qm = part(late, 5120, 2, 8, NS_TOK)
        rot = part(mem, g0, 2, 3, MH * HD)
        pin = part(mem, g0, 2, 384)
        pexp = part(mem, g0 + 768, 2, 384)
        ptp = part(mem, g0 + 1536, 2, 384)
        om_tok = part(mem, g0 + 2304, 2, MH * HD)
        kTs = part(mem, g0, PAIRS, PAGE * NPAGES)
        pex = part(mem, g0 + 4096, PAGE * NPAGES + NS_TOK)
        pts = part(mem, g0 + 5184, NPAGES, P)
        pto = part(mem, g0 + 6208, P)
        qs = part(mem, g0 + 6336, PAIRS, 32)
        osm = part(mem, g0 + 6464, P)
        e0 = g0 + 7168
        modT = part(mem, e0, 6, KD, 9)
        vT = part(mem, e0 + 432, NVEC)
        w_ga = part(mem, e0 + 512, KD, 16)
        wa2 = part(mem, o + 13312, GH * DK)
        gaT = part(late, 7488, T)
        w_rt = part(mem, e0 + 640, KD, NE)
        b_rt = part(mem, e0 + 896, NE)
        small = e0 + 928
        s1 = part(mem, small, KD, 9)
        colA = part(mem, small + 72, 16)
        colB = part(mem, small + 88, 16)
        colC = part(mem, small + 104, 16)
        colD = part(mem, small + 120, 16)
        eps = part(mem, small + 136, 1)
        eqT = part(late, 0, GH, T)
        ekT = part(late, 1280, GH, T)
        e0T = part(late, 2560, GH, T)
        elT = part(late, 3840, GH, T)
        baT = part(late, 0, KD, T)
        bbT = part(late, 2560, KD, T)
        craw = part(late, 0, D)
        cexp = part(late, 1024, D)
        bT = part(late, 5120, GH, T)
        rstd = part(late, 6400, T)
        scT = part(late, 6720, KD, 32)
        mod_sb = part(late, 6976, 512)
        vraw = part(late, 6976, P)
        att = part(late, 7488, 2, P)
        edec = part(late, 7744, GH, 24)
        tmp = part(late, 7840, 320)
        e32 = part(late, 8096, GH, 8)
        e64 = part(late, 8128, GH, 4)
        e128 = part(late, 8144, GH, 2)
        m0 = o + 10752
        bias = [part(mem, m0, 3072), part(mem, m0 + 3072, 3072)]
        x_in = [part(mem, m0 + 6144, D), part(mem, m0 + 7168, D)]
        xeT = [part(mem, m0 + 8192, KD, BT), part(mem, m0 + 8704, KD, BT)]
        glu = part(mem, m0 + 9216, 512)
        lin = part(mem, m0 + 9728, 512)
        sig = part(mem, m0 + 10240, 512)
        act_m = part(mem, m0 + 10752, 512)
        actT = part(mem, m0 + 11264, 4, 2, BT)
        y_out = [part(mem, m0 + 11776, 512), part(mem, m0 + 12288, 512)]
        r0 = o + 5120
        lg = part(mem, r0, 3, NE)
        top = part(mem, r0 + 96, 3, 8)
        topf = part(mem, r0 + 120, 3, 8)
        oh = part(mem, r0 + 144, 3, TOPK, NE)
        pick = part(mem, r0 + 528, 3, NE)
        pos = part(mem, r0 + 624, 3, NE)
        cnt = part(mem, r0 + 720, NE)
        xtra = part(mem, r0 + 752, NE)
        xend = part(mem, r0 + 784, NE)
        nblk = part(mem, r0 + 816, 3, NE)
        col = part(mem, r0 + 912, 3, NE)
        lg_f = part(mem, r0 + 1772, T)
        rtmp = part(mem, m0 + 9216, 3, TOPK, NE)
        row_k = part(mem, m0 + 9600, 3 * TOPK)
        col_k = part(mem, m0 + 9612, 3 * TOPK)
        row_oh = part(mem, m0 + 9624, 3 * TOPK, BT)
        col_oh = part(mem, m0 + 10392, 3 * TOPK, NCOL)
        asgf = part(mem, r0 + 1136, 3 * TOPK)
        gates = part(mem, r0 + 1148, 3, TOPK)
        gsum = part(mem, r0 + 1160, 3)
        xcmp = part(mem, r0 + 1164, NX, NE)
        gate_p = part(mem, o + 2560, D)
        gate_s = part(mem, o + 3584, D)
        gate_x = part(mem, m0 + 8192, KD, NS_TOK)
        x_res = h2_tok
        gfin = part(mem, g0 + 6144, D)
        ysum = part(mem, m0, 3, D)
        ssq = part(mem, r0 + 2092, 3)
        rinv = part(mem, r0 + 2095, 3)
        topi = sb("topi", [P, 3, 8], U32)
        asg = sb("asg", [P, 3 * TOPK], I32)
        slots = sb("slots", [P, NCOL], I32)
        tok_ix = sb("tok_ix", [P, NCOL], I32)
        row_ix = sb("row_ix", [P, NCOL], I32)
        tok_col = sb("tok_col", [P, 2], I32)
        row_col = sb("row_col", [P, 2], I32)
        eid = sb("eid", [P, NX + 1], I32)
        ptab = sb("ptab", [P, NB * NPAGES], I32)

        ps = ctx.enter_context(nc.psum_tensor("ps", [P, 8, 512], F32))

        land = [sem(f"land{i}") for i in range(RING)]
        slot_used = sem("slot_used")
        s0_used = sem("s0_used")
        cst_in, vec_in, c_in, x_in_s, wsm_in, pt_in = (sem(n) for n in ("cst_in", "vec_in", "c_in", "x_land", "wsm_in", "pt_in"))
        dve_step, act_step, eps_sb = sem("dve_step"), sem("act_step"), sem("eps_sb")
        vecT_ps, vecT_sb, c_exp, c_silu, cT_ps, cT_sb = (sem(n) for n in ("vecT_ps", "vecT_sb", "c_exp", "c_silu", "cT_ps", "cT_sb"))
        xT_ps, xT_sb, sq_sb, ss_ps = (sem(n) for n in ("xT_ps", "xT_sb", "sq_sb", "ss_ps"))
        ada_ps, mod_rows, modT_ps, mod_done = (sem(n) for n in ("ada_ps", "mod_rows", "modT_ps", "mod_done"))
        hp_sb, h_done, hs_done, rms_sb = sem("hp_sb"), sem("h_done"), sem("hs_done"), sem("rms_sb")
        fm_ps, fm_sb, gr_sb, tm_ps, tm_sb = (sem(n) for n in ("fm_ps", "fm_sb", "gr_sb", "tm_ps", "tm_sb"))
        gla_d, gla_a, q128_sb = sem("gla_d"), sem("gla_a"), sem("q128_sb")
        kt_ps, kt_sb, km_sb, qm_sb, att_ps, att_sb, d_ps, s_new, o_part = (
            sem(n) for n in ("kt_ps", "kt_sb", "km_sb", "qm_sb", "att_ps", "att_sb", "d_ps", "s_new", "o_part"))
        o_sq, o_norm, ot_ps, ot_sb = (sem(n) for n in ("o_sq", "o_norm", "ot_ps", "ot_sb"))
        ms_ps, ms_max, ms_exp, mt_ps, mt_sb, mo_ps, mo_sb, mot_ps, mot_sb = (
            sem(n) for n in ("ms_ps", "ms_max", "ms_exp", "mt_ps", "mt_sb", "mo_ps", "mo_sb", "mot_ps", "mot_sb"))
        q_sb, kt2_ps, kt2_sb, cs_ps, cs_max, cs_exp, cp_ps, cp_a, cp_d, co_ps, co_sb, cot_ps, cot_sb = (
            sem(n) for n in ("q_sb", "kt2_ps", "kt2_sb", "cs_ps", "cs_max", "cs_exp", "cp_ps", "cp_a", "cp_d",
                             "co_ps", "co_sb", "cot_ps", "cot_sb"))
        pj_ps, pj_sb, sq2_sb, ss2_ps, rt_ps, h2t_ps, h2t_sb, h2_out = (
            sem(n) for n in ("pj_ps", "pj_sb", "sq2_sb", "ss2_ps", "rt_ps", "h2t_ps", "h2t_sb", "h2_out"))
        asg_in, lgf_ps, lgf_sb, picked, rank_ps, hot_sb, slots_ps, g_max, g_exp, ix_done, route_done = (
            sem(n) for n in ("asg_in", "lgf_ps", "lgf_sb", "picked", "rank_ps", "hot_sb", "slots_ps", "g_max", "g_exp",
                             "ix_done", "route_done"))
        v_land = [sem("v_land0"), sem("v_land1")]
        x_land = [sem("xg_land0"), sem("xg_land1")]
        b_land = [sem("b_land0"), sem("b_land1")]
        y_sent = [sem("y_sent0"), sem("y_sent1")]
        ix_sb, xe_ps, xe_sb, glu_sb, sig_sb, act_sb, at_ps, at_sb, y_sb = (
            sem(n) for n in ("ix_sb", "xe_ps", "xe_sb", "glu_sb", "sig_sb", "act_sb", "at_ps", "at_sb", "y_sb"))
        dve_moe, zero_sb, moe_done, y_free, gfin_in, gate_x_sb, dve_tail, pool_tail = (
            sem(n) for n in ("dve_moe", "zero_sb", "moe_done", "y_free", "gfin_in", "gate_x_sb", "dve_tail", "pool_tail"))
        y_in, y1_sb, x3_sb, rms3_sb, rinv_sb, out_sb = ([sem(f"{w}{t}") for t in range(3)] for w in ("y_in", "y1_sb", "x3_sb", "rms3_sb", "rinv_sb", "out_sb"))
        turns = sem("turns")
        k_out, v_out, gs_out, y_stored = (sem(n) for n in ("k_out", "v_out", "gs_out", "y_stored"))

        N_ADA = [[0, 1, 2, 3], [7, 9, 11, 13], [15, 17, 19, 20]]
        N_GQ, N_GK, N_TM, N_GR = 4, 5, (6, 8, 10, 12, 14), (16, 18)
        N_S0, N_BA, N_CACHE, N_PROJ = 21, 23, 27, 43
        N_PRE = 48
        w_in2 = w_in[0]
        w2d = {N_GQ: (w_in2, C_GQ), N_GK: (w_in2, C_GK)}
        for c, c0 in enumerate((C_GV, C_GV + 512, C_MQ, C_MK, C_MV)):
            w2d[N_TM[c]] = (w_in2, c0)
        for c in range(2):
            w2d[N_GR[c]], w2d[N_BA + c], w2d[N_BA + 2 + c] = (w_in2, C_GR + 512 * c), (w_in2, C_BA + 512 * c), (w_in2, C_BB + 512 * c)
        for n, w, c0 in ((N_PROJ, w_proj_gla, 0), (N_PROJ + 1, w_proj_gla, 512), (N_PROJ + 3, w_out, 0), (N_PROJ + 4, w_out, 512)):
            w2d[n] = (w[0], c0)
        ada_of = {N_ADA[g][q]: (g, q) for g in range(3) for q in range(4)}
        landed, total = {}, [0] * PRE
        for n in range(N_PRE):
            pages = N_CACHE <= n < N_PROJ
            if pages and (n - N_CACHE) % 2:
                continue
            total[n % PRE] += 16 * (NPAGES if pages else 1)
            landed[n] = total[n % PRE]
        land0 = total + [0, 0]
        used = {}
        for n, (g, q) in ada_of.items():
            used[n] = (ada_ps, 4 * g + q + 1)
        for j in range(4):
            used[N_BA + j] = (fm_ps, 33 + 4 * j)
        used[N_GQ], used[N_GK] = (fm_ps, 5), (fm_ps, 9)
        for c in range(5):
            used[N_TM[c]] = (tm_ps, 3 * c + 3)
        used[N_GR[0]], used[N_GR[1]] = (fm_ps, 17), (fm_ps, 21)
        for half in range(2):
            used[N_S0 + half] = (s0_used, 16 * (half + 1))
        for b in range(NB):
            used[N_CACHE + 2 * b], used[N_CACHE + 2 * b + 1] = (kt2_ps, 8 * b + 8), (co_ps, b + 1)
        for j, jobs in enumerate((4, 8, 16, 20, 24)):
            used[N_PROJ + j] = (pj_ps, jobs)

        def item(n):
            return ring[:, n % PRE, :].rearrange("p (a b) -> p a b", b=512)

        def wait_item(eng, n):
            eng.wait_ge(land[n % PRE], landed[n])

        k_pages = cache_k[0].rearrange("n s h d -> n s (h d)")
        v_pages = cache_v[0].rearrange("n s h d -> n s (h d)")
        block = ctx.enter_context(nc.Block())

        @block.sync
        def _(sp):
            sp.dma_start(cst, consts).then_inc(cst_in, 16)
            sp.dma_start(craw[0:1, :], c_prompt).then_inc(c_in, 16)
            sp.dma_start(craw[1:9, :], c_sample).then_inc(c_in, 16)
            for vec, at, n in ((b_ada, V_BADA, 48), (g_norm1, V_G1, 8), (g_norm2, V_G2, 8), (b_gla_a2, V_BA2, 4), (g_gla_head, V_GH, 2)):
                sp.dma_start(vraw[at:at + n, :], vec[0].rearrange("(a b) -> a b", b=P)).then_inc(vec_in, 16)
            sp.dma_start(x_tok[:, 0:2, :], x_prompt[0].rearrange("(a p) d -> p a d", p=P)).then_inc(x_in_s, 16)
            sp.dma_start(x_tok[0:64, 2, :], x_sample.rearrange("b l d -> (b l) d")).then_inc(x_in_s, 16)
            sp.dma_start(w_ga, w_in2[:, C_GA:C_GA + 16].rearrange("(k p) n -> p k n", p=P)).then_inc(wsm_in, 16)
            sp.dma_start(wa2[0:16, :], w_gla_a2[0]).then_inc(wsm_in, 16)
            sp.dma_start(w_rt, w_router[0].rearrange("(k p) n -> p k n", p=P)).then_inc(wsm_in, 16)
            sp.dma_start(b_rt, b_router.to_broadcast([P, NE])).then_inc(wsm_in, 16)
            sp.dma_start(ptab[0:1, :], page_table.rearrange("(o b) n -> o (b n)", o=1)).then_inc(pt_in, 16)

            def load(n):
                if n >= PRE:
                    sp.wait_ge(*used[n - PRE])
                if n in w2d:
                    w, c0 = w2d[n]
                    sp.dma_start(item(n), w[:, c0:c0 + 512].rearrange("(k p) n -> p k n", p=P)).then_inc(land[n % PRE], 16)
                elif n in ada_of:
                    g, q = ada_of[n]
                    sp.dma_start(ring[:, n % PRE, :].rearrange("p (k n) -> p k n", k=2),
                                 w_ada[0, 2 * P * q:2 * P * (q + 1), 2048 * g:2048 * (g + 1)].rearrange("(k p) n -> p k n", p=P)).then_inc(land[n % PRE], 16)
                elif n in (N_S0, N_S0 + 1):
                    b = 4 * (n - N_S0)
                    sp.dma_start(ring[:, n % PRE, :].rearrange("p (b n) -> p b n", n=DV),
                                 state_gla[0, b:b + 4].rearrange("b h k v -> k (b h) v")).then_inc(land[n % PRE], 16)
                else:
                    sp.dma_start(ring[:, n % PRE, :].rearrange("p (k n) -> p k n", n=D),
                                 w_proj_moba[0].rearrange("(k p) n -> p k n", p=P)).then_inc(land[n % PRE], 16)

            for n in range(N_S0 - 1):
                load(n)
            sp.wait_ge(tm_sb, 12)
            sp.dma_start(k_prompt[0, 0].rearrange("(a p) h d -> p a (h d)", p=P), rot[:, 1, 0:2, :]).then_inc(k_out, 16)
            sp.dma_start(k_sample[0].rearrange("b l h d -> (b l) (h d)"), rot[0:64, 1, 2, :]).then_inc(k_out, 16)
            load(N_S0 - 1)
            sp.wait_ge(tm_sb, 15)
            sp.dma_start(v_prompt[0, 0].rearrange("(a p) h d -> p a (h d)", p=P), mv_tok[:, 0:2, :]).then_inc(v_out, 16)
            sp.dma_start(v_sample[0].rearrange("b l h d -> (b l) (h d)"), mv_tok[0:64, 2, :]).then_inc(v_out, 16)
            for n in range(N_S0, N_S0 + PRE):
                load(n)
            sp.wait_ge(s_new, 2 * GH)
            sp.dma_start(gla_prompt[0, 0].rearrange("h k v -> k h v"), state).then_inc(gs_out, 16)
            for half in range(2):
                sp.wait_ge(s_new, 2 * GH + 8 * GH)
                n = N_S0 + half
                sp.dma_start(gla_sample[0, 4 * half:4 * half + 4].rearrange("b h k v -> k (b h) v"),
                             ring[:, n % PRE, :].rearrange("p (b n) -> p b n", n=DV)).then_inc(s0_used, 16)
                sp.wait_ge(s0_used, 16 * (half + 1))
            for n in range(N_S0 + PRE, N_CACHE):
                load(n)
            sp.wait_ge(pt_in, 16)
            def key_pages(b, par):
                n = N_CACHE + 2 * par
                for j in range(NPAGES):
                    page = sp.value_load(ptab[0:1, bass.ds(b * NPAGES + j, 1)], min_val=0, max_val=cache_k.shape[1] - 1)
                    sp.dma_start(item(n)[:, j, :], k_pages[bass.ds(page, 1)].rearrange("o s n -> s (o n)")).then_inc(land[n % PRE], 16)

            for b in range(2):
                sp.wait_ge(*used[N_CACHE + 2 * b - PRE])
                key_pages(b, b)
            with sp.Fori(1, NB // 2) as i:
                for par in range(2):
                    b = i * 2 + par
                    sp.wait_ge(kt2_ps, b * 8 - 8)
                    sp.sem_inc(turns, 1)
                    key_pages(b, par)
            for n in range(N_PROJ, N_PRE):
                load(n)

            def expert_slot(e, s):
                if s < PRE:
                    sp.dma_start(ring[:, s, :].rearrange("p (k n) -> p k n", k=2),
                                 w_gate_up[0, bass.ds(e, 1), 2 * P * s:2 * P * (s + 1), :].rearrange("o (k p) n -> p (o k) n", p=P)).then_inc(land[s], 16)
                else:
                    k = s - PRE
                    sp.dma_start(ring[:, s, :].rearrange("p (k n) -> p k n", k=4),
                                 w_down[0, bass.ds(e, 1), 4 * P * k:4 * P * (k + 1), :].rearrange("o (k p) n -> p (o k) n", p=P)).then_inc(land[s], 16)

            def expert_bias(e, par):
                sp.dma_start(bias[par][0:1, 0:2 * D], b_gate_up[0, bass.ds(e, 1), :]).then_inc(b_land[par], 16)
                sp.dma_start(bias[par][0:1, 2 * D:3 * D], b_down[0, bass.ds(e, 1), :]).then_inc(b_land[par], 16)

            for s in range(PRE):
                sp.wait_ge(*used[N_PRE - PRE + s])
                expert_slot(0, s)
            sp.wait_ge(cot_sb, NB + 1)
            sp.dma_start(gfin, g_final.rearrange("(o d) -> o d", o=1).to_broadcast([P, D])).then_inc(gfin_in, 16)
            for t, (t0, n) in enumerate(TILES):
                sp.wait_ge(h2t_sb, 2 * t + 2)
                sp.dma_start(h2_rows[t0:t0 + n, :], h2_tok[0:n, t, :]).then_inc(h2_out, 16)
            sp.wait_ge(hs_done, 2)
            sp.wait_ge(h_done, 2 * KD)
            expert_slot(0, PRE)
            expert_slot(0, PRE + 1)
            sp.wait_ge(zero_sb, 2)
            expert_bias(0, 0)
            expert_bias(1, 1)

            def expert_loads(e):
                for s in range(RING):
                    sp.wait_ge(slot_used, e * RING + (s + 1 - RING))
                    expert_slot(e, s)

            expert_loads(1)
            with sp.Fori(1, NE // 2) as i:
                for par in range(2):
                    e = i * 2 + par
                    sp.wait_ge(slot_used, e * RING - RING)
                    expert_bias(e, par)
                    expert_loads(e)
            sp.wait_ge(route_done, 1)
            n_extra = sp.value_load(eid[0:1, NX:NX + 1], min_val=0, max_val=NX)
            with sp.If(n_extra > 0):
                with sp.Fori(0, NX) as i:
                    with sp.If(i < n_extra):
                        e = sp.value_load(eid[0:1, bass.ds(i, 1)], min_val=0, max_val=NE - 1)
                        sp.wait_ge(slot_used, (i + NE) * RING)
                        expert_bias(e, 0)
                        for s in range(RING):
                            expert_slot(e, s)
                    sp.nop()
            sp.wait_ge(moe_done, 1)
            for t in TAIL:
                t0, n = TILES[t]
                sp.dma_start(ring[0:n, t, :], y_rows[t0 * 8:(t0 + n) * 8, :].rearrange("(p a) d -> p (a d)", a=8)).then_inc(y_in[t], 16)
            for t in (0, 1, 2):
                t0, n = TILES[t]
                sp.wait_ge(out_sb[t], 1)
                out = y_prompt[0, t0:t0 + n, :] if t < 2 else y_sample.rearrange("b l d -> (b l) d")
                sp.dma_start(out, ysum[0:n, t, :]).then_inc(y_stored, 16)
            sp.wait_ge(gfin_in, 16)
            sp.wait_ge(y_stored, 48)
            sp.wait_ge(k_out, 32)
            sp.wait_ge(v_out, 32)
            sp.wait_ge(gs_out, 16)
            sp.wait_ge(s0_used, 32)

        @block.tensor
        def _(pe):
            mm = nc.tensor.matmul

            def tr(out, in_, n=P):
                return nc.tensor.transpose(out, in_, ident[0:n, 0:n])

            pe.wait_ge(cst_in, 16)
            pe.wait_ge(vec_in, 80)
            tr(ps[:, 0, 0:NVEC], vraw[0:NVEC, :], NVEC).then_inc(vecT_ps, 1)
            pe.wait_ge(x_in_s, 32)
            for k in range(KD):
                if k >= 3:
                    pe.wait_ge(xT_sb, k - 2)
                for t, (t0, n) in enumerate(TILES):
                    last = tr(ps[:, 2 + k % 3, t0:t0 + n], x_tok[0:n, t, k * P:(k + 1) * P], n)
                last.then_inc(xT_ps, 1)
            pe.wait_ge(c_silu, 1)
            for k in range(KD):
                last = tr(ps[:, 1, 16 * k:16 * k + 9], craw[0:9, k * P:(k + 1) * P], 9)
            last.then_inc(cT_ps, 1)
            pe.wait_ge(sq_sb, 8)
            for k in range(KD):
                last = mm(ps[:, 5, 0:T], ones, sq[:, k, :], start=k == 0, stop=k == KD - 1)
            last.then_inc(ss_ps, 1)

            def ada(g, q):
                if q == 0 and g:
                    pe.wait_ge(mod_done, g)
                elif q == 0:
                    pe.wait_ge(cT_sb, 1)
                wait_item(pe, N_ADA[g][q])
                w = ring[:, N_ADA[g][q] % PRE, :].rearrange("p (k n) -> p k n", k=2)
                for k in range(2):
                    for j in range(4):
                        last = mm(ps[32 * j:32 * j + 32, 6, :], scT[:, 2 * q + k, :], w[:, k, 512 * j:512 * j + 512],
                                  start=q == 0 and k == 0, stop=q == 3 and k == 1)
                last.then_inc(ada_ps, 1)

            def ada_rows(g):
                pe.wait_ge(mod_rows, g + 1)
                for c in range(4):
                    last = tr(ps[:, 7, c * P:(c + 1) * P], mod_sb[:, c * P:(c + 1) * P])
                last.then_inc(modT_ps, 1)

            for q in range(4):
                ada(0, q)
            ada_rows(0)

            def fm_free(n):
                if n >= 3:
                    pe.wait_ge(fm_sb, n - 2)
                    if 13 <= n - 3 < 21:
                        pe.wait_ge(gr_sb, n - 15)

            def fm(n, w, M=P):
                fm_free(n)
                for k in range(KD):
                    if n == 0:
                        pe.wait_ge(h_done, k + 1)
                    last = mm(ps[0:M, n % 3, 0:T], w[:, k, :], hT[:, k, :], start=k == 0, stop=k == KD - 1)
                last.then_inc(fm_ps, 1)

            def fm_item(n0, it):
                wait_item(pe, it)
                for m in range(4):
                    fm(n0 + m, item(it)[:, :, m * P:(m + 1) * P])

            pe.wait_ge(hs_done, 1)
            pe.wait_ge(wsm_in, 64)
            fm(0, w_ga, 16)
            fm_item(1, N_GQ)
            fm_item(5, N_GK)
            pe.wait_ge(fm_sb, 1)
            for h in range(GH):
                fm_free(9 + h)
                mm(ps[:, (9 + h) % 3, 0:T], wa2[0:16, h * DK:(h + 1) * DK], gaT[0:16, :], start=True, stop=True).then_inc(fm_ps, 1)
            for c in range(5):
                wait_item(pe, N_TM[c])
                for t, (t0, n) in enumerate(TILES):
                    if 3 * c + t >= 3:
                        pe.wait_ge(tm_sb, 3 * c + t - 2)
                    for k in range(KD):
                        if t < 2:
                            last = mm(ps[0:n, 3 + t, :], hT[:, k, t0:t0 + n], item(N_TM[c])[:, k, :], start=k == 0, stop=k == KD - 1)
                            continue
                        for f in range(2):
                            last = mm(ps[64 * f:64 * f + 64, 5, 0:256], hT[:, k, t0:t0 + n], item(N_TM[c])[:, k, 256 * f:256 * f + 256],
                                      start=k == 0, stop=k == KD - 1)
                    last.then_inc(tm_ps, 1)
                    if c == 4 and t == 0:
                        ada_rows(1)
                if c < 4:
                    ada(1, c)
            ada(2, 0)
            fm_item(13, N_GR[0])
            ada(2, 1)
            fm_item(17, N_GR[1])
            ada(2, 2)
            ada(2, 3)
            pe.wait_ge(tm_sb, 12)
            for j in range(8):
                which, p = divmod(j, 4)
                fm_free(21 + j)
                for t, (t0, n) in enumerate(TILES):
                    last = tr(ps[:, (21 + j) % 3, t0:t0 + n], rot[0:n, which, t, p * P:(p + 1) * P], n)
                last.then_inc(fm_ps, 1)
            ada_rows(2)

            pe.wait_ge(fm_sb, 29)
            pe.wait_ge(gla_d, 5)
            pe.wait_ge(tm_sb, 15)
            pe.wait_ge(mod_done, 3)
            for t, (t0, n) in enumerate(TILES):
                for h in range(GH):
                    last = tr(ps[0:n, (2, 7, 3)[t], h * DK:(h + 1) * DK], (elT if t == 2 else k128)[:, h, t0:t0 + n])
            last.then_inc(kt_ps, 1)

            def att_scores(u):
                t, h = divmod(u, GH)
                cols = slice(t * P, (t + 1) * P)
                if u:
                    pe.wait_ge(att_sb, u)
                for j, (kk, qq) in enumerate(((ekT, eqT), (elT, e0T), (k32, q32), (k64, q64))):
                    last = mm(ps[:, 4, j * P:(j + 1) * P], kk[:, h, cols], qq[:, h, cols], start=True, stop=True)
                last.then_inc(att_ps, 1)

            def o_and_delta(u):
                t, h = divmod(u, GH)
                values = v_tok[:, t, h * DV:(h + 1) * DV]
                pe.wait_ge(att_sb, u + 1)
                if u >= 2:
                    pe.wait_ge(o_norm, u - 1)
                if t:
                    pe.wait_ge(s_new, h + 1)
                    pe.wait_ge(q128_sb, 1)
                    mm(ps[:, 5 + u % 2, 0:DV], q128[:, h, P:2 * P], state[:, h, :], start=True, stop=False)
                mm(ps[:, 5 + u % 2, 0:DV], att[:, u % 2, :], values, start=t == 0, stop=True).then_inc(o_part, 1)
                pe.wait_ge(kt_sb, 1)
                if u >= 2:
                    pe.wait_ge(s_new, u - 1)
                mm(ps[:, u % 2, 0:DV], k_tok[:, t, h * DK:(h + 1) * DK], values, start=True, stop=True).then_inc(d_ps, 1)

            def o_transposes(t):
                n = TILES[t][1]
                pe.wait_ge(o_norm, GH * (t + 1))
                if t:
                    pe.wait_ge(ot_sb, t)
                for m in range(KD):
                    last = tr(ps[:, 7 if m < 4 else 2, (m % 4) * n:(m % 4 + 1) * n], o_tok[0:n, m * P:(m + 1) * P], n)
                last.then_inc(ot_ps, 1)

            att_scores(0)
            for u in range(2 * GH):
                if u + 1 < 2 * GH:
                    att_scores(u + 1)
                o_and_delta(u)
                if u == GH:
                    o_transposes(0)
            n, s0 = NS_TOK, slice(NP_TOK, T)
            for h in range(GH):
                u = 2 * GH + h
                x0 = 2 * GH + 8 * h
                pe.wait_ge(att_sb, u)
                mm(ps[0:n, 4, 0:n], ekT[:, h, s0], eqT[:, h, s0], start=True, stop=True).then_inc(att_ps, 1)
                if h == 0:
                    o_transposes(1)
                    wait_item(pe, N_S0)
                    wait_item(pe, N_S0 + 1)
                pe.wait_ge(att_sb, u + 1)
                pe.wait_ge(km_sb, h + 1)
                pe.wait_ge(qm_sb, h + 1)
                pe.wait_ge(o_norm, u - 1)
                values = v_tok[:, 2, h * DV:(h + 1) * DV]
                mm(ps[0:n, 5 + u % 2, 0:DV], att[:, u % 2, 0:n], values, start=True, stop=False)

                def delta(c):
                    pe.wait_ge(s_new, max(2 * GH, x0 + c - 2))
                    if h == 0 and c == 2:
                        pe.wait_ge(ot_sb, 2)
                    mm(ps[:, (8 * h + c) % 3, 0:DV], km[:, h % 2, c, :], values, start=True, stop=True).then_inc(d_ps, 1)

                delta(0)
                delta(1)
                for c in range(8):
                    prior = ring[:, (N_S0 + c // 4) % PRE, ((c % 4) * GH + h) * DV:((c % 4) * GH + h + 1) * DV]
                    mm(ps[0:n, 5 + u % 2, 0:DV], qm[:, h % 2, c, :], prior, start=False, stop=c == 7).then_inc(o_part, 1)
                    if c < 6:
                        delta(c + 2)
            o_transposes(2)

            pe.wait_ge(s_new, 10 * GH)
            pe.wait_ge(ot_sb, 3)

            def gate_job(n):
                it, m = N_BA + (n - 29) // 4, (n - 29) % 4
                wait_item(pe, it)
                if n >= 31:
                    pe.wait_ge(fm_sb, n - 1)
                for k in range(KD):
                    last = mm(ps[:, n % 2, 0:T], item(it)[:, k, m * P:(m + 1) * P], hT[:, k, :], start=k == 0, stop=k == KD - 1)
                last.then_inc(fm_ps, 1)

            def prompt_scores(h):
                p, q0 = h // 2, HD * (h % 2)
                if h >= 2:
                    pe.wait_ge(ms_max, h - 1)
                bank = 2 + h % 2
                mm(ps[:, bank, 0:128], mqT[q0:q0 + HD, p, 0:128], mkT[q0:q0 + HD, p, 0:128], start=True, stop=True)
                mm(ps[:, bank, 128:384], mqT[q0:q0 + HD, p, 128:256], mkT[q0:q0 + HD, p, 0:256], start=True, stop=True).then_inc(ms_ps, 1)

            def prompt_probs(h):
                pe.wait_ge(ms_exp, h + 1)
                if h >= 2:
                    pe.wait_ge(mt_sb, h - 1)
                for j in range(3):
                    last = tr(ps[:, 4 + h % 2, j * P:(j + 1) * P], pexp[:, h % 2, j * P:(j + 1) * P])
                last.then_inc(mt_ps, 1)

            def prompt_values(h):
                pe.wait_ge(mt_sb, h + 1)
                if h >= 2:
                    pe.wait_ge(mo_sb, h - 1)
                bank, hs = 6 + h % 2, slice(h * HD, (h + 1) * HD)
                mm(ps[:, bank, 0:HD], ptp[:, h % 2, 0:P], mv_tok[:, 0, hs], start=True, stop=True)
                mm(ps[:, bank, HD:2 * HD], ptp[:, h % 2, P:2 * P], mv_tok[:, 0, hs], start=True, stop=False)
                mm(ps[:, bank, HD:2 * HD], ptp[:, h % 2, 2 * P:3 * P], mv_tok[:, 1, hs], start=False, stop=True).then_inc(mo_ps, 1)

            for h in range(MH):
                gate_job(29 + 2 * h)
                if h:
                    prompt_values(h - 1)
                prompt_scores(h)
                gate_job(30 + 2 * h)
                prompt_probs(h)
            prompt_values(MH - 1)
            pe.wait_ge(mo_sb, MH)
            for p in range(PAIRS):
                for t in range(2):
                    last = tr(ps[:, 4 + p // 2, (p % 2) * 256 + t * P:(p % 2) * 256 + (t + 1) * P], om_tok[:, t, p * P:(p + 1) * P])
            last.then_inc(mot_ps, 1)
            pe.wait_ge(mot_sb, 2)
            pe.wait_ge(fm_sb, 45)

            def probs_copied(n):
                pe.wait_ge(cp_a, n)
                pe.wait_ge(cp_d, n)

            def cache_keys(b, half, par):
                nk = N_CACHE + 2 * par
                pe.wait_ge(land[nk % PRE], half * (16 * NPAGES) + landed[nk])
                for jj in range(2 * PAIRS):
                    p, f = divmod(jj, 2)
                    if jj >= 4:
                        pe.wait_ge(kt2_sb, b * 8 + jj - 3)
                    for q in range(4):
                        last = tr(ps[:, jj % 4, q * P:(q + 1) * P], item(nk)[:, 4 * f + q, p * P:(p + 1) * P])
                    last.then_inc(kt2_ps, 1)

            def cache_scores(b):
                pe.wait_ge(kt2_sb, b * 8 + 8)
                pe.wait_ge(q_sb, b + 1)
                for f in range(2):
                    for p in range(PAIRS):
                        mm(ps[32 * p:32 * p + 32, 4 + f, :], qs[:, p, :], kTs[:, p, 512 * f:512 * f + 512], start=True, stop=True)
                for p in range(PAIRS):
                    last = mm(ps[32 * p:32 * p + 32, 6, 0:NS_TOK], qs[:, p, :], mkT[:, p, NP_TOK:T], start=True, stop=True)
                last.then_inc(cs_ps, 1)

            def cache_probs(b, keys_before):
                pe.wait_ge(kt2_sb, keys_before)
                pe.wait_ge(cs_exp, b + 1)
                for j in range(NPAGES):
                    last = tr(ps[:, j // 4, (j % 4) * P:(j % 4 + 1) * P], pex[:, j * P:(j + 1) * P])
                last = tr(ps[0:NS_TOK, 2, 0:P], pex[:, PAGE * NPAGES:])
                last.then_inc(cp_ps, 1)

            def cache_values(b, half, par):
                nv = N_CACHE + 2 * par + 1
                pe.wait_ge(v_land[par], (half + 1) * (16 * NPAGES))
                for j in range(NPAGES + 1):
                    for p in range(PAIRS):
                        if j < NPAGES:
                            last = mm(ps[32 * p:32 * p + 32, 7, 0:P], pts[:, j, 32 * p:32 * p + 32], item(nv)[:, j, p * P:(p + 1) * P],
                                      start=j == 0, stop=False)
                        else:
                            last = mm(ps[32 * p:32 * p + 32, 7, 0:P], pto[:, 32 * p:32 * p + 32],
                                      mv_tok[:, 2, p * P:(p + 1) * P], start=False, stop=True)
                last.then_inc(co_ps, 1)

            def cache_out(b):
                pe.wait_ge(co_sb, b + 1)
                tr(ps[:, 7, 0:P], osm).then_inc(cot_ps, 1)

            def square_sum(k):
                pe.wait_ge(sq2_sb, k + 1)
                last = mm(ps[:, 4, 0:T], ones, sq[:, k, :], start=k == 0, stop=k == KD - 1)
                if k == KD - 1:
                    last.then_inc(ss2_ps, 1)

            def project(n):
                which, m = divmod(n, KD)
                it = N_PROJ + (m // 4 if which == 0 else 2 if which == 1 else 3 + m // 4)
                wait_item(pe, it)
                if n >= 4:
                    pe.wait_ge(pj_sb, n - 3)
                if n == 16:
                    pe.wait_ge(pj_sb, 16)
                kc = PAIRS if which == 1 else KD
                w = ring[:, it % PRE, :].rearrange("p (k n) -> p k n", k=kc)
                src = (oTg, oTm, hT)[which]
                c0 = m * P if which == 1 else (m % 4) * P
                for k in range(kc):
                    last = mm(ps[:, n % 4, 0:T], w[:, k, c0:c0 + P], src[:, k, :], start=k == 0, stop=k == kc - 1)
                last.then_inc(pj_ps, 1)
            pe.sem_inc(cot_sb, 1)
            cache_keys(0, 0, 0)
            cache_scores(0)
            cache_keys(1, 0, 1)
            cache_probs(0, 15)

            def cache_turn(b, half, par):
                cache_scores(b)
                probs_copied(b)
                cache_keys(b + 1, half + par, 1 - par)
                pe.wait_ge(cot_sb, b)
                cache_values(b - 1, half + par - 1, 1 - par)
                cache_probs(b, b * 8 + 15)
                cache_out(b - 1)

            with pe.Fori(0, NB // 2 - 1) as i:
                for sub in range(2):
                    cache_turn(i * 2 + 1 + sub, i + sub, 1 - sub)
            cache_scores(NB - 1)
            probs_copied(NB - 1)
            for n in range(4):
                project(n)
            pe.wait_ge(cot_sb, NB - 1)
            cache_values(NB - 2, NB // 2 - 1, 0)
            pe.wait_ge(pj_sb, 4)
            cache_probs(NB - 1, NB * 8)
            cache_out(NB - 2)
            probs_copied(NB)
            pe.wait_ge(cot_sb, NB)
            cache_values(NB - 1, NB // 2 - 1, 1)
            cache_out(NB - 1)

            for n in range(4, 24):
                project(n)
                if n > 17:
                    square_sum(n - 18)
            square_sum(6)

            square_sum(7)
            pe.wait_ge(hs_done, 2)
            for a in range(2):
                for j in range(4):
                    pe.wait_ge(h_done, KD + 4 * a + j + 1)
                    last = mm(ps[32 * j:32 * j + 32, 5, 0:T], w_rt[:, 4 * a + j, :], hT[:, 4 * a + j, :], start=a == 0, stop=a == 1)
            last.then_inc(lgf_ps, 1)
            pe.wait_ge(lgf_sb, 1)
            for t, (t0, n) in enumerate(TILES):
                last = mm(ps[0:n, 6, NE * t:NE * t + NE], lg_f[:, t0:t0 + n], const("stack"), start=True, stop=True)
            last.then_inc(rt_ps, 1)
            for t, (t0, n) in enumerate(TILES):
                for f in range(2):
                    if 2 * t + f >= 4:
                        pe.wait_ge(h2t_sb, 2 * t + f - 3)
                    for q in range(4):
                        last = tr(ps[0:n, (2 * t + f) % 4, q * P:(q + 1) * P], hT[:, 4 * f + q, t0:t0 + n])
                    last.then_inc(h2t_ps, 1)
            pe.wait_ge(picked, 1)
            mm(ps[:, 4, 0:NE], const("before"), pick[:, 0, :], start=True, stop=True)
            for tt in range(3):
                nn, cols = TILES[tt][1], slice(NE * (tt + 1), 4 * NE)
                mm(ps[:, 4, cols], ones[0:nn, :], pick[0:nn, tt, None, :].to_broadcast([nn, 3 - tt, NE]), start=tt == 0, stop=False)
            for t in (2, 1):
                n = TILES[t][1]
                last = mm(ps[0:n, 4, NE * t:NE * t + NE], const("before")[0:n, 0:n], pick[0:n, t, :], start=False, stop=t == 1)
            last.then_inc(rank_ps, 1)
            pe.wait_ge(gate_x_sb, 1)
            for i in range(10):
                pe.wait_ge(h2t_sb, i + 3)
                for q in range(4):
                    m, cols = 4 * (i % 2) + q, slice(q * P, (q + 1) * P)
                    if i < 2:
                        last = mm(ps[:, (6 + i) % 4, cols], modT[:, 5, m, 0:1].to_broadcast([P, P]), ident, start=True, stop=True)
                    elif i < 4:
                        last = mm(ps[0:NS_TOK, (6 + i) % 4, cols], gate_x[:, m, :], ident, start=True, stop=True)
                    else:
                        t0, n = TILES[(i - 4) // 2]
                        last = tr(ps[0:n, (6 + i) % 4, cols], xT[:, m, t0:t0 + n])
                last.then_inc(h2t_ps, 1)
            pe.wait_ge(hot_sb, 1)
            for j in range(3 * TOPK):
                nn = TILES[j // TOPK][1]
                last = mm(ps[0:BT, 7, 0:NCOL], row_oh[0:nn, j, :], col_oh[0:nn, j, :], start=j == 0, stop=j == 3 * TOPK - 1)
            last.then_inc(slots_ps, 1)

            def xe_transposes(par, n, gathered):
                pe.wait_ge(x_land[par], gathered)
                pe.sem_inc(turns, 1)
                for k in range(KD):
                    last = tr(ps[:, par, k * BT:(k + 1) * BT], x_in[par][0:BT, k * P:(k + 1) * P], BT)
                last.then_inc(xe_ps, 1)

            def gate_up_bias(par, biases):
                pe.wait_ge(b_land[par], biases)
                for q in range(4):
                    out = ps[64 * (q % 2):64 * (q % 2) + 64, 2 + 2 * (q // 2) + par, :]
                    mm(out, const("row0"), bias[par][:, 512 * q:512 * q + 512], start=True, stop=False)

            def gate_up(par, n, weights):
                pe.wait_ge(xe_sb, n + 1)
                for s in range(PRE):
                    pe.wait_ge(land[s], weights + land0[s])
                    w = ring[:, s, :].rearrange("p (k n) -> p k n", k=2)
                    for k in range(2):
                        for q in range(4):
                            out = ps[64 * (q % 2):64 * (q % 2) + 64, 2 + 2 * (q // 2) + par, :]
                            last = mm(out, xeT[par][:, 2 * s + k, :], w[:, k, 512 * q:512 * q + 512], start=False, stop=s == 3 and k == 1)
                    last.then_inc(slot_used, 1)

            def down(par, n, weights):
                pe.wait_ge(act_sb, n + 1)
                for c in range(4):
                    last = tr(ps[:, 6, c * P:(c + 1) * P], act_m[:, c * P:(c + 1) * P])
                last.then_inc(at_ps, 1)
                for f in range(2):
                    mm(ps[64 * f:64 * f + 64, 7, :], const("row0"), bias[par][:, 2048 + 512 * f:2560 + 512 * f], start=True, stop=False)
                pe.wait_ge(at_sb, n + 1)
                for s in range(2):
                    pe.wait_ge(land[PRE + s], weights)
                    w = ring[:, PRE + s, :].rearrange("p (k n) -> p k n", k=4)
                    for k in range(4):
                        for f in range(2):
                            last = mm(ps[64 * f:64 * f + 64, 7, :], actT[:, k, s, :], w[:, k, 512 * f:512 * f + 512], start=False, stop=s == 1 and k == 3)
                    last.then_inc(slot_used, 1)

            pe.wait_ge(ix_done, 1)
            pe.wait_ge(h2t_sb, 16)
            with pe.Fori(0, NE // 2) as i:
                for par in range(2):
                    n = i * 2 + par
                    gate_up_bias(par, (i + 1) * 32)
                    xe_transposes(par, n, (i + 1) * 16)
                    gate_up(par, n, (n + 1) * 16)
                    down(par, n, (n + 1) * 16)
            pe.wait_ge(route_done, 1)
            n_extra = pe.value_load(eid[0:1, NX:NX + 1], min_val=0, max_val=NX)
            with pe.If(n_extra > 0):
                with pe.Fori(0, NX) as i:
                    with pe.If(i < n_extra):
                        n = i + NE
                        gate_up_bias(0, (i + (NE // 2 + 1)) * 32)
                        xe_transposes(0, n, (i + (NE // 2 + 1)) * 16)
                        gate_up(0, n, (n + 1) * 16)
                        down(0, n, (n + 1) * 16)
                    pe.nop()

        @block.scalar
        def _(act):
            a = nc.scalar
            act.wait_ge(c_in, 32)
            a.activation(cexp[0:9, :], craw[0:9, :], ACT.Exp, scale=-1.0).then_inc(c_exp, 1)
            for k in range(KD):
                act.wait_ge(xT_ps, k + 1)
                a.copy(xT[:, k, :], ps[:, 2 + k % 3, 0:T]).then_inc(xT_sb, 1)
            act.wait_ge(vecT_sb, 1)
            act.wait_ge(eps_sb, 1)
            act.wait_ge(ss_ps, 1)
            a.activation(rstd, ps[:, 5, 0:T], ACT.Sqrt, scale=1.0 / D, bias=eps).then_inc(rms_sb, 1)

            def shifted(shift, before):
                for k in range(KD):
                    act.wait_ge(hp_sb, before + k + 1)
                    a.activation(hT[:, k, 0:NP_TOK], hT[:, k, 0:NP_TOK], ACT.Identity, bias=modT[:, shift, k, 0:1]).then_inc(h_done, 1)

            shifted(0, 0)
            for n in range(13):
                act.wait_ge(fm_ps, n + 1)
                bank = ps[:, n % 3, 0:T]
                if n == 0:
                    a.copy(gaT[0:16, :], bank[0:16, :]).then_inc(fm_sb, 1)
                elif n < 5:
                    a.copy(gqT[:, n - 1, :], bank).then_inc(fm_sb, 1)
                elif n < 9:
                    a.copy(gkT[:, n - 5, :], bank).then_inc(fm_sb, 1)
                else:
                    h = n - 9
                    a.activation(elT[:, h, :], bank, ACT.Identity, bias=vT[:, V_BA2 + h:V_BA2 + h + 1]).then_inc(fm_sb, 1)
            act.wait_ge(gla_d, 1)
            a.activation(eqT, eqT, ACT.Exp).then_inc(act_step, 1)
            act.wait_ge(act_step, 1)
            a.activation(eqT, eqT, ACT.Ln, bias=1.0).then_inc(gla_a, 1)
            act.wait_ge(gla_d, 3)
            a.activation(ekT, eqT, ACT.Exp, scale=-1.0 / GATE_NORM).then_inc(act_step, 1)
            act.wait_ge(act_step, 2)
            a.activation(eqT, eqT, ACT.Exp, scale=1.0 / GATE_NORM).then_inc(act_step, 1)
            a.activation(e0T, bT, ACT.Exp, scale=1.0 / GATE_NORM).then_inc(gla_a, 1)
            act.wait_ge(gla_d, 4)
            a.activation(elT, elT, ACT.Exp, scale=1.0 / GATE_NORM).then_inc(gla_a, 1)
            for n in range(13, 21):
                act.wait_ge(fm_ps, n + 1)
                a.activation(grT[:, n - 13, :], ps[:, n % 3, 0:T], ACT.Sigmoid).then_inc(fm_sb, 1)
            for n in range(21, 29):
                act.wait_ge(fm_ps, n + 1)
                which, p = divmod(n - 21, 4)
                a.copy((mqT, mkT)[which][:, p, :], ps[:, n % 3, 0:T]).then_inc(fm_sb, 1)
            act.wait_ge(kt_ps, 1)
            a.copy(k_tok[:, 0, :], ps[:, 2, :])
            a.copy(k_tok[:, 1, :], ps[:, 7, :]).then_inc(kt_sb, 1)
            for t, (t0, n) in enumerate(TILES):
                for h in range(GH):
                    u = GH * t + h
                    act.wait_ge(o_part, u + 1 if t < 2 else 2 * GH + 8 * h + 8)
                    if u >= 2:
                        act.wait_ge(o_norm, u - 1)
                    a.activation(tmp[0:n, 0:DV], ps[0:n, 5 + u % 2, 0:DV], ACT.Square, accum_out=colA[0:n, u % 2:u % 2 + 1]).then_inc(act_step, 1)
                    act.wait_ge(act_step, 4 + u)
                    a.activation(colC[0:n, u % 2:u % 2 + 1], colA[0:n, u % 2:u % 2 + 1], ACT.Sqrt, scale=1.0 / DV, bias=eps[0:n]).then_inc(o_sq, 1)
            def gate(n):
                act.wait_ge(fm_ps, n + 1)
                m = n - 29
                a.activation((baT if m < 8 else bbT)[:, m % 8, :], ps[:, n % 2, 0:T], ACT.Sigmoid).then_inc(fm_sb, 1)

            for h in range(MH):
                gate(29 + 2 * h)
                act.wait_ge(ms_max, h + 1)
                if h >= 2:
                    act.wait_ge(mt_ps, h - 1)
                    act.wait_ge(mo_sb, h - 1)
                e = pexp[:, h % 2, :]
                x = pin[:, h % 2, :]
                for t, (c0, c1) in enumerate(((0, P), (P, 3 * P))):
                    last = a.activation(e[:, c0:c1], x[:, c0:c1], ACT.Exp, scale=HD ** -0.5, bias=colB[:, 2 * (h % 2) + t:2 * (h % 2) + t + 1],
                                        accum_out=colC[:, 2 * (h % 2) + t:2 * (h % 2) + t + 1])
                last.then_inc(ms_exp, 1)
                gate(30 + 2 * h)
                act.wait_ge(mt_ps, h + 1)
                if h >= 2:
                    act.wait_ge(mo_ps, h - 1)
                a.copy(ptp[:, h % 2, :], ps[:, 4 + h % 2, 0:384]).then_inc(mt_sb, 1)
            act.wait_ge(mot_ps, 1)
            for f in range(2):
                a.copy(oTm[:, 2 * f:2 * f + 2, 0:NP_TOK], ps[:, 4 + f, :].rearrange("p (a b) -> p a b", b=NP_TOK)).then_inc(mot_sb, 1)
            def cache_keys(b):
                for jj in range(8):
                    act.wait_ge(kt2_ps, b * 8 + jj + 1)
                    f = jj % 2
                    a.copy(kTs[:, jj // 2, 512 * f:512 * f + 512], ps[:, jj % 4, :]).then_inc(kt2_sb, 1)

            def cache_exp(b):
                act.wait_ge(cs_max, b + 1)
                for j in range(NBLK + 1):
                    c0, c1 = (BLOCK * j, BLOCK * (j + 1)) if j < NBLK else (PAGE * NPAGES, PAGE * NPAGES + NS_TOK)
                    src = ps[:, 4 + j // 2, (j % 2) * BLOCK:(j % 2 + 1) * BLOCK] if j < NBLK else tmp[:, 0:NS_TOK]
                    last = a.activation(pex[:, c0:c1], src, ACT.Exp, scale=HD ** -0.5, bias=colB[:, j:j + 1], accum_out=colC[:, j:j + 1])
                last.then_inc(cs_exp, 1)
                act.wait_ge(cp_ps, b + 1)
                a.copy(pts[:, 0:4, :], ps[:, 0, :].rearrange("p (a b) -> p a b", b=P))
                a.copy(pto[0:NS_TOK, :], ps[0:NS_TOK, 2, 0:P]).then_inc(cp_a, 1)

            cache_keys(0)
            with act.Fori(0, NB - 1) as b:
                cache_keys(b + 1)
                cache_exp(b)
            cache_exp(NB - 1)
            act.wait_ge(ss2_ps, 1)
            a.activation(rstd, ps[:, 4, 0:T], ACT.Sqrt, scale=1.0 / D, bias=eps).then_inc(rms_sb, 1)
            shifted(3, KD)
            act.wait_ge(lgf_ps, 1)
            a.copy(lg_f, ps[:, 5, 0:T]).then_inc(lgf_sb, 1)
            for j in range(6):
                t, f = divmod(j, 2)
                n = TILES[t][1]
                act.wait_ge(h2t_ps, j + 1)
                a.copy(h2_tok[0:n, t, 512 * f:512 * f + 512], ps[0:n, j % 4, :]).then_inc(h2t_sb, 1)
            act.wait_ge(g_max, 1)
            for t, (t0, n) in enumerate(TILES):
                last = a.activation(gates[0:n, t, :], top[0:n, t, 0:TOPK], ACT.Exp, bias=colD[0:n, t:t + 1], accum_out=gsum[0:n, t:t + 1])
            last.then_inc(g_exp, 1)
            for i in range(10):
                act.wait_ge(h2t_ps, 7 + i)
                if i == 4:
                    act.wait_ge(h2_out, 48)
                half = slice(512 * (i % 2), 512 * (i % 2) + 512)
                if i < 4:
                    n = P if i < 2 else NS_TOK
                    to = (gate_p if i < 2 else gate_s)[0:n, half]
                else:
                    n = TILES[(i - 4) // 2][1]
                    to = x_res[0:n, (i - 4) // 2, half]
                a.copy(to, ps[0:n, (6 + i) % 4, :]).then_inc(h2t_sb, 1)

            def expert(par, n):
                act.wait_ge(xe_ps, n + 1)
                a.copy(xeT[par], ps[:, par, :].rearrange("p (k n) -> p k n", n=BT)).then_inc(xe_sb, 1)
                act.wait_ge(glu_sb, n + 1)
                a.activation(sig, glu, ACT.Sigmoid, scale=ALPHA).then_inc(sig_sb, 1)
                act.wait_ge(at_ps, n + 1)
                a.copy(actT, ps[:, 6, :].rearrange("p (c f n) -> p c f n", c=4, f=2)).then_inc(at_sb, 1)

            with act.Fori(0, NE // 2) as i:
                for par in range(2):
                    expert(par, i * 2 + par)
            act.wait_ge(route_done, 1)
            n_extra = act.value_load(eid[0:1, NX:NX + 1], min_val=0, max_val=NX)
            with act.If(n_extra > 0):
                with act.Fori(0, NX) as i:
                    with act.If(i < n_extra):
                        expert(0, i + NE)
                    act.nop()
            for t in TAIL:
                n = TILES[t][1]
                act.wait_ge(y_in[t], 16)
                for k in (range(TOPK) if t == 2 else (1,)):
                    yk = ring[0:n, t, D * k:D * (k + 1)]
                    a.activation(yk, yk, ACT.Copy, scale=gates[0:n, t, k:k + 1]).then_inc(y1_sb[t], 1)
            for t in (0, 2, 1):
                n = TILES[t][1]
                act.wait_ge(x3_sb[t], 1)
                a.activation(ring[0:n, 3 + t, 0:D], ysum[0:n, t, :], ACT.Square, accum_out=ssq[0:n, t:t + 1]).then_inc(rms3_sb[t], 1)
                act.wait_ge(rms3_sb[t], 1)
                a.activation(ssq[0:n, t:t + 1], ssq[0:n, t:t + 1], ACT.Sqrt, scale=1.0 / D, bias=eps[0:n]).then_inc(rms3_sb[t], 1)
            act.wait_ge(rinv_sb[2], 1)
            a.activation(ring[0:NS_TOK, 2, 0:D], ysum[0:NS_TOK, 2, :], ACT.Copy, scale=rinv[0:NS_TOK, 2:3]).then_inc(rms3_sb[2], 1)

        def combined(v, eng, link, t):
            n = TILES[t][1]
            eng.wait_ge(y_in[t], 16)
            eng.wait_ge(y1_sb[t], 1)
            y = ring[0:n, t, :].rearrange("p (k d) -> p k d", k=TOPK)
            acc = ysum[0:n, t, :]
            link(v.scalar_tensor_tensor(acc, y[:, 0, :], gates[0:n, t, 0:1], y[:, 1, :], ALU.mult, ALU.add))
            for k in range(2, TOPK):
                link(v.scalar_tensor_tensor(acc, y[:, k, :], gates[0:n, t, k:k + 1], acc, ALU.mult, ALU.add))
            link(v.tensor_tensor(acc, acc, gate_p[0:n, :], ALU.mult))
            v.tensor_tensor(acc, acc, x_res[0:n, t, :], ALU.add).then_inc(x3_sb[t], 1)

        def final_norm(v, t):
            n = TILES[t][1]
            v.scalar_tensor_tensor(ysum[0:n, t, :], ysum[0:n, t, :], rinv[0:n, t:t + 1], gfin[0:n, :], ALU.mult, ALU.mult).then_inc(out_sb[t], 1)

        @block.vector
        def _(dve):
            v = nc.vector
            st = Steps(dve, dve_step)
            link = st.link
            v.memset(eps, EPS).then_inc(eps_sb, 1)
            link(v.memset(scT, 0.0))
            dve.wait_ge(vecT_ps, 1)
            v.tensor_copy(vT, ps[:, 0, 0:NVEC]).then_inc(vecT_sb, 1)
            dve.wait_ge(c_exp, 1)
            link(v.tensor_scalar_add(cexp[0:9, :], cexp[0:9, :], 1.0))
            link(v.reciprocal(cexp[0:9, :], cexp[0:9, :]))
            v.tensor_tensor(craw[0:9, :], craw[0:9, :], cexp[0:9, :], ALU.mult).then_inc(c_silu, 1)
            for k in range(KD):
                dve.wait_ge(xT_sb, k + 1)
                v.tensor_tensor(sq[:, k, :], xT[:, k, :], xT[:, k, :], ALU.mult).then_inc(sq_sb, 1)
            dve.wait_ge(cT_ps, 1)
            v.tensor_copy(scT[:, :, 0:9], ps[:, 1, 0:128].rearrange("p (k n) -> p k n", n=16)[:, :, 0:9]).then_inc(cT_sb, 1)

            def inverse_rms(sm, n):
                dve.wait_ge(sm, n)
                link(v.reciprocal(rstd, rstd))

            inverse_rms(rms_sb, 1)

            def modulation(g):
                dve.wait_ge(ada_ps, 4 * g + 4)
                v.tensor_copy(mod_sb, ps[:, 6, :]).then_inc(mod_rows, 1)
                dve.wait_ge(modT_ps, g + 1)
                dve.wait_ge(vecT_sb, 1)
                for j in range(4):
                    src = ps[:, 7, :].rearrange("p (c r) -> p c r", c=4)[:, :, 32 * j:32 * j + 9]
                    add = vT[:, V_BADA + 16 * g + 4 * j:V_BADA + 16 * g + 4 * j + 4, None].to_broadcast([P, 4, 9])
                    last = v.tensor_tensor(modT[:, 2 * g + j // 2, 4 * (j % 2):4 * (j % 2) + 4, :], src, add, ALU.add)
                last.then_inc(mod_done, 1)

            def scale_gain(gain, scale):
                link(v.scalar_tensor_tensor(s1, modT[:, scale], 1.0, vT[:, gain:gain + KD, None].to_broadcast([P, KD, 9]), ALU.add, ALU.mult))

            def modulated(shift):
                hs = hT[:, :, NP_TOK:T].rearrange("p k (b l) -> p k b l", l=LS)
                link(v.tensor_tensor(hT[:, :, NP_TOK:T], xT[:, :, NP_TOK:T], rstd[:, None, NP_TOK:T].to_broadcast([P, KD, NS_TOK]), ALU.mult))
                link(v.tensor_tensor(hs, hs, s1[:, :, 1:9, None].to_broadcast([P, KD, NB, LS]), ALU.mult))
                v.tensor_tensor(hs, hs, modT[:, shift, :, 1:9, None].to_broadcast([P, KD, NB, LS]), ALU.add).then_inc(hs_done, 1)
                for k in range(KD):
                    v.scalar_tensor_tensor(hT[:, k, 0:NP_TOK], xT[:, k, 0:NP_TOK], s1[:, k, 0:1], rstd[:, 0:NP_TOK], ALU.mult, ALU.mult).then_inc(hp_sb, 1)

            modulation(0)
            dve.wait_ge(mod_done, 1)
            scale_gain(V_G1, 1)
            modulated(0)

            def chunks(x, which):
                if which == 0:
                    return x[:, :, 0:NP_TOK].rearrange("p h (c l) -> p h c l", l=CH)
                return x[:, :, NP_TOK:T].rearrange("p h (c l) -> p h c l", l=LS)

            def against(out, at):
                for w, ln in ((0, CH), (1, LS)):
                    b = chunks(bT, w)
                    ref = b[:, :, :, at(ln):at(ln) + 1]
                    for h in range(GH):
                        yield chunks(out, w)[:, h], b[:, h], ref[:, h].to_broadcast([P, b.shape[2], ln])

            def level(w, q, k, e, q2, k2):
                for src, dst, mine, other in ((q, q2, 1, 0), (k, k2, 0, 1)):
                    if dst is None:
                        continue
                    for h in range(GH):
                        x, y = (z[:, h, 0:NP_TOK].rearrange("p (c a l) -> p a c l", a=2, l=w) for z in (src, dst))
                        d = e[:, h, 0:NP_TOK // w].rearrange("p (c a) -> p a c", a=2)[:, other, :, None].to_broadcast([P, NP_TOK // w // 2, w])
                        v.tensor_tensor(y[:, mine], x[:, mine], d, ALU.mult)
                        last = v.tensor_copy(y[:, other], x[:, other])
                return last

            def decay(step):
                if step == 0:
                    dve.wait_ge(fm_sb, 13)
                    v.scalar_tensor_tensor(eqT, elT, -1.0, elT, ALU.mult, ALU.min).then_inc(gla_d, 1)
                if step == 1:
                    dve.wait_ge(gla_a, 1)
                    link(v.scalar_tensor_tensor(elT, elT, 0.0, eqT, ALU.min, ALU.subtract))
                    for h in range(GH):
                        last = v.tensor_tensor_scan(bT[:, h, :], const("scan"), elT[:, h, :], 0.0, ALU.mult, ALU.add)
                    last.then_inc(gla_d, 1)
                if step == 2:
                    dve.wait_ge(gla_d, 2)
                    for dst, x, y in against(eqT, lambda ln: ln // 2 - 1):
                        last = v.tensor_tensor(dst, x, y, ALU.subtract)
                    link(last)
                    v.tensor_scalar(eqT, eqT, CLAMP, -CLAMP, ALU.min, ALU.max).then_inc(gla_d, 1)
                if step == 3:
                    for dst, x, y in against(elT, lambda ln: ln - 1):
                        last = v.tensor_tensor(dst, y, x, ALU.subtract)
                    last.then_inc(gla_d, 1)
                if step == 4:
                    dve.wait_ge(gla_a, 2)
                    v.tensor_copy(edec[:, :, 0:16], chunks(e0T, 0)[:, :, :, CH - 1])
                    link(v.tensor_copy(edec[:, :, 16:24], chunks(e0T, 1)[:, :, :, LS - 1]))
                    v.scalar_tensor_tensor(eqT, gqT, DK ** -0.5, eqT, ALU.mult, ALU.mult)
                    v.tensor_tensor(ekT, gkT, ekT, ALU.mult)
                if step == 5:
                    v.scalar_tensor_tensor(e0T, gqT, DK ** -0.5, e0T, ALU.mult, ALU.mult)
                    dve.wait_ge(gla_a, 3)
                    link(v.tensor_tensor(elT, gkT, elT, ALU.mult))
                if step == 6:
                    link(level(16, e0T, elT, edec, q32, k32))
                    link(v.tensor_tensor(e32, edec[:, :, 0:16:2], edec[:, :, 1:16:2], ALU.mult))
                if step == 7:
                    link(level(32, q32, k32, e32, q64, k64))
                    link(v.tensor_tensor(e64, e32[:, :, 0:8:2], e32[:, :, 1:8:2], ALU.mult))
                if step == 8:
                    link(level(64, q64, k64, e64, None, k128))
                    v.tensor_tensor(e128, e64[:, :, 0:4:2], e64[:, :, 1:4:2], ALU.mult).then_inc(gla_d, 1)

            dve.wait_ge(xT_ps, KD)
            v.memset(v_tok[NS_TOK:P, 2, :], 0.0)
            v.memset(mv_tok[NS_TOK:P, 2, :], 0.0)
            for n in range(15):
                c, t = divmod(n, 3)
                rows = TILES[t][1]
                dve.wait_ge(tm_ps, n + 1)
                bank = ps[0:rows, 3 + t, :]
                if t == 2:
                    to = v_tok[0:rows, 2, 512 * c:512 * c + 512] if c < 2 else raw[0:rows, :] if c < 4 else mv_tok[0:rows, 2, :]
                    for f in range(2):
                        last = v.tensor_copy(to[:, 256 * f:256 * f + 256], ps[64 * f:64 * f + 64, 5, 0:256])
                    if c in (2, 3):
                        link(last)
                        bank = raw[0:rows, :]
                    else:
                        last.then_inc(tm_sb, 1)
                elif c < 2:
                    v.tensor_copy(v_tok[0:rows, t, 512 * c:512 * c + 512], bank).then_inc(tm_sb, 1)
                elif c == 4:
                    v.tensor_copy(mv_tok[0:rows, t, :], bank).then_inc(tm_sb, 1)
                if 2 <= c < 4:
                    x = bank.rearrange("p (h a d) -> p h a d", a=2, d=HD // 2)
                    r = rot[0:rows, c - 2, t, :].rearrange("p (h a d) -> p h a d", a=2, d=HD // 2)
                    cos = const("cos")[0:rows, None, 32 * t:32 * t + 32].to_broadcast([rows, MH, 32])
                    sin = const("sin")[0:rows, None, 32 * t:32 * t + 32].to_broadcast([rows, MH, 32])
                    s = tmp[0:rows, 0:256].rearrange("p (h d) -> p h d", d=32)
                    v.tensor_tensor(r[:, :, 0, :], x[:, :, 0, :], cos, ALU.mult)
                    v.tensor_tensor(r[:, :, 1, :], x[:, :, 1, :], cos, ALU.mult)
                    link(v.tensor_tensor(s, x[:, :, 1, :], sin, ALU.mult))
                    link(v.tensor_tensor(r[:, :, 0, :], r[:, :, 0, :], s, ALU.subtract))
                    link(v.tensor_tensor(s, x[:, :, 0, :], sin, ALU.mult))
                    v.tensor_tensor(r[:, :, 1, :], r[:, :, 1, :], s, ALU.add).then_inc(tm_sb, 1)
                    dve.wait_ge(tm_sb, n + 1)
                if n >= 6:
                    decay(n - 6)
                if n == 11:
                    modulation(1)
            for m in range(8):
                dve.wait_ge(fm_sb, 14 + m)
                v.tensor_tensor(grT[:, m, :], ps[:, (13 + m) % 3, 0:T], grT[:, m, :], ALU.mult).then_inc(gr_sb, 1)
            modulation(2)

            dve.wait_ge(fm_sb, 29)
            dve.wait_ge(k_out, 32)
            level(64, q64, None, e64, q128, None).then_inc(q128_sb, 1)

            def masked(u):
                dve.wait_ge(att_ps, u + 1)
                four = ps[:, 4, :]
                link(v.tensor_tensor(four, four, const("gla_p"), ALU.mult))
                if u >= 2:
                    dve.wait_ge(o_part, u - 1)
                v.tensor_reduce(att[:, u % 2, :], four.rearrange("p (j n) -> p n j", j=4), AX, ALU.add).then_inc(att_sb, 1)

            def new_state(u):
                t, h = divmod(u, GH)
                dve.wait_ge(d_ps, u + 1)
                if t == 0:
                    v.tensor_copy(state[:, h, :], ps[:, u % 2, 0:DV]).then_inc(s_new, 1)
                else:
                    dve.wait_ge(o_part, u + 1)
                    v.scalar_tensor_tensor(state[:, h, :], state[:, h, :], e128[:, h, t:t + 1], ps[:, u % 2, 0:DV], ALU.mult, ALU.add).then_inc(s_new, 1)

            def normed(u):
                t, h = divmod(u, GH)
                n = TILES[t][1]
                dve.wait_ge(o_sq, u + 1)
                if u >= 2:
                    dve.wait_ge(o_norm, u - 1)
                link(v.reciprocal(colB[0:n, u % 2:u % 2 + 1], colC[0:n, u % 2:u % 2 + 1]))
                if t and h == 0:
                    dve.wait_ge(ot_ps, t)
                v.tensor_scalar(o_tok[0:n, h * DV:(h + 1) * DV], ps[0:n, 5 + u % 2, 0:DV], colB[0:n, u % 2:u % 2 + 1], None, ALU.mult).then_inc(o_norm, 1)

            def gated(t):
                t0, n = TILES[t]
                dve.wait_ge(ot_ps, t + 1)
                for f in range(2):
                    for j in range(2):
                        src = ps[:, 2 if f else 7, 0:4 * n].rearrange("p (h j n) -> p j h n", j=2, n=n)[:, j]
                        gr = grT[:, 4 * f:4 * f + 4, t0:t0 + n].rearrange("p (h j) n -> p j h n", j=2)[:, j]
                        to = oTg[:, 4 * f:4 * f + 4, t0:t0 + n].rearrange("p (h j) n -> p j h n", j=2)[:, j]
                        last = v.scalar_tensor_tensor(to, src, vT[:, V_GH + j:V_GH + j + 1], gr, ALU.mult, ALU.mult)
                last.then_inc(ot_sb, 1)

            masked(0)
            dve.wait_ge(kt_ps, 1)
            link(v.memset(qm, 0.0))
            for u in range(2 * GH):
                if u + 1 < 2 * GH:
                    masked(u + 1)
                new_state(u)
                if u:
                    normed(u - 1)
                if u == GH:
                    gated(0)
            normed(2 * GH - 1)

            def sample_masks(h):
                if h >= 2:
                    dve.wait_ge(o_part, 2 * GH + 8 * (h - 1))
                else:
                    dve.wait_ge(att_ps, 2 * GH)
                at = 5120 + 8 * NS_TOK * (h % 2)
                diag = late[:, at:at + 8 * (NS_TOK + LS)].rearrange("p (c x) -> p c x", x=NS_TOK + LS)[:, :, 0:LS]
                v.tensor_copy(diag, e0T[:, h, NP_TOK:T].rearrange("p (c l) -> p c l", l=LS)).then_inc(qm_sb, 1)
                v.tensor_tensor(km[0:NS_TOK, h % 2], ps[0:NS_TOK, 3, None, h * DK:(h + 1) * DK].to_broadcast([NS_TOK, 8, DK]),
                                const("rows_s")[0:NS_TOK, :, None].to_broadcast([NS_TOK, 8, DK]), ALU.mult).then_inc(km_sb, 1)

            n = NS_TOK
            for h in range(GH):
                u = 2 * GH + h
                x0 = 2 * GH + 8 * h
                if h == 0:
                    sample_masks(0)
                dve.wait_ge(att_ps, u + 1)
                v.tensor_tensor(att[0:n, u % 2, 0:n], ps[0:n, 4, 0:n], const("gla_s")[0:n, 0:n], ALU.mult).then_inc(att_sb, 1)
                if h == 0:
                    gated(1)
                for c in range(8):
                    if h and c == 2:
                        normed(u - 1)
                    if h + 1 < GH and c == 4:
                        sample_masks(h + 1)
                    dve.wait_ge(d_ps, x0 + c + 1)
                    dve.wait_ge(o_part, x0 + c + 1)
                    s0 = ring[:, (N_S0 + c // 4) % PRE, ((c % 4) * GH + h) * DV:((c % 4) * GH + h + 1) * DV]
                    v.scalar_tensor_tensor(s0, s0, edec[:, h, 16 + c:17 + c], ps[:, (8 * h + c) % 3, 0:DV], ALU.mult, ALU.add).then_inc(s_new, 1)
            normed(3 * GH - 1)
            gated(2)

            dve.wait_ge(gs_out, 16)
            def prompt_out(h):
                dve.wait_ge(mo_ps, h + 1)
                link(v.reciprocal(colD[:, 2 * (h % 2):2 * (h % 2) + 2], colC[:, 2 * (h % 2):2 * (h % 2) + 2]))
                for t in range(2):
                    last = v.tensor_scalar(om_tok[:, t, h * HD:(h + 1) * HD], ps[:, 6 + h % 2, t * HD:(t + 1) * HD],
                                           colD[:, 2 * (h % 2) + t:2 * (h % 2) + t + 1], None, ALU.mult)
                last.then_inc(mo_sb, 1)

            for h in range(MH):
                dve.wait_ge(ms_ps, h + 1)
                if h >= 2:
                    dve.wait_ge(ms_exp, h - 1)
                x = pin[:, h % 2, :]
                link(v.tensor_tensor(x, ps[:, 2 + h % 2, 0:384], const("causal"), ALU.add))
                v.tensor_reduce(colA[:, 0:1], x[:, 0:P], AX, ALU.max)
                link(v.tensor_reduce(colA[:, 1:2], x[:, P:3 * P], AX, ALU.max))
                v.tensor_scalar(colB[:, 2 * (h % 2):2 * (h % 2) + 2], colA[:, 0:2], -HD ** -0.5, None, ALU.mult).then_inc(ms_max, 1)
                if h:
                    prompt_out(h - 1)
            prompt_out(MH - 1)

            dve.wait_ge(mot_sb, 2)
            v.memset(pto[NS_TOK:P, :], 0.0)
            link(v.memset(qs, 0.0))
            def queries(b):
                for hh in range(2):
                    rows = slice(64 * hh, 64 * hh + 64)
                    last = v.tensor_copy(qs[rows, :, 8 * hh:8 * hh + 8], mqT[rows, :, bass.ds(b * LS + NP_TOK, LS)])
                last.then_inc(q_sb, 1)

            def cache_max(b):
                dve.wait_ge(cs_ps, b + 1)
                sc = ps[:, 4:6, :].rearrange("p a (b c) -> p a b c", c=BLOCK)
                gsum4 = colA[:, 0:4]
                v.tensor_reduce(gsum4.rearrange("p (a b) -> p a b", b=2), sc, AX, ALU.add)
                v.tensor_reduce(colD[:, 0:4].rearrange("p (a b) -> p a b", b=2), sc, AX, ALU.max)
                link(v.tensor_tensor(tmp[:, 0:NS_TOK], ps[:, 6, 0:NS_TOK], const("own")[:, bass.ds(b * NS_TOK, NS_TOK)], ALU.add))
                v.tensor_reduce(colD[:, 4:5], tmp[:, 0:NS_TOK], AX, ALU.max)
                mine = gsum4[:, :, None].to_broadcast([P, 4, 4])
                other = gsum4[:, None, :].to_broadcast([P, 4, 4])
                w = tmp[:, 64:80].rearrange("p (a b) -> p a b", b=4)
                w2 = tmp[:, 80:96].rearrange("p (a b) -> p a b", b=4)
                tri = const("tri").rearrange("p (a b) -> p a b", b=4)
                v.tensor_tensor(w, other, mine, ALU.is_gt)
                link(v.tensor_tensor(w2, other, mine, ALU.is_equal))
                link(v.tensor_tensor(w2, w2, tri, ALU.mult))
                link(v.tensor_tensor(w, w, w2, ALU.add))
                link(v.tensor_reduce(colA[:, 4:8], w, AX, ALU.add))
                link(v.tensor_scalar(colA[:, 8:12], colA[:, 4:8], 3.0, NEG, ALU.is_ge, ALU.mult))
                link(v.tensor_tensor(colD[:, 0:4], colD[:, 0:4], colA[:, 8:12], ALU.add))
                link(v.tensor_reduce(colD[:, 5:6], colD[:, 0:5], AX, ALU.max))
                link(v.tensor_scalar(colB[:, 4:5], colD[:, 5:6], -HD ** -0.5, None, ALU.mult))
                v.tensor_scalar(colB[:, 0:4], colA[:, 8:12], colB[:, 4:5], None, ALU.add).then_inc(cs_max, 1)

            def cache_probs(b):
                dve.wait_ge(cs_exp, b + 1)
                link(v.tensor_reduce(colD[:, 8:9], colC[:, 0:5], AX, ALU.add))
                link(v.reciprocal(colD[:, 9:10], colD[:, 8:9]))
                dve.wait_ge(cp_ps, b + 1)
                v.tensor_copy(pts[:, 4:8, :], ps[:, 1, :].rearrange("p (a b) -> p a b", b=P)).then_inc(cp_d, 1)

            def cache_scale(b):
                dve.wait_ge(co_ps, b + 1)
                v.tensor_scalar(osm, ps[:, 7, 0:P], colD[:, 9:10], None, ALU.mult).then_inc(co_sb, 1)

            def cache_out(b):
                dve.wait_ge(cot_ps, b + 1)
                for hh in range(2):
                    rows = slice(64 * hh, 64 * hh + 64)
                    src = ps[rows, 7, 0:P].rearrange("p (a r) -> p a r", r=32)[:, :, 8 * hh:8 * hh + 8]
                    last = v.tensor_copy(oTm[rows, :, bass.ds(b * LS + NP_TOK, LS)], src)
                last.then_inc(cot_sb, 1)

            def projected(n):
                which, m = divmod(n, KD)
                dve.wait_ge(pj_ps, n + 1)
                bank = ps[:, n % 4, 0:T]
                if which == 0:
                    v.tensor_tensor(baT[:, m, :], bank, baT[:, m, :], ALU.mult).then_inc(pj_sb, 1)
                elif which == 1:
                    link(v.tensor_tensor(bbT[:, m, :], bank, bbT[:, m, :], ALU.mult))
                    v.tensor_tensor(hT[:, m, :], baT[:, m, :], bbT[:, m, :], ALU.add).then_inc(pj_sb, 1)
                else:
                    v.scalar_tensor_tensor(xT[:, m, 0:NP_TOK], bank[:, 0:NP_TOK], modT[:, 2, m, 0:1], xT[:, m, 0:NP_TOK], ALU.mult, ALU.add)
                    w = tmp[:, 0:NS_TOK].rearrange("p (b l) -> p b l", l=LS)
                    link(v.tensor_tensor(w, bank[:, NP_TOK:T].rearrange("p (b l) -> p b l", l=LS),
                                         modT[:, 2, m, 1:9, None].to_broadcast([P, NB, LS]), ALU.mult))
                    v.tensor_tensor(xT[:, m, NP_TOK:T], xT[:, m, NP_TOK:T], tmp[:, 0:NS_TOK], ALU.add).then_inc(pj_sb, 1)
                    dve.wait_ge(pj_sb, n + 1)
                    v.tensor_tensor(sq[:, m, :], xT[:, m, :], xT[:, m, :], ALU.mult).then_inc(sq2_sb, 1)

            queries(0)
            cache_max(0)
            queries(1)
            cache_probs(0)
            with dve.Fori(0, NB - 2) as i:
                st.enter(i, 11)
                cache_max(i + 1)
                queries(i + 2)
                cache_scale(i)
                cache_probs(i + 1)
                cache_out(i)
            st.leave(NB - 2)
            cache_max(NB - 1)
            for n in range(4):
                projected(n)
            cache_scale(NB - 2)
            cache_probs(NB - 1)
            cache_out(NB - 2)
            cache_scale(NB - 1)
            cache_out(NB - 1)

            for n in range(4, 24):
                projected(n)
            scale_gain(V_G2, 4)
            inverse_rms(rms_sb, 2)
            modulated(3)
            dve.wait_ge(asg_in, 1)
            v.tensor_copy(asgf, asg[:])
            v.tensor_copy(gate_x.rearrange("p k (b l) -> p k b l", l=LS), modT[:, 5, :, 1:9, None].to_broadcast([P, KD, NB, LS])).then_inc(gate_x_sb, 1)
            link(v.memset(lg, 0.0))
            dve.wait_ge(rt_ps, 1)
            for t, (t0, n) in enumerate(TILES):
                last = v.tensor_tensor(lg[0:n, t, :], ps[0:n, 6, NE * t:NE * t + NE], b_rt[0:n, :], ALU.add)
            link(last)
            for t in range(3):
                last = v.max(top[:, t, :], lg[:, t, :])
            link(last)
            for t in range(3):
                last = v.max_index(topi[:, t, :], top[:, t, :], lg[:, t, :])
            link(last)
            v.tensor_scalar(colD[:, 0:3], top[:, :, 0], -1.0, None, ALU.mult).then_inc(g_max, 1)
            link(v.tensor_copy(topf, topi[:]))
            for t in range(3):
                for k in range(TOPK):
                    last = v.tensor_scalar(oh[:, t, k, :], const("iota")[:, 0:NE], topf[:, t, k:k + 1], None, ALU.is_equal)
            link(last)
            for t in range(3):
                last = v.tensor_reduce(pick[:, t, :], oh[:, t].rearrange("p k e -> p e k"), AX, ALU.add)
            last.then_inc(picked, 1)
            dve.wait_ge(rank_ps, 1)
            v.memset(pos, 0.0)
            link(v.tensor_copy(cnt, ps[:, 4, 96:128]))
            for t, (t0, n) in enumerate(TILES):
                last = v.tensor_copy(pos[0:n, t, :], ps[0:n, 4, NE * t:NE * t + NE])
            link(last)
            v.tensor_scalar(nblk, pos, float(BT), None, ALU.is_ge)
            link(v.tensor_scalar(xtra, cnt, float(BT), None, ALU.is_gt))
            for j in range(2, 5):
                v.scalar_tensor_tensor(nblk, pos, float(BT * j), nblk, ALU.is_ge, ALU.add)
                link(v.scalar_tensor_tensor(xtra, cnt, float(BT * j), xtra, ALU.is_gt, ALU.add))
            link(v.tensor_tensor_scan(xend, ones[:, 0:NE], xtra, 0.0, ALU.mult, ALU.add))
            v.tensor_scalar(col, nblk, 0.0, None, ALU.is_equal)
            link(v.scalar_tensor_tensor(xtra, xend, float(NE - 1), xtra, ALU.add, ALU.subtract))
            v.scalar_tensor_tensor(pos, nblk, float(-BT), pos, ALU.mult, ALU.add)
            link(v.tensor_tensor(cnt, const("iota")[:, 0:NE], xtra, ALU.subtract))
            link(v.tensor_tensor(col, col, cnt[:, None, :].to_broadcast([P, 3, NE]), ALU.mult))
            v.tensor_tensor(rtmp, oh, pos[:, :, None, :].to_broadcast([P, 3, TOPK, NE]), ALU.mult)
            link(v.tensor_tensor(col, col, nblk, ALU.add))
            v.tensor_reduce(row_k.rearrange("p (t k) -> p t k", k=TOPK), rtmp, AX, ALU.add)
            link(v.tensor_tensor(col, col, xtra[:, None, :].to_broadcast([P, 3, NE]), ALU.add))
            link(v.tensor_tensor(rtmp, oh, col[:, :, None, :].to_broadcast([P, 3, TOPK, NE]), ALU.mult))
            v.tensor_tensor(row_oh, row_k[:, :, None].to_broadcast([P, 3 * TOPK, BT]), const("iota")[:, None, :].to_broadcast([P, 3 * TOPK, BT]), ALU.is_equal)
            link(v.tensor_reduce(col_k.rearrange("p (t k) -> p t k", k=TOPK), rtmp, AX, ALU.add))
            link(v.tensor_tensor(col_oh, col_k[:, :, None].to_broadcast([P, 3 * TOPK, NCOL]),
                                 const("iota")[:, None, 0:NCOL].to_broadcast([P, 3 * TOPK, NCOL]), ALU.is_equal))
            v.tensor_tensor(col_oh, col_oh, asgf[:, :, None].to_broadcast([P, 3 * TOPK, NCOL]), ALU.mult).then_inc(hot_sb, 1)
            dve.wait_ge(slots_ps, 1)
            for half in range(2):
                last = v.tensor_scalar(slots[BT * half:BT * half + BT, :], ps[0:BT, 7, 0:NCOL], float(FREE), None, ALU.add)
            link(last)
            v.tensor_scalar(tok_ix[0:BT, :], slots[0:BT, :], 2, None, ALU.logical_shift_right)
            v.tensor_scalar(row_ix[:], slots[:], 2.0, const("half"), ALU.mult, ALU.add).then_inc(ix_done, 1)
            link(v.tensor_tensor(xcmp[0:1], xend[0:1, None, :].to_broadcast([1, NX, NE]),
                                 const("iota")[0:1, 0:NX, None].to_broadcast([1, NX, NE]), ALU.is_le))
            link(v.tensor_reduce(cnt[0:1, 0:NX], xcmp[0:1], AX, ALU.add))
            link(v.tensor_scalar(cnt[0:1, 0:NX], cnt[0:1, 0:NX], float(NE - 1), None, ALU.min))
            link(v.tensor_copy(cnt[0:1, NX:NX + 1], xend[0:1, NE - 1:NE]))
            v.tensor_copy(eid[0:1, :], cnt[0:1, 0:NX + 1]).then_inc(route_done, 1)
            dve.wait_ge(g_exp, 1)
            for t, (t0, n) in enumerate(TILES):
                last = v.reciprocal(gsum[0:n, t:t + 1], gsum[0:n, t:t + 1])
            link(last)
            for t, (t0, n) in enumerate(TILES):
                last = v.tensor_scalar(gates[0:n, t, :], gates[0:n, t, :], gsum[0:n, t:t + 1], None, ALU.mult)
            link(last)

            def expert(par, n):
                dve.wait_ge(slot_used, n * RING + PRE)
                v.tensor_scalar(glu, ps[:, 2 + par, :], LIMIT, None, ALU.min).then_inc(glu_sb, 1)
                v.tensor_scalar(lin, ps[:, 4 + par, :], LIMIT, -LIMIT, ALU.min, ALU.max).then_inc(dve_moe, 1)
                dve.wait_ge(dve_moe, n * 2 + 1)
                dve.wait_ge(glu_sb, n + 1)
                v.scalar_tensor_tensor(lin, lin, 1.0, glu, ALU.add, ALU.mult).then_inc(dve_moe, 1)
                dve.wait_ge(dve_moe, n * 2 + 2)
                dve.wait_ge(sig_sb, n + 1)
                v.tensor_tensor(act_m, lin, sig, ALU.mult).then_inc(act_sb, 1)
                dve.wait_ge(slot_used, n * RING + RING)
                dve.wait_ge(y_free, n + 1)
                v.tensor_copy(y_out[par], ps[:, 7, :]).then_inc(y_sb, 1)

            with dve.Fori(0, NE // 2) as i:
                for par in range(2):
                    expert(par, i * 2 + par)
            dve.wait_ge(route_done, 1)
            n_extra = dve.value_load(eid[0:1, NX:NX + 1], min_val=0, max_val=NX)
            with dve.If(n_extra > 0):
                with dve.Fori(0, NX) as i:
                    with dve.If(i < n_extra):
                        expert(0, i + NE)
                    dve.nop()

            dve.wait_ge(gfin_in, 16)
            st = Steps(dve, dve_tail)

            def row_rms(t):
                dve.wait_ge(rms3_sb[t], 2)
                n = TILES[t][1]
                v.reciprocal(rinv[0:n, t:t + 1], ssq[0:n, t:t + 1]).then_inc(rinv_sb[t], 1)
                dve.wait_ge(rinv_sb[t], 1)

            combined(v, dve, st.link, 0)
            combined(v, dve, st.link, 1)
            row_rms(0)
            final_norm(v, 0)
            row_rms(2)
            row_rms(1)
            final_norm(v, 1)

        @block.gpsimd
        def _(pool):
            g = nc.gpsimd
            g.iota(asg[:].rearrange("p (t k) -> p t k", k=TOPK), pattern=[[P * TOPK, 3], [1, TOPK]], base=-FREE, channel_multiplier=TOPK).then_inc(asg_in, 1)
            pool.wait_ge(pt_in, 16)
            def value_pages(b, par):
                n = N_CACHE + 2 * par + 1
                for j in range(NPAGES):
                    page = pool.value_load(ptab[0:1, bass.ds(b * NPAGES + j, 1)], min_val=0, max_val=cache_k.shape[1] - 1)
                    pool.dma_start(item(n)[:, j, :], v_pages[bass.ds(page, 1)].rearrange("o s n -> s (o n)")).then_inc(v_land[par], 16)

            for b in range(2):
                pool.wait_ge(*used[N_CACHE + 2 * b + 1 - PRE])
                value_pages(b, b)
            with pool.Fori(1, NB // 2) as i:
                for par in range(2):
                    b = i * 2 + par
                    pool.wait_ge(co_ps, b - 1)
                    pool.sem_inc(turns, 1)
                    value_pages(b, par)
            pool.wait_ge(pj_sb, 24)
            for par in range(2):
                g.memset(bias[par], 0.0).then_inc(zero_sb, 1)
            for par in range(2):
                g.memset(x_in[par], 0.0).then_inc(zero_sb, 1)
            pool.wait_ge(ix_done, 1)
            pool.wait_ge(h2_out, 48)
            pool.wait_ge(zero_sb, 4)

            def gather(par, col, turn):
                g.tensor_copy(tok_col[0:BT, par:par + 1], tok_ix[0:BT, bass.ds(col, 1)]).then_inc(ix_sb, 1)
                pool.wait_ge(ix_sb, turn)
                pool.sem_inc(turns, 1)
                pool.indirect_dma_start(out=x_in[par][0:BT, :], out_offset=None, in_=h2_rows,
                                        in_offset=bass.IndirectOffsetOnAxis(ap=tok_col[0:BT, par:par + 1], axis=0),
                                        bounds_check=T - 1, oob_is_err=False).then_inc(x_land[par], 16)

            def scatter(par, col, turn):
                g.tensor_copy(row_col[:, par:par + 1], row_ix[:, bass.ds(col, 1)]).then_inc(ix_sb, 1)
                pool.wait_ge(ix_sb, turn)
                pool.sem_inc(turns, 1)
                pool.indirect_dma_start(out=y_rows, out_offset=bass.IndirectOffsetOnAxis(ap=row_col[:, par:par + 1], axis=0),
                                        in_=y_out[par], in_offset=None, bounds_check=T * TOPK * 2 - 1, oob_is_err=False).then_inc(y_sent[par], 16)

            pool.sem_inc(y_free, 2)
            gather(0, 0, 1)
            gather(1, 1, 2)
            with pool.Fori(0, NE // 2) as i:
                for par in range(2):
                    n = i * 2 + par
                    pool.wait_ge(y_sb, n + 1)
                    scatter(par, n, n * 2 + 3)
                    pool.wait_ge(xe_ps, n + 1)
                    gather(par, n + 2, n * 2 + 4)
                    pool.wait_ge(y_sent[par], (i + 1) * 16)
                    pool.sem_inc(y_free, 1)
            pool.wait_ge(x_land[0], 16 * (NE // 2 + 1))
            pool.wait_ge(x_land[1], 16 * (NE // 2 + 1))
            pool.wait_ge(route_done, 1)
            n_extra = pool.value_load(eid[0:1, NX:NX + 1], min_val=0, max_val=NX)
            with pool.If(n_extra > 0):
                with pool.Fori(0, NX) as i:
                    with pool.If(i < n_extra):
                        pool.wait_ge(y_sb, i + NE + 1)
                        scatter(0, i + NE, i * 2 + 2 * NE + 3)
                        gather(0, i + NE + 1, i * 2 + 2 * NE + 4)
                        pool.wait_ge(y_sent[0], (i + (NE // 2 + 1)) * 16)
                        pool.sem_inc(y_free, 1)
                        pool.wait_ge(x_land[0], (i + (NE // 2 + 2)) * 16)
                    pool.nop()
            pool.nop().then_inc(moe_done, 1)
            pool.wait_ge(g_exp, 1)
            pool.wait_ge(gfin_in, 16)
            link = Steps(pool, pool_tail).link
            n = NS_TOK
            y = ring[0:n, 2, :].rearrange("p (k d) -> p k d", k=TOPK)
            acc = ysum[0:n, 2, :]
            for k in range(1, TOPK):
                pool.wait_ge(y1_sb[2], k + 1)
                link(g.tensor_tensor(acc, y[:, 0, :] if k == 1 else acc, y[:, k, :], ALU.add))
            link(g.tensor_tensor(acc, acc, gate_s[0:n, :], ALU.mult))
            g.tensor_tensor(acc, acc, x_res[0:n, 2, :], ALU.add).then_inc(x3_sb[2], 1)
            pool.wait_ge(rms3_sb[2], 3)
            g.tensor_tensor(acc, y[:, 0, :], gfin[0:n, :], ALU.mult).then_inc(out_sb[2], 1)


_INS = ['x_prompt', 'x_sample', 'cache_k', 'cache_v', 'state_gla', 'page_table', 'c_prompt', 'c_sample',
        'w_ada', 'b_ada', 'g_norm1', 'w_in', 'w_gla_a2', 'b_gla_a2', 'g_gla_head', 'w_proj_gla', 'w_proj_moba',
        'w_out', 'g_norm2', 'w_router', 'b_router', 'w_gate_up', 'b_gate_up', 'w_down', 'b_down', 'g_final']
_OUTS = [(1, 256, 1024), (8, 8, 1024), (1, 1, 256, 8, 64), (1, 1, 256, 8, 64), (1, 1, 4, 128, 256),
         (1, 8, 8, 8, 64), (1, 8, 8, 8, 64), (1, 8, 4, 128, 256)]


def kernel(**inputs):
    import numpy as np
    import concourse.bacc as bacc
    from concourse.bass_utils import run_bass_kernel_spmd

    nc = bacc.Bacc("TRN2", target_bir_lowering=False, num_devices=1)
    arrays = {f"in_{name}": np.ascontiguousarray(inputs[name]) for name in _INS}
    arrays["in_consts"] = constants()
    args = [nc.dram_tensor(n, a.shape, mybir.dt.from_np(a.dtype), kind="ExternalInput").ap() for n, a in arrays.items()]
    args += [nc.dram_tensor(f"out_{i}", shape, F32, kind="ExternalOutput").ap() for i, shape in enumerate(_OUTS)]
    decoder_layer(nc, *args)
    r = run_bass_kernel_spmd(nc, [arrays], core_ids=[0])
    return tuple(r.results[0][f"out_{i}"] for i in range(len(_OUTS)))
```
